# Optimizing a Trainium2 kernel written in Bass

```python
import math
import jax, jax.numpy as jnp
from jax import lax
import numpy as np

D_MODEL = 1024
BATCH = 1
SEQ = 512
DEPTH = 1

MEM_LEN = 256
A_HEADS = 8
A_HEAD_DIM = 64
A_WIDTH = A_HEADS * A_HEAD_DIM
MOBA_BLOCK = 256
MOBA_TOPK = 3
Q_BLOCK = 128
G_HEADS = 4
G_WIDTH = D_MODEL - A_WIDTH
G_HEAD_V = G_WIDTH // G_HEADS
G_KEY_WIDTH = G_WIDTH // 2
G_HEAD_K = G_KEY_WIDTH // G_HEADS
G_GATE_RANK = 16
G_GATE_NORM = 16.0
G_CHUNK = 64
MIX_WIDTH = A_WIDTH + G_WIDTH
IN_SPLITS = (A_WIDTH, A_WIDTH, A_WIDTH, G_KEY_WIDTH, G_KEY_WIDTH, G_WIDTH, G_GATE_RANK, G_WIDTH)
IN_COLS = 3 * A_WIDTH + 2 * G_KEY_WIDTH + G_WIDTH + G_GATE_RANK + G_WIDTH
X_HEADS = 4
X_HEAD_DIM = D_MODEL // X_HEADS
D_FF = 4 * D_MODEL
RP_BUCKETS = 32
RP_MAX_DIST = 128
EPS = 1e-6


def rms_norm(x, g):
    xf = x.astype(jnp.float32)
    y = xf * lax.rsqrt(jnp.mean(xf * xf, axis=-1, keepdims=True) + EPS)
    return (y * g.astype(jnp.float32)).astype(x.dtype)

def rel_bucket(dist):
    max_exact = RP_BUCKETS // 2
    d = jnp.maximum(dist, 0)
    large = max_exact + (jnp.log(jnp.maximum(d, 1).astype(jnp.float32) / max_exact)
                         / math.log(RP_MAX_DIST / max_exact) * (RP_BUCKETS - max_exact)).astype(jnp.int32)
    large = jnp.minimum(large, RP_BUCKETS - 1)
    return jnp.where(d < max_exact, d, large)

def moba_attention(q, k, v, rp_table):
    B, T, H, dh = q.shape
    nb = -(-T // MOBA_BLOCK)
    pad = nb * MOBA_BLOCK - T
    kp = jnp.pad(k, ((0, 0), (0, pad), (0, 0), (0, 0)))
    vp = jnp.pad(v, ((0, 0), (0, pad), (0, 0), (0, 0)))
    kb = kp.reshape(B, nb, MOBA_BLOCK, H, dh).transpose(0, 3, 1, 2, 4)
    vb = vp.reshape(B, nb, MOBA_BLOCK, H, dh).transpose(0, 3, 1, 2, 4)
    nq = T // Q_BLOCK
    qc = q.reshape(B, nq, Q_BLOCK, H, dh).transpose(0, 1, 3, 2, 4).reshape(B * nq, H, Q_BLOCK, dh)
    scale = dh ** -0.5
    n_sel = min(MOBA_TOPK, nb - 1)
    table_t = rp_table.T.astype(jnp.float32)
    key_off = jnp.arange(MOBA_BLOCK, dtype=jnp.int32)
    hidx = jnp.arange(H)[:, None, None]
    b_ids = jnp.repeat(jnp.arange(B, dtype=jnp.int32), nq)
    qb_ids = jnp.tile(jnp.arange(nq, dtype=jnp.int32), B)
    xs = (qc, b_ids, qb_ids)
    if n_sel > 0:
        pos = jnp.arange(T, dtype=jnp.int32)
        q_blk = pos // MOBA_BLOCK
        kmean = jnp.mean(kb.astype(jnp.float32), axis=3)
        gate = jnp.einsum('bthd,bhnd->bhtn', q.astype(jnp.float32), kmean)
        past = jnp.arange(nb)[None, :] < q_blk[:, None]
        gate = jnp.where(past[None, None], gate, -jnp.inf)
        _, sel = lax.top_k(gate, n_sel)
        valid = sel < q_blk[None, None, :, None]
        sel_c = sel.reshape(B, H, nq, Q_BLOCK, n_sel).transpose(0, 2, 1, 3, 4).reshape(B * nq, H, Q_BLOCK, n_sel)
        valid_c = valid.reshape(B, H, nq, Q_BLOCK, n_sel).transpose(0, 2, 1, 3, 4).reshape(B * nq, H, Q_BLOCK, n_sel)
        xs = xs + (sel_c, valid_c)

    def step(args):
        qi, b, qb = args[0], args[1], args[2]
        kb_b = kb[b]
        vb_b = vb[b]
        q_pos = qb * Q_BLOCK + jnp.arange(Q_BLOCK, dtype=jnp.int32)
        own = (qb * Q_BLOCK) // MOBA_BLOCK
        k_own = lax.dynamic_index_in_dim(kb_b, own, axis=1, keepdims=False)
        v_own = lax.dynamic_index_in_dim(vb_b, own, axis=1, keepdims=False)
        d_own = q_pos[:, None] - (own * MOBA_BLOCK + key_off)[None, :]
        s_own = jnp.einsum('hqd,hld->hql', qi, k_own).astype(jnp.float32) * scale + table_t[:, rel_bucket(d_own)]
        s_own = jnp.where(d_own[None] >= 0, s_own, -jnp.inf)
        if n_sel > 0:
            sel_i, valid_i = args[3], args[4]
            k_sel = kb_b[hidx, sel_i]
            v_sel = vb_b[hidx, sel_i]
            d_sel = q_pos[None, :, None, None] - (sel_i[..., None] * MOBA_BLOCK + key_off)
            s_sel = (jnp.einsum('hqd,hqcld->hqcl', qi, k_sel).astype(jnp.float32) * scale
                     + table_t[hidx[..., None], rel_bucket(d_sel)])
            s_sel = jnp.where(valid_i[..., None], s_sel, -jnp.inf)
            s = jnp.concatenate([s_sel.reshape(H, Q_BLOCK, n_sel * MOBA_BLOCK), s_own], axis=-1)
            p = jax.nn.softmax(s, axis=-1).astype(v.dtype)
            p_sel = p[..., :n_sel * MOBA_BLOCK].reshape(H, Q_BLOCK, n_sel, MOBA_BLOCK)
            p_own = p[..., n_sel * MOBA_BLOCK:]
            return jnp.einsum('hqcl,hqcld->hqd', p_sel, v_sel) + jnp.einsum('hql,hld->hqd', p_own, v_own)
        p_own = jax.nn.softmax(s_own, axis=-1).astype(v.dtype)
        return jnp.einsum('hql,hld->hqd', p_own, v_own)

    o = lax.map(step, xs)
    return o.reshape(B, nq, H, Q_BLOCK, dh).transpose(0, 1, 3, 2, 4).reshape(B, T, H * dh)

def gla_chunked(q, k, v, log_a):
    B, T, H, dk = q.shape
    dv = v.shape[-1]
    nc = T // G_CHUNK
    scale = dk ** -0.5

    def to_chunks(t):
        return t.reshape(B, nc, G_CHUNK, H, t.shape[-1]).transpose(1, 0, 3, 2, 4)

    causal = jnp.tril(jnp.ones((G_CHUNK, G_CHUNK), dtype=bool))

    def body(S, inp):
        qi, ki, vi, gi = inp
        qf = qi.astype(jnp.float32) * scale
        kf = ki.astype(jnp.float32)
        vf = vi.astype(jnp.float32)
        b = jnp.cumsum(gi.astype(jnp.float32), axis=2)
        o_inter = jnp.einsum('bhcd,bhde->bhce', qf * jnp.exp(b), S)
        diff = b[:, :, :, None, :] - b[:, :, None, :, :]
        decay = jnp.exp(jnp.where(causal[None, None, :, :, None], diff, -jnp.inf))
        A = jnp.einsum('bhid,bhjd,bhijd->bhij', qf, kf, decay)
        o_intra = jnp.einsum('bhij,bhje->bhie', A, vf)
        b_last = b[:, :, -1:, :]
        S_new = jnp.exp(b_last[:, :, 0, :])[..., None] * S + jnp.einsum('bhcd,bhce->bhde', kf * jnp.exp(b_last - b), vf)
        return S_new, o_inter + o_intra

    S0 = jnp.zeros((B, H, dk, dv), jnp.float32)
    _, o = lax.scan(body, S0, (to_chunks(q), to_chunks(k), to_chunks(v), to_chunks(log_a)))
    return o.transpose(1, 0, 3, 2, 4).reshape(B, T, H, dv).astype(v.dtype)

def first_inputs(seed: int = 0) -> dict:
    key = jax.random.key(seed)
    ks = jax.random.split(key, 20)

    def nrm(k, shape, scale):
        return jax.random.normal(k, shape, jnp.float32) * scale

    def gain(k, shape):
        return 1.0 + 0.05 * jax.random.normal(k, shape, jnp.float32)

    L = DEPTH
    return {
        "x": nrm(ks[0], (BATCH, SEQ, D_MODEL), 1.0),
        "mem": nrm(ks[1], (BATCH, MEM_LEN, D_MODEL), 1.0),
        "rp_table": nrm(ks[2], (RP_BUCKETS, A_HEADS), 0.5),
        "norm_mix": gain(ks[3], (L, D_MODEL)),
        "w_in": nrm(ks[4], (L, D_MODEL, IN_COLS), D_MODEL ** -0.5),
        "w_gate_up": nrm(ks[5], (L, G_GATE_RANK, G_KEY_WIDTH), G_GATE_RANK ** -0.5),
        "b_gate": nrm(ks[6], (L, G_KEY_WIDTH), 0.1),
        "g_norm": gain(ks[7], (L, G_HEAD_V)),
        "w_out": nrm(ks[8], (L, MIX_WIDTH, D_MODEL), MIX_WIDTH ** -0.5),
        "norm_xattn": gain(ks[9], (L, D_MODEL)),
        "norm_mem": gain(ks[10], (L, D_MODEL)),
        "w_xq": nrm(ks[11], (L, D_MODEL, D_MODEL), D_MODEL ** -0.5),
        "w_xkv": nrm(ks[12], (L, D_MODEL, 2 * D_MODEL), D_MODEL ** -0.5),
        "w_xo": nrm(ks[13], (L, D_MODEL, D_MODEL), D_MODEL ** -0.5),
        "norm_mlp": gain(ks[14], (L, D_MODEL)),
        "w_up": nrm(ks[15], (L, D_MODEL, D_FF), D_MODEL ** -0.5),
        "w_down": nrm(ks[16], (L, D_FF, D_MODEL), D_FF ** -0.5),
        "norm_final": gain(ks[17], (D_MODEL,)),
    }

def first_block(x, mem, rp_table, norm_mix, w_in, w_gate_up, b_gate, g_norm, w_out,
              norm_xattn, norm_mem, w_xq, w_xkv, w_xo, norm_mlp, w_up, w_down, norm_final):
    B, T, _ = x.shape
    M = mem.shape[1]
    offsets = [int(o) for o in np.cumsum(IN_SPLITS)[:-1]]
    for l in range(DEPTH):
        h = rms_norm(x, norm_mix[l])
        proj = h @ w_in[l]
        qa, ka, va, qg, kg, vg, glr, rg = jnp.split(proj, offsets, axis=-1)
        o_a = moba_attention(qa.reshape(B, T, A_HEADS, A_HEAD_DIM),
                             ka.reshape(B, T, A_HEADS, A_HEAD_DIM),
                             va.reshape(B, T, A_HEADS, A_HEAD_DIM), rp_table)
        log_a = jax.nn.log_sigmoid((glr @ w_gate_up[l] + b_gate[l]).astype(jnp.float32)) / G_GATE_NORM
        o_g = gla_chunked(qg.reshape(B, T, G_HEADS, G_HEAD_K),
                          kg.reshape(B, T, G_HEADS, G_HEAD_K),
                          vg.reshape(B, T, G_HEADS, G_HEAD_V),
                          log_a.reshape(B, T, G_HEADS, G_HEAD_K))
        o_g = rms_norm(o_g, g_norm[l]).reshape(B, T, G_WIDTH) * jax.nn.silu(rg)
        x = x + jnp.concatenate([o_a, o_g], axis=-1) @ w_out[l]
        h = rms_norm(x, norm_xattn[l])
        m = rms_norm(mem, norm_mem[l])
        qx = (h @ w_xq[l]).reshape(B, T, X_HEADS, X_HEAD_DIM)
        kx, vx = jnp.split(m @ w_xkv[l], 2, axis=-1)
        kx = kx.reshape(B, M, X_HEADS, X_HEAD_DIM)
        vx = vx.reshape(B, M, X_HEADS, X_HEAD_DIM)
        s = jnp.einsum('bthd,bmhd->bhtm', qx, kx).astype(jnp.float32) * (X_HEAD_DIM ** -0.5)
        p = jax.nn.softmax(s, axis=-1).astype(vx.dtype)
        ox = jnp.einsum('bhtm,bmhd->bthd', p, vx).reshape(B, T, D_MODEL)
        x = x + ox @ w_xo[l]
        h = rms_norm(x, norm_mlp[l])
        x = x + jnp.square(jax.nn.relu(h @ w_up[l])) @ w_down[l]
    return rms_norm(x, norm_final)


GMLP_WIDTH = 512
GMLP_GROUPS = 4
GMLP_GROUP_DIM = GMLP_WIDTH // GMLP_GROUPS
CHUNK = 128

ATTN_PATTERNS = ((128, 1), (512, 4), (2048, 16))
N_ATTN_GROUPS = len(ATTN_PATTERNS)
HEADS_PER_GROUP = 4
HEAD_DIM = 128
ATTN_GROUP_WIDTH = HEADS_PER_GROUP * HEAD_DIM
ATTN_WIDTH = N_ATTN_GROUPS * ATTN_GROUP_WIDTH
ROPE_DIM = HEAD_DIM // 4
ROPE_THETA = 500000.0

N_BRANCHES = 2
D_FF_2 = 4 * D_MODEL
D_IN = 2 * GMLP_WIDTH + 3 * ATTN_WIDTH + N_BRANCHES * D_MODEL
NORM_EPS = 1e-6
MASK_VALUE = -1e30


def rms_norm_2(x, gain):
    xf = x.astype(jnp.float32)
    y = xf * lax.rsqrt(jnp.mean(xf * xf, axis=-1, keepdims=True) + NORM_EPS)
    return (y * gain.astype(jnp.float32)).astype(x.dtype)

def layer_norm(x, gain, bias):
    xf = x.astype(jnp.float32)
    mu = jnp.mean(xf, axis=-1, keepdims=True)
    var = jnp.mean(jnp.square(xf - mu), axis=-1, keepdims=True)
    y = (xf - mu) * lax.rsqrt(var + NORM_EPS)
    return (y * gain.astype(jnp.float32) + bias.astype(jnp.float32)).astype(x.dtype)

def partial_rope(t):
    S = t.shape[1]
    half = ROPE_DIM // 2
    inv_freq = ROPE_THETA ** (-jnp.arange(0, ROPE_DIM, 2, dtype=jnp.float32) / ROPE_DIM)
    ang = jnp.arange(S, dtype=jnp.float32)[:, None] * inv_freq[None, :]
    cos = jnp.cos(ang)[None, :, None, :]
    sin = jnp.sin(ang)[None, :, None, :]
    tf = t.astype(jnp.float32)
    x1, x2, rest = tf[..., :half], tf[..., half:ROPE_DIM], tf[..., ROPE_DIM:]
    out = jnp.concatenate([x1 * cos - x2 * sin, x2 * cos + x1 * sin, rest], axis=-1)
    return out.astype(t.dtype)

def dilated_window_attention(q, k, v, dilation, radius):
    B, S, H, Dh = q.shape
    L = S // dilation
    nb = -(-L // radius)
    Lp = nb * radius

    def strided(t):
        return t.astype(jnp.float32).reshape(B, L, dilation, H, Dh).transpose(0, 2, 1, 3, 4)

    qs, ks, vs = strided(q), strided(k), strided(v)
    qb = jnp.pad(qs, ((0, 0), (0, 0), (0, Lp - L), (0, 0), (0, 0))).reshape(B, dilation, nb, radius, H, Dh)

    def windows(t):
        tb = jnp.pad(t, ((0, 0), (0, 0), (radius, Lp - L + radius), (0, 0), (0, 0)))
        tb = tb.reshape(B, dilation, nb + 2, radius, H, Dh)
        return jnp.concatenate([tb[:, :, :-2], tb[:, :, 1:-1], tb[:, :, 2:]], axis=3)

    kw, vw = windows(ks), windows(vs)
    blk = jnp.arange(nb)[:, None, None]
    qpos = blk * radius + jnp.arange(radius)[None, :, None]
    kpos = blk * radius - radius + jnp.arange(3 * radius)[None, None, :]
    valid = (jnp.abs(qpos - kpos) <= radius) & (kpos >= 0) & (kpos < L)

    scale = 1.0 / math.sqrt(Dh)
    s = jnp.einsum('bdnqhe,bdnkhe->bdnhqk', qb, kw) * scale
    s = jnp.where(valid[None, None, :, None], s, MASK_VALUE)
    m = jnp.max(s, axis=-1, keepdims=True)
    p = jnp.exp(s - m)
    denom = jnp.sum(p, axis=-1, keepdims=True)
    o = jnp.einsum('bdnhqk,bdnkhe->bdnhqe', p, vw) / denom
    lse = (m + jnp.log(denom))[..., 0]

    o = o.transpose(0, 1, 2, 4, 3, 5).reshape(B, dilation, Lp, H, Dh)[:, :, :L]
    o = o.transpose(0, 2, 1, 3, 4).reshape(B, S, H, Dh)
    lse = lse.transpose(0, 1, 2, 4, 3).reshape(B, dilation, Lp, H)[:, :, :L]
    lse = lse.transpose(0, 2, 1, 3).reshape(B, S, H)
    return o, lse

def gmlp_spatial_gating(z, ln_gain, ln_bias, w_spatial, b_spatial):
    B, S, _ = z.shape
    u, v = z[..., :GMLP_WIDTH], z[..., GMLP_WIDTH:]
    v = layer_norm(v, ln_gain, ln_bias)
    v = v.reshape(B, S // CHUNK, CHUNK, GMLP_GROUPS, GMLP_GROUP_DIM)
    sv = jnp.einsum('bcsge,gts->bctge', v, w_spatial) + b_spatial.T[None, None, :, :, None]
    return u * sv.reshape(B, S, GMLP_WIDTH)

def second_inputs(seed: int = 0) -> dict:
    key = jax.random.key(seed)
    ks = jax.random.split(key, 17)
    f32 = jnp.float32

    def nrm(k, shape, scale):
        return jax.random.normal(k, shape, f32) * scale

    def gain(k, shape):
        return 1.0 + 0.05 * jax.random.normal(k, shape, f32)

    return {
        "x": jax.random.normal(ks[0], (BATCH, SEQ, D_MODEL), f32),
        "norm_mix_pre": gain(ks[1], (DEPTH, D_MODEL)),
        "w_in": nrm(ks[2], (DEPTH, D_MODEL, D_IN), D_MODEL ** -0.5),
        "b_gate": nrm(ks[3], (DEPTH, N_BRANCHES * D_MODEL), 0.02),
        "ln_v_gain": gain(ks[4], (DEPTH, GMLP_WIDTH)),
        "ln_v_bias": nrm(ks[5], (DEPTH, GMLP_WIDTH), 0.02),
        "w_spatial": nrm(ks[6], (DEPTH, GMLP_GROUPS, CHUNK, CHUNK), CHUNK ** -0.5),
        "b_spatial": gain(ks[7], (DEPTH, GMLP_GROUPS, CHUNK)),
        "w_branch_a": nrm(ks[8], (DEPTH, GMLP_WIDTH, D_MODEL), GMLP_WIDTH ** -0.5),
        "w_branch_b": nrm(ks[9], (DEPTH, ATTN_GROUP_WIDTH, D_MODEL), ATTN_GROUP_WIDTH ** -0.5),
        "w_out": nrm(ks[10], (DEPTH, D_MODEL, D_MODEL), D_MODEL ** -0.5),
        "norm_mix_post": gain(ks[11], (DEPTH, D_MODEL)),
        "norm_mlp_pre": gain(ks[12], (DEPTH, D_MODEL)),
        "w_up": nrm(ks[13], (DEPTH, D_MODEL, D_FF_2), D_MODEL ** -0.5),
        "w_down": nrm(ks[14], (DEPTH, D_FF_2, D_MODEL), D_FF_2 ** -0.5),
        "norm_mlp_post": gain(ks[15], (DEPTH, D_MODEL)),
    }

def second_block(x, norm_mix_pre, w_in, b_gate, ln_v_gain, ln_v_bias, w_spatial, b_spatial,
              w_branch_a, w_branch_b, w_out, norm_mix_post, norm_mlp_pre, w_up, w_down,
              norm_mlp_post):
    B, S, D = x.shape
    split_points = list(np.cumsum([GMLP_WIDTH * 2, ATTN_WIDTH, ATTN_WIDTH, ATTN_WIDTH])) 
    h = x
    for l in range(DEPTH):
        n = rms_norm_2(h, norm_mix_pre[l])
        proj = jnp.einsum('bsd,de->bse', n, w_in[l])
        z_gmlp, q, k, v, gates = jnp.split(proj, split_points, axis=-1)

        y_a = gmlp_spatial_gating(jax.nn.gelu(z_gmlp), ln_v_gain[l], ln_v_bias[l],
                                  w_spatial[l], b_spatial[l])

        n_heads = N_ATTN_GROUPS * HEADS_PER_GROUP
        q = partial_rope(q.reshape(B, S, n_heads, HEAD_DIM))
        k = partial_rope(k.reshape(B, S, n_heads, HEAD_DIM))
        v = v.reshape(B, S, n_heads, HEAD_DIM)
        outs, lses = [], []
        for g, (window, dilation) in enumerate(ATTN_PATTERNS):
            sl = slice(g * HEADS_PER_GROUP, (g + 1) * HEADS_PER_GROUP)
            o_g, lse_g = dilated_window_attention(q[:, :, sl], k[:, :, sl], v[:, :, sl],
                                                  dilation, window // (2 * dilation))
            outs.append(o_g)
            lses.append(lse_g)
        o_all = jnp.stack(outs, axis=0)
        w_mix = jax.nn.softmax(jnp.stack(lses, axis=0), axis=0)
        y_b = jnp.sum(w_mix[..., None] * o_all, axis=0).reshape(B, S, ATTN_GROUP_WIDTH).astype(h.dtype)

        g_all = jax.nn.sigmoid((gates + b_gate[l]).astype(jnp.float32)).astype(h.dtype)
        g_a, g_b = g_all[..., :D_MODEL], g_all[..., D_MODEL:]
        merged = (g_a * jnp.einsum('bse,ed->bsd', y_a, w_branch_a[l])
                  + g_b * jnp.einsum('bse,ed->bsd', y_b, w_branch_b[l]))
        mix_out = jnp.einsum('bsd,de->bse', merged, w_out[l])
        h = h + rms_norm_2(mix_out, norm_mix_post[l])

        n2 = rms_norm_2(h, norm_mlp_pre[l])
        hid = jnp.square(jax.nn.relu(jnp.einsum('bsd,df->bsf', n2, w_up[l])))
        mlp_out = jnp.einsum('bsf,fd->bsd', hid, w_down[l])
        h = h + rms_norm_2(mlp_out, norm_mlp_post[l])
    return h


def setup_inputs(seed=0):
    out = dict(first_inputs(seed))
    for name, value in second_inputs(seed + 1).items():
        if name != "x":
            out[name + "_2"] = value
    return out


def reference(
    x, mem, rp_table, norm_mix, w_in, w_gate_up, b_gate, g_norm, w_out, norm_xattn, norm_mem,
    w_xq, w_xkv, w_xo, norm_mlp, w_up, w_down, norm_final, norm_mix_pre_2, w_in_2, b_gate_2,
    ln_v_gain_2, ln_v_bias_2, w_spatial_2, b_spatial_2, w_branch_a_2, w_branch_b_2, w_out_2,
    norm_mix_post_2, norm_mlp_pre_2, w_up_2, w_down_2, norm_mlp_post_2,
):
    x = first_block(
        x, mem, rp_table, norm_mix, w_in, w_gate_up, b_gate, g_norm, w_out, norm_xattn,
        norm_mem, w_xq, w_xkv, w_xo, norm_mlp, w_up, w_down, norm_final,
    )
    return second_block(
        x, norm_mix_pre_2, w_in_2, b_gate_2, ln_v_gain_2, ln_v_bias_2, w_spatial_2, b_spatial_2,
        w_branch_a_2, w_branch_b_2, w_out_2, norm_mix_post_2, norm_mlp_pre_2, w_up_2, w_down_2,
        norm_mlp_post_2,
    )


_drawn_inputs = setup_inputs


def setup_inputs(seed=0):
    import zlib

    import numpy as np

    out = dict(_drawn_inputs(seed))
    spreads = {}
    factors = {'norm_xattn': 8.0,
     'norm_mem': 6.001,
     'b_gate_2': 8.0,
     'ln_v_bias_2': 5.854,
     'norm_mlp': 3.855}
    for name, (base, spread) in spreads.items():
        noise = np.random.default_rng([zlib.crc32(name.encode()), seed]).standard_normal(out[name].shape)
        drawn = base * np.exp(spread * noise) if base else spread * noise
        out[name] = __import__('jax').numpy.asarray(drawn.astype(out[name].dtype))
    for name, factor in factors.items():
        out[name] = (out[name] * factor).astype(out[name].dtype)
    return out
```

```python
import math
from contextlib import ExitStack

import numpy as np

import concourse.bass as bass
from concourse import mybir

F32 = mybir.dt.float32
F32R = mybir.dt.float32r
I32 = mybir.dt.int32
ACT = mybir.ActivationFunctionType
ALU = mybir.AluOpType
AX = mybir.AxisListType

P = 128
T = 512
TT = T // P
D = 1024
KC = D // P
M = 256
MT = M // P
A_HEADS, A_DIM = 8, 64
G_HEADS, G_DK, G_DV, G_RANK = 4, 64, 128, 16
G_NORM = 16.0
X_HEADS, X_DIM = 4, 256
FF = 4096
CHUNKS = FF // T
B_HEADS, B_DIM = 4, 128
PATTERNS = 3
RADIUS = 64
DILATION = (1, 4, 16)
ROPE_DIM = 32
ROPE_THETA = 500000.0
EPS = 1e-6
MASKED = -1e30
RP_BUCKETS, RP_MAX_DIST = 32, 128
LEVELS = (64, 32, 16, 8, 4, 2, 1)
WORDS = 1024
NEAR = 2 * P
REL = 3 * P

COLS = {}
_at = 0
for _name, _n in (("norm_mix", KC), ("norm_xattn", KC), ("norm_mem", KC), ("norm_mlp", KC),
                  ("norm_mix_pre_2", KC), ("norm_mlp_pre_2", KC), ("b_gate_2", 2 * KC), ("g_norm", 1),
                  ("b_gate", 2)):
    COLS[_name] = _at
    _at += _n
NCOLS = _at



W_IN = dict(qa=0, ka=512, va=1024, glaqk=1536, vg=2048, glr=2560, rg=2576)


def mlp_order():
    return ([("up", 0)] + [x for c in range(0, CHUNKS - 2, 2)
                           for x in (("up", c + 1), ("down", c), ("up", c + 2), ("down", c + 1))]
            + [("up", CHUNKS - 1), ("down", CHUNKS - 2), ("down", CHUNKS - 1)])


def stream_groups():
    out = [("w_xkv", 0, D, 512 * n, 512) for n in range(4)]
    out += [("w_in", 0, D, W_IN[n], 512) for n in ("glaqk", "vg", "qa", "ka", "va", "rg")]
    out += [("w_out", 0, D, 512 * n, 512) for n in range(2)]
    out += [("w_xq", 0, D, 512 * n, 512) for n in range(2)]
    out += [("w_xo", 0, D, 512 * n, 512) for n in range(2)]
    mlp = lambda up, down: [(up, 0, D, 512 * c, 512) if kind == "up" else (down, 512 * c, 512, 0, D)
                            for kind, c in mlp_order()]
    out += mlp("w_up", "w_down")
    width = B_HEADS * B_DIM
    for p in range(PATTERNS):
        out += [("w_in_2", 0, D, 1024 + (PATTERNS * n + p) * width, 512) for n in range(3)]
    out += [("w_in_2", 0, D, 512 * n, 512) for n in range(2)]
    out += [("w_in_2", 0, D, 1024 + 3 * PATTERNS * width + 512 * n, 512) for n in range(4)]
    out += [("w_branch_a_2", 0, 512, 0, D), ("w_branch_b_2", 0, 512, 0, D)]
    out += [("w_out_2", 0, D, 512 * n, 512) for n in range(2)]
    out += mlp("w_up_2", "w_down_2")
    return out


GROUPS = stream_groups()
TILES = 4 * len(GROUPS)
RAW = 2



class Step:

    def __init__(self, kind, banks, fill, *, n=0, h=0, p=None, out=None, major=None, src=None, dst=None, rows=KC,
                 half=0, first=False, splits=(), tile=None, slots_free=None, ready=None, bank=0, blk=0, mid=None,
                 after=None, tiles=TT, gains=(), chunks=(), after_rows=None, row=None, row_n=0, qk_ready=None,
                 roped=None, packed=None, rstd=None, xn=None, hi=None, xrows=None, smax=None, merged=None, relu=None):
        self.kind, self.banks, self.fill = kind, banks, fill
        self.n, self.h, self.p = n, h, p
        self.out, self.major, self.src, self.dst = out, major, src, dst
        self.rows, self.half, self.bank, self.blk, self.mid = rows, half, bank, blk, mid
        self.first, self.splits, self.tile, self.slots_free = first, splits, tile, slots_free
        self.ready, self.qk_ready, self.after, self.after_rows = ready, qk_ready, after, after_rows
        self.tiles, self.gains, self.chunks, self.row, self.row_n = tiles, gains, chunks, row, row_n
        self.roped, self.packed, self.rstd, self.xn, self.hi, self.xrows, self.smax, self.merged, self.relu = (
            roped, packed, rstd, xn, hi, xrows, smax, merged, relu)


class Schedule:

    def __init__(self):
        self.items, self.body, self.open = [], None, []
        self.fills, self.counts = [0] * 8, {}
        self.group = 0
        self.last_bank = None

    def fill(self, bank):
        c = [self.fills[bank], 0]
        self.fills[bank] += 1
        if self.body is not None:
            self.open.append((c, ("bank", bank)))
        return c

    def fills_of(self, bank):
        c = [self.fills[bank], 0]
        if self.body is not None:
            self.open.append((c, ("bank", bank)))
        return c

    def count(self, name, n):
        c = [self.counts.get(name, 0), 0]
        self.counts[name] = c[0] + n
        if self.body is not None:
            self.open.append((c, ("count", name)))
        return c

    def add(self, kind, banks=(), counts=(), **more):
        fields = dict(more)
        for name, n in dict(counts).items():
            fields[name] = self.count(name, n)
        st = Step(kind, list(banks), [self.fill(b) for b in banks], **fields)
        (self.items if self.body is None else self.body).append(st)
        return st

    def begin_loop(self, turns):
        self.turns, self.body, self.open = turns, [], []
        self.before = (list(self.fills), dict(self.counts), self.group)

    def end_loop(self):
        fills, counts, group = self.before
        growth = {("bank", b): self.fills[b] - fills[b] for b in range(8)}
        growth |= {("count", n): v - counts.get(n, 0) for n, v in self.counts.items()}
        growth["tile"] = 4 * (self.group - group)
        for c, key in self.open:
            c[1] = growth[key]
        more = self.turns - 1
        for b in range(8):
            self.fills[b] += more * growth["bank", b]
        for n in self.counts:
            self.counts[n] += more * growth["count", n]
        self.group += more * (self.group - group)
        self.items.append((self.turns, self.body))
        self.body, self.open = None, []

    def gemm(self, out, major, src, rows=KC, banks=4, halves=1, ready=None, blk=0, mid=None, dst=None, p=None,
             after=None):
        g = self.group
        self.group += 1
        steps = halves * banks
        free_bank = self.last_bank
        slots_free = None if g == 0 else (free_bank, self.fills_of(free_bank))
        for i in range(steps):
            half, b = divmod(i, banks)
            splits = [4 * (g + 1) + j for j in range(4) if j * steps // 4 == i and g + 1 < len(GROUPS)]
            tiles = []
            for t in splits + [4 * g]:
                c = [t, 0]
                if self.body is not None:
                    self.open.append((c, "tile"))
                tiles.append(c)
            counts = {"up": {"hi": 1, "relu": 1}, "merge": {"hi": 1, "merged": 1}, "rope": {"packed": 1}}.get(out, {})
            st = self.add("gemm", [b], counts, out=out, major=major, src=src, rows=rows, half=half,
                          first=(b == 0), splits=tiles[:-1], tile=tiles[-1], slots_free=slots_free,
                          ready=ready if i == 0 else None, bank=b, blk=blk, mid=mid, dst=dst, p=p, after=after)
        self.last_bank = banks - 1
        return st


def at(count, turn, plus=0):
    value, growth = count
    if turn is None or growth == 0:
        return value + plus
    assert value + plus > 0
    return turn * growth + (value + plus)


SIDE = (4, 5, 6, 7)
CAUSAL = [(i, k) for i in range(TT) for k in range(i + 1)]
BAND = [(i, k) for i in range(TT) for k in range(max(0, i - 1), min(TT, i + 2))]
OWN = [(i, i) for i in range(TT)]
PAIRS = [(j, i) for i in range(TT) for j in range(i)]


def make_schedule():
    s = Schedule()
    s.rows_done = None

    def norm(src, tiles, gain, dst, src_ready):
        ready = [(b, s.fills_of(b), 0) for b in range(TT)] if src_ready == "evac" else src_ready
        st = s.add("scale", counts={"rstd": tiles, "xn": tiles}, src=src, tiles=tiles, ready=ready, after_rows=s.rows_done)
        return transposed(tiles, [gain] * KC, dst, st.xn)

    def transposed(tiles, gains, dst, src):
        chunks = [4, 5, 6, 7, 0, 1, 2, 3] if src == "mix" else list(range(KC))
        st = s.add("turn", SIDE + SIDE, {"hi": KC}, tiles=tiles, gains=gains, dst=dst, src=src, chunks=chunks,
                   ready=all_out() if src == "mix" else None)
        return [(SIDE[c % 4], st.fill[chunks.index(c)], 1) for c in range(KC)]

    def ready():
        return [(b, s.fills_of(b), 0) for b in range(4)]

    def all_out():
        return [(b, s.fills_of(b), 0) for b in range(8)]

    def filled_by(st):
        return [(b, f, 1) for b, f in zip(st.banks, st.fill)]

    def run_mlp(dst, act_ready):
        def up(act_ready, c):
            s.gemm("up", "T", "act", ready=act_ready, mid=c % 2)

        def down(mid_ready, c):
            s.gemm("add", "tok", "mid", rows=4, halves=2, ready=mid_ready, mid=c % 2, dst=dst)

        up(act_ready, 0)
        s.begin_loop((CHUNKS - 2) // 2)
        even = ready()
        up(None, 1)
        odd = ready()
        down(even, 0)
        up(None, 2)
        down(odd, 1)
        s.end_loop()
        even = ready()
        up(None, 1)
        odd = ready()
        down(even, 0)
        down(odd, 1)

    def rows(name, src, row_n):
        st = s.add("rows", counts={"rstd": TT, "xrows": TT}, ready=ready(), row=name, src=src, row_n=row_n)
        s.rows_done = st.xrows

    s.add("start")
    s.add("relbias", (4,))
    mem_ready = norm("mem", MT, "norm_mem", "memT", "mem")
    act_ready = norm("x", TT, "norm_mix", "act", "x")
    s.gemm("kx", "T", "memT", ready=mem_ready, blk=0)
    s.gemm("kx", "T", "memT", blk=1)
    s.gemm("vx", "tok", "memT", banks=2, blk=0)
    s.gemm("vx", "tok", "memT", banks=2, blk=1)
    near_ready = filled_by(s.add("flip", SIDE))
    s.gemm("glaqk", "T", "act", ready=act_ready)
    qk_ready = ready()
    s.glr = s.add("glr", (4,))
    s.add("gate", (5, 6), qk_ready=qk_ready)
    s.gemm("vg", "tok", "act")
    s.gemm("qa", "T", "act")
    s.gemm("ka", "T", "act")
    s.gemm("va", "tok", "act")
    s.gemm("rg", "tok", "act")
    s.levels = [s.add("level", SIDE, n=n, ready=ready(), qk_ready=qk_ready) for n in range(len(LEVELS) + 1)]
    s.add("far", [SIDE[n % 4] for n in range(len(PAIRS))])
    s.add("glaout", SIDE)
    qk = s.add("sa_qk", SIDE, {"smax": 4}, h=0, ready=near_ready)
    for h in range(A_HEADS):
        t = s.add("sa_t", (0, 1, 2), h=h, ready=filled_by(qk))
        if h + 1 < A_HEADS:
            qk = s.add("sa_qk", SIDE, {"smax": 4}, h=h + 1)
        s.add("sa_pv", (3,), h=h, ready=filled_by(t))
    mix_ready = transposed(TT, [None] * 4 + ["g_norm"] * 4, "mid", "mix")
    s.gemm("add", "tok", "mid", ready=mix_ready, dst="x", blk=0, after="x_back")
    s.gemm("add", "tok", "mid", dst="x", blk=1)
    act_ready = norm("x", TT, "norm_xattn", "act", "evac")
    s.gemm("qx", "T", "act", ready=act_ready, blk=0)
    s.gemm("qx", "T", "act", blk=1)
    s.add("ca_qk", (4, 5), {"smax": 1}, h=0, ready=ready())
    for h in range(X_HEADS):
        if h + 1 < X_HEADS:
            s.add("ca_qk", (6, 7) if h % 2 == 0 else (4, 5), {"smax": 1}, h=h + 1, ready=[])
        t = s.add("ca_t", (0, 1), h=h)
        s.add("ca_pv", (2, 3), {"hi": 2}, h=h, ready=filled_by(t))
    ox_ready = [(2 + c % 2, [s.fills[2 + c % 2] - (X_HEADS - 1 - c // 2), 0], 0) for c in range(KC)]
    s.add("load2", ready=all_out())
    s.gemm("add", "tok", "mid", ready=ox_ready, dst="x", blk=0)
    s.gemm("add", "tok", "mid", dst="x", blk=1)
    act_ready = norm("x", TT, "norm_mlp", "act", "evac")
    run_mlp("x", act_ready)
    rows("norm_final", "x", 1)
    act_ready = norm("x", TT, "norm_mix_pre_2", "act", "rows")
    roped = None
    for p in range(PATTERNS):
        s.gemm("rope", "T", "act", ready=act_ready if p == 0 else None, dst="q", p=p, after=roped)
        roped = s.add("rope", counts={"roped": 1, "packed": 0}, dst="q", p=p).roped
        s.gemm("rope", "T", "act", dst="k", p=p, after=roped)
        roped = s.add("rope", counts={"roped": 1, "packed": 0}, dst="k", p=p).roped
        s.gemm("v2", "tok", "act", p=p)
        qk_banks = lambda h: SIDE if p == 0 else (SIDE[h],)
        blocks = len(BAND if p == 0 else OWN)
        pt_banks = range((blocks + 3) // 4)
        v_ready = ready()
        qk = s.add("bt_qk", qk_banks(0), {"smax": 1}, h=0, p=p, roped=roped)
        for h in range(B_HEADS):
            t = s.add("bt_t", pt_banks, h=h, p=p, ready=filled_by(qk))
            if h + 1 < B_HEADS:
                qk = s.add("bt_qk", qk_banks(h + 1), {"smax": 1}, h=h + 1, p=p, roped=roped)
            s.add("bt_pv", (3,), h=h, p=p, ready=filled_by(t) + (v_ready[:3] if h == 0 else []))
        s.add("stats", p=p, ready=all_out())
    attended = all_out()
    s.gemm("u", "T", "act")
    s.add("joint", ready=attended)
    s.gemm("v", "tok", "act")
    s.add("ybsum", ready=attended)
    s.add("lnv", counts={"rstd": 1}, ready=ready(), row_n=3)
    ya = s.add("spatial", SIDE, {"hi": 4, "merged": 4})
    s.add("ybsplit", counts={"hi": 1}, ready=all_out())
    for n in range(4):
        s.gemm("gate", "T", "act", blk=n)
    s.gemm("bra", "T", "mid", rows=4, halves=2, mid=0, ready=filled_by(ya))
    s.gemm("merge", "T", "mid", rows=4, halves=2, mid=1, after="yb")
    merged_ready = ready() * 2
    s.gemm("copy", "tok", "act", ready=merged_ready, dst="y", blk=0)
    s.gemm("copy", "tok", "act", dst="y", blk=1)
    rows("norm_mix_post_2", "y", 4)
    act_ready = norm("x", TT, "norm_mlp_pre_2", "act", "rows")
    s.add("clear", ready=all_out())
    run_mlp("y", act_ready)
    rows("norm_mlp_post_2", "y", 5)
    s.add("store")
    return s



def two_blocks(nc, a, out):
    s = make_schedule()
    with ExitStack() as ctx:
        def sem(name):
            return ctx.enter_context(nc.semaphore(name))

        slab_bytes = 212800
        base = -(-nc.sbuf_base // 64) * 64
        ctx.enter_context(nc.sbuf_tensor("slab", [P, slab_bytes], mybir.dt.uint8, align_bytes=64))
        top = [0]
        KB = 1024
        region = {}
        for name, size in (("x", 16 * KB), ("raw", 8 * KB), ("whi", 32 * KB), ("wlo", 32 * KB), ("act", 32 * KB),
                           ("mid", 32 * KB), ("y", 16 * KB), ("v", 8 * KB), ("u", 8 * KB), ("const", 23 * KB)):
            region[name] = top[0]
            top[0] += size
        assert top[0] <= slab_bytes, top[0]

        def place(name, where, shape, dtype=F32, skip=0):
            return nc.alloc_sbuf_tensor_at(name, [P] + shape, dtype, offset=base + region[where] + skip)

        x = place("x_tok", "x", [TT, D])
        w_raw = place("w_raw", "raw", [RAW, WORDS])
        w_hi = place("w_hi", "whi", [8, WORDS], F32R)
        w_lo = place("w_lo", "wlo", [8, WORDS], F32R)
        act_hi = place("act_hi", "act", [KC, T], F32R)
        act_lo = place("act_lo", "act", [KC, T], F32R, 16 * KB)
        mid_hi = [place(f"mid_hi{n}", "mid", [4, T], F32R, 16 * KB * n) for n in range(2)]
        mid_lo = [place(f"mid_lo{n}", "mid", [4, T], F32R, 16 * KB * n + 8 * KB) for n in range(2)]
        y = place("y_tok", "y", [TT, D])

        cat = [0]

        def const(name, shape, dtype=F32, rows=P):
            n = int(np.prod(shape)) * 4
            t = nc.alloc_sbuf_tensor_at(name, [rows] + shape, dtype, offset=base + region["const"] + cat[0])
            cat[0] += -(-n // 32) * 32
            assert cat[0] <= 23 * KB, (name, cat[0])
            return t

        ident = const("ident", [P])
        cols = const("cols", [NCOLS])
        row = const("row", [D])
        eps = const("eps", [1])
        sumsq = const("sumsq", [16])
        lnv = const("lnv", [16])
        rstd = const("rstd", [16])
        phase = cat[0]
        lvl_mask = const("lvl_mask", [len(LEVELS) + 1, P], I32)
        w_gu = const("w_gu", [G_HEADS * G_DK], rows=G_RANK)
        glr_t = const("glr_t", [T], rows=G_RANK)
        near = const("near", [A_HEADS, NEAR])
        bucket = place("bucket", "const", [REL], skip=cat[0] - 8 * KB)
        table = place("table", "const", [A_HEADS], skip=cat[0] - 4 * KB)
        bias_row = place("bias_row", "const", [REL], skip=cat[0] - 10 * KB)
        mirror = const("mirror", [P])
        nmax = const("nmax", [A_HEADS, TT])
        den = const("den", [A_HEADS, TT])
        rden = const("rden", [A_HEADS, TT])
        decay = const("decay", [2, TT])
        cat[0] = phase
        cosine = const("cosine", [T])
        sine = const("sine", [T])
        band = const("band", [3 * P])
        own = const("own", [P])
        pack = const("pack", [T])
        ya_sum = place("ya_sum", "const", [2, T], skip=cat[0] - 2 * KB)
        turned = const("turned", [T])
        mden = const("mden", [PATTERNS, TT, B_HEADS, 2])
        nbias = const("nbias", [B_HEADS, TT])
        nat = const("nat", [PATTERNS, TT, B_HEADS, 2])
        least = const("least", [TT, B_HEADS])
        ex = const("ex", [PATTERNS, TT, B_HEADS])
        zd = const("zd", [PATTERNS, TT, B_HEADS])
        share = const("share", [PATTERNS, TT, B_HEADS])
        vstat = const("vstat", [TT, 6])
        vmean = const("vmean", [TT, 2])
        ws_t = place("ws_t", "const", [4, P], skip=cat[0])
        bs_row = place("bs_row", "const", [4, P], skip=cat[0] + 2 * KB)
        assert cat[0] + 4 * KB <= 23 * KB

        mem = place("mem_tok", "v", [MT, D])
        memn = place("mem_n", "u", [MT, D])
        mem_hi = place("mem_hi", "mid", [KC, M], F32R)
        mem_lo = place("mem_lo", "mid", [KC, M], F32R, 8 * KB)
        kx = place("kx", "v", [KC, M])
        vx = place("vx", "u", [MT, D])
        qk_g = place("qk_g", "mid", [4, T])
        vg = place("vg", "mid", [TT, 4 * P], skip=8 * KB)
        sg = place("sg", "mid", [TT, 4 * P], skip=16 * KB)
        va = place("va", "mid", [TT, 4 * P], skip=24 * KB)
        g_hi = place("g_hi", "mid", [KC, P], F32R, 16 * KB)
        g_lo = place("g_lo", "mid", [KC, P], F32R, 20 * KB)
        g_raw = place("g_raw", "mid", [KC, G_RANK], skip=24 * KB)
        og = place("og", "mid", [TT, 4 * P])
        qa = place("qa", "y", [4, T])
        ka = place("ka", "y", [4, T], skip=8 * KB)
        cum = place("cum", "x", [2, T])
        ex_g = place("ex_g", "x", [2, T], skip=4 * KB)
        lev = [place(f"lev{n}", "x", [2, T], skip=(8 + 4 * n) * KB) for n in range(2)]
        near_back = place("near_back", "x", [A_HEADS, NEAR])
        a_own = place("a_own", "act", [2, TT, 2, P])
        a_far = place("a_far", "act", [2, len(PAIRS), 2, P], skip=8 * KB)
        q_far = place("q_far", "act", [2, T], skip=20 * KB)
        k_far = place("k_far", "act", [2, T], skip=24 * KB)
        q_mid = place("q_mid", "act", [2, 3, P], skip=28 * KB)
        n_causal = len(CAUSAL) * P
        p_a = [place(f"p_a{n}", "act", [n_causal], skip=n * 4 * n_causal) for n in range(2)]
        pt_a = [place(f"pt_a{n}", "act", [n_causal], skip=(2 + n) * 4 * n_causal) for n in range(2)]
        o_a = place("o_a", "act", [TT, 4 * P], skip=24 * KB)
        qx = place("qx", "y", [KC, T])
        p_x = [place(f"p_x{n}", "act", [TT, M], skip=n * 4 * KB) for n in range(2)]
        pt_x = [place(f"pt_x{n}", "act", [MT, T], skip=(8 + 4 * n) * KB) for n in range(2)]
        relu = [place(f"relu{n}", "v", [T], skip=2 * n * KB) for n in range(2)]
        square = [place(f"square{n}", "v", [T], skip=(4 + 2 * n) * KB) for n in range(2)]
        qk_b = {"q": place("q_b", "mid", [B_HEADS, T], skip=16 * KB), "k": place("k_b", "mid", [B_HEADS, T], skip=24 * KB)}
        n_band = len(BAND) * P
        p_b = [place(f"p_b{n}", "mid", [n_band], skip=n * 4 * n_band) for n in range(2)]
        pt_b = place("pt_b", "mid", [n_band], skip=8 * n_band)
        v_b = place("v_b", "v", [TT, 4 * P])
        u_b = [place("u_b0", "y", [B_HEADS, T]), place("u_b1", "y", [B_HEADS, T], skip=8 * KB), place("u_b2", "u", [B_HEADS, T])]
        wide = [place("wide0", "v", [T, B_HEADS]), place("wide1", "mid", [T, B_HEADS]), place("wide2", "mid", [T, B_HEADS], skip=8 * KB)]
        ut = place("ut", "mid", [4, T], skip=16 * KB)
        vt = place("vt", "mid", [TT, 4 * P], skip=24 * KB)
        gate = [place(f"gate{n}", *(("y", [4, T], F32, 8 * KB * n) if n < 2 else (("v", "u")[n - 2], [4, T]))) for n in range(4)]
        junk = {"x": y, "mem": memn, "y1": place("junk_mid", "mid", [TT, D]), "y2": place("junk_act", "act", [TT, D])}

        psum = ctx.enter_context(nc.psum_tensor("banks", [P, 8, 512], F32))
        bias_dram = nc.dram_tensor("bias_dram", [A_HEADS, REL], F32).ap()
        stat_dram = nc.dram_tensor("stat_dram", [PATTERNS, T, B_HEADS * 2], F32).ap()
        share_dram = nc.dram_tensor("share_dram", [PATTERNS, T * B_HEADS], F32).ap()

        bank_done = [sem(f"bank_done{b}") for b in range(8)]
        bank_free = [sem(f"bank_free{b}") for b in range(8)]
        raw_in = [sem(f"raw_in{n}") for n in range(RAW)]
        hi_w = sem("hi_w")
        lo_w = sem("lo_w")
        hi_made = sem("hi_made")
        relu_made = sem("relu_made")
        square_made = sem("square_made")
        rstd_made = sem("rstd_made")
        xn_made = sem("xn_made")
        x_rows = sem("x_rows")
        mem_in, x_in, cols_in, const_in, glr_in, table_in = (sem(n) for n in ("mem_in", "x_in", "cols_in", "const_in", "glr_in", "table_in"))
        glr_hi, glr_lo, gate_abs, gate_log, cum_made = (sem(n) for n in ("glr_hi", "glr_lo", "gate_abs", "gate_log", "cum_made"))
        pad_made, lev_diff, lev_exp, lev_made, far_exp, far_made, far_diff, own_clear = (
            sem(n) for n in ("pad_made", "lev_diff", "lev_exp", "lev_made", "far_exp", "far_made", "far_diff", "own_clear"))
        sq_g, ss_g, rstd_g = sem("sq_g"), sem("ss_g"), sem("rstd_g")
        sig_made = sem("sig_made")
        smax = sem("smax")
        px_made = sem("px_made")
        bias_out, near_in = sem("bias_out"), sem("near_in")
        bias_made = sem("bias_made")
        mirror_in = sem("mirror_in")
        x_back = sem("x_back")
        packed, roped = sem("packed"), sem("roped")
        row_in = sem("row_in")
        stat_out, nat_in, joint_diff, joint_exp, share_made, share_out = (
            sem(n) for n in ("stat_out", "nat_in", "joint_diff", "joint_exp", "share_made", "share_out"))
        wide_in = [sem(f"wide_in{p}") for p in range(PATTERNS)]
        yb_sum, yb_split, vn_stats, vn_made = sem("yb_sum"), sem("yb_split"), sem("vn_stats"), sem("vn_made")
        ws_in = sem("ws_in")
        b2_in = sem("b2_in")
        merged = sem("merged")
        y_clear = sem("y_clear")
        stored = sem("stored")
        dve_step, act_step, pool_step = sem("dve_step"), sem("act_step"), sem("pool_step")

        def wait(eng, s_, value):
            if not isinstance(value, int) or value > 0:
                eng.wait_ge(s_, value)

        def wait_ready(eng, ready, turn):
            for b, count, plus in ready:
                wait(eng, bank_free[b], at(count, turn, plus))

        def walk(eng, handle):
            for item in s.items:
                if isinstance(item, tuple):
                    turns, body = item
                    with eng.Fori(0, turns) as turn:
                        for st in body:
                            handle(st, turn)
                else:
                    handle(item, None)

        def col(name, n=0, rows=P):
            return cols[0:rows, COLS[name] + n:COLS[name] + n + 1]

        def per_pattern(ap, p):
            return ap if p == 0 else ap.rearrange("q (r m) -> q m r", r=4)

        def natural(ap, p):
            return ap if p == 0 else ap.rearrange("q (m r) -> q m r", r=4)

        def over(ap, n):
            return ap.unsqueeze(1).broadcast_to([ap.shape[0], n, ap.shape[1]])

        def each(ap, n):
            return ap.unsqueeze(2).broadcast_to([ap.shape[0], ap.shape[1], n])

        def copies_of(st):
            b, half = st.bank, st.half
            full = psum[:, b, :]
            if st.out == "kx":
                return kx[:, 4 * st.blk + b, :], psum[:, b, 0:M], 1.0, b % 2 == 0
            if st.out == "vx":
                return vx[:, b, 512 * st.blk:512 * st.blk + 512], full, 1.0, b % 2 == 0
            if st.out == "glaqk":
                return qk_g[:, b, :], full, G_DK ** -0.5 if b < 2 else 1.0, b % 2 == 0
            if st.out == "vg":
                return vg[:, b, :], full, 1.0, b % 2 == 0
            if st.out == "va":
                return va[:, b, :], full, 1.0, b % 2 == 0
            if st.out == "qa":
                return qa[:, b, :], full, A_DIM ** -0.5, b % 2 == 0
            if st.out == "ka":
                return ka[:, b, :], full, 1.0, b % 2 == 0
            if st.out == "qx":
                return qx[:, 4 * st.blk + b, :], full, X_DIM ** -0.5, b % 2 == 0
            if st.out == "v2":
                return v_b[:, b, :], full, 1.0, b % 2 == 0
            if st.out == "copy":
                return y[:, b, 512 * st.blk:512 * st.blk + 512], full, 1.0, b % 2 == 0
            return None

        def blocks_of(p):
            return BAND if p == 0 else OWN

        block = ctx.enter_context(nc.Block())

        @block.sync
        def _(sp):
            sp.dma_start(mem[:], a["mem"].rearrange("(t p) d -> p t d", p=P)).then_inc(mem_in, 16)
            sp.dma_start(cols[:], a["cols"]).then_inc(cols_in, 16)
            sp.dma_start(ident[:], a["ident"]).then_inc(cols_in, 16)
            sp.dma_start(x[:], a["x"].rearrange("(t p) d -> p t d", p=P)).then_inc(x_in, 16)
            sp.dma_start(mirror[:], a["mirror"]).then_inc(mirror_in, 16)
            for t in range(RAW):
                sp.dma_start(w_raw[:, t, :], a["weights"][t]).then_inc(raw_in[t], 16)
            with sp.Fori(1, TILES // RAW) as n:
                for slot in range(RAW):
                    sp.wait_ge(lo_w, n * RAW + (slot + 1 - RAW))
                    sp.dma_start(w_raw[:, slot, :], a["weights"][bass.ds(n * RAW + slot, 1)].rearrange("o p w -> p (o w)")
                                 ).then_inc(raw_in[slot], 16)
            for tt in range(TT):
                sp.wait_ge(x_rows, s.counts["xrows"] - TT + tt + 1)
                sp.dma_start(out[P * tt:P * tt + P, :], x[:, tt, :]).then_inc(stored, 16)
            sp.wait_ge(stored, 16 * TT)

        def split_waits(eng, st, turn):
            if st.slots_free is not None:
                b, count = st.slots_free
                wait(eng, bank_done[b], at(count, turn))

        @block.tensor
        def _(pe):
            def product(out_ap, lhs, rhs, start, stop):
                pe.matmul(out_ap, lhs[0], rhs[0], start=start, stop=False)
                pe.matmul(out_ap, lhs[0], rhs[1], start=False, stop=False)
                return pe.matmul(out_ap, lhs[1], rhs[0], start=False, stop=stop)

            def begin(bank, count, turn):
                wait(pe, bank_free[bank], at(count, turn))

            def gemm(st, turn):
                begin(st.bank, st.fill[0], turn)
                set_at = 4 * (st.tile[0] // 4 % 2)
                b = st.bank
                if st.after == "yb" and st.half == 0 and b == 0:
                    pe.wait_ge(yb_split, 1)
                for k in range(st.rows):
                    tile = k // 2 + st.half * (st.rows // 2)
                    if st.first and k % 2 == 0:
                        pe.wait_ge(lo_w, at(st.tile, turn, tile + 1))
                    if st.ready is not None:
                        wait_ready(pe, st.ready[k:k + 1], turn)
                    if st.src == "mid":
                        n = k // 4 if st.mid is None else st.mid
                        act = (mid_hi[n][:, k % 4, :], mid_lo[n][:, k % 4, :])
                    elif st.src == "memT":
                        act = (mem_hi[:, k, :], mem_lo[:, k, :])
                    else:
                        act = (act_hi[:, k, :], act_lo[:, k, :])
                    w = [x_[:, set_at + tile, (k % 2) * 512:(k % 2) * 512 + 512] for x_ in (w_hi, w_lo)]
                    start, stop = k == 0, k == st.rows - 1
                    if st.major == "T":
                        n = M if st.src == "memT" else T
                        mm = product(psum[:, b, 0:n], [x_[:, b * P:b * P + P] for x_ in w], act, start, stop)
                    else:
                        if st.out == "v2" and st.p > 0:
                            act = [x_.rearrange("q (m r) -> q r m", r=4)[:, b, :] for x_ in act]
                        else:
                            act = [x_[:, b * P:b * P + P] for x_ in act]
                        mm = product(psum[:, b, :], act, w, start, stop)
                mm.then_inc(bank_done[b], 1)

            def handle(st, turn):
                k = st.kind
                if k == "gemm":
                    gemm(st, turn)
                elif k == "flip":
                    pe.wait_ge(mirror_in, 16)
                    pe.wait_ge(near_in, 16)
                    for n in range(4):
                        begin(SIDE[n], st.fill[n], turn)
                        pe.matmul(psum[:, SIDE[n], :], mirror[:], near_back[:, 2 * n:2 * n + 2, :].rearrange("q h j -> q (h j)"),
                                  start=True, stop=True).then_inc(bank_done[SIDE[n]], 1)
                elif k == "turn":
                    for half in range(2):
                        chunks = st.chunks[4 * half:4 * half + 4]
                        for n in range(4):
                            begin(SIDE[n], st.fill[4 * half + n], turn)
                        for tt in range(st.tiles):
                            if half == 0 and st.src != "mix":
                                pe.wait_ge(xn_made, at(st.src, turn, tt + 1))
                            if half == 0 and tt == 0 and st.src == "mix":
                                wait_ready(pe, st.ready, turn)
                            for c in chunks:
                                if st.src == "mix":
                                    src = o_a[:, tt, c * P:c * P + P] if c < 4 else og[:, tt, (c - 4) * P:(c - 3) * P]
                                else:
                                    src = (y if st.tiles == TT else memn)[:, tt, c * P:c * P + P]
                                mm = pe.transpose(psum[:, SIDE[c % 4], tt * P:tt * P + P], src, ident[:])
                                if tt == st.tiles - 1:
                                    mm.then_inc(bank_done[SIDE[c % 4]], 1)
                elif k == "glr":
                    begin(4, st.fill[0], turn)
                    pe.wait_ge(glr_lo, 1)
                    for c in range(KC):
                        mm = product(psum[:, 4, :], (g_hi[:, c, :], g_lo[:, c, :]), (act_hi[:, c, :], act_lo[:, c, :]),
                                     c == 0, c == KC - 1)
                    mm.then_inc(bank_done[4], 1)
                elif k == "gate":
                    wait(pe, bank_free[4], at(s.glr.fill[0], None, 1))
                    pe.wait_ge(const_in, 32)
                    for pair in range(2):
                        b = 5 + pair
                        begin(b, st.fill[pair], turn)
                        pe.matmul(psum[:, b, :], w_gu[:, pair * P:pair * P + P], glr_t[:], start=True, stop=True
                                  ).then_inc(bank_done[b], 1)
                elif k == "relbias":
                    begin(4, st.fill[0], turn)
                    pe.wait_ge(table_in, 32)
                    pe.matmul(psum[0:A_HEADS, 4, 0:REL], table[0:RP_BUCKETS, :], bucket[0:RP_BUCKETS, :], start=True,
                              stop=True).then_inc(bank_done[4], 1)
                elif k == "level":
                    if st.n < len(LEVELS):
                        pe.wait_ge(lev_made, st.n + 1)
                    for half in range(2):
                        for kind in range(2):
                            begin(SIDE[2 * half + kind], st.fill[2 * half + kind], turn)
                        for n in range(4):
                            tt, pair = 2 * half + n // 2, n % 2
                            for kind in range(2):
                                rows = slice(64 * kind, 64 * kind + 64)
                                if st.n < len(LEVELS):
                                    lhs = rhs = lev[st.n % 2][rows, pair, tt * P:tt * P + P]
                                else:
                                    lhs = qk_g[rows, 2 + pair, tt * P:tt * P + P]
                                    rhs = qk_g[rows, pair, tt * P:tt * P + P]
                                mm = pe.matmul(psum[:, SIDE[2 * half + kind], n * P:n * P + P], lhs, rhs, start=True, stop=True)
                                if n == 3:
                                    mm.then_inc(bank_done[SIDE[2 * half + kind]], 1)
                elif k == "far":
                    pe.wait_ge(far_made, 8)
                    for fill in range(0, len(PAIRS), 2):
                        for kind in range(2):
                            begin(SIDE[(fill + kind) % 4], st.fill[fill + kind], turn)
                        for n in range(4):
                            (j, i), pair = PAIRS[fill + n // 2], n % 2
                            for kind in range(2):
                                rows, b = slice(64 * kind, 64 * kind + 64), SIDE[(fill + kind) % 4]
                                if i - j == 1:
                                    rhs = q_far[rows, pair, i * P:i * P + P]
                                else:
                                    rhs = q_mid[rows, pair, {(0, 2): 0, (1, 3): 1, (0, 3): 2}[j, i], :]
                                mm = pe.matmul(psum[:, b, n * P:n * P + P], k_far[rows, pair, j * P:j * P + P], rhs,
                                               start=True, stop=True)
                                if n == 3:
                                    mm.then_inc(bank_done[b], 1)
                elif k == "glaout":
                    for i in range(TT):
                        b = SIDE[i]
                        if i == 0:
                            for n in range(4):
                                begin(SIDE[n], st.fill[n], turn)
                        for h in range(G_HEADS):
                            for j in range(i + 1):
                                lhs = a_own[:, h % 2, i, h // 2, :] if j == i else a_far[:, h % 2, PAIRS.index((j, i)), h // 2, :]
                                mm = pe.matmul(psum[:, b, h * P:h * P + P], lhs, vg[:, j, h * P:h * P + P],
                                               start=(j == 0), stop=(j == i))
                        mm.then_inc(bank_done[b], 1)
                elif k == "sa_qk":
                    rows, pair = slice(64 * (st.h % 2), 64 * (st.h % 2) + 64), st.h // 2
                    for i in range(TT):
                        begin(SIDE[i], st.fill[i], turn)
                        pe.matmul(psum[:, SIDE[i], 0:P * (i + 1)], qa[rows, pair, i * P:i * P + P],
                                  ka[rows, pair, 0:P * (i + 1)], start=True, stop=True).then_inc(bank_done[SIDE[i]], 1)
                elif k in ("sa_t", "bt_t"):
                    blocks = CAUSAL if k == "sa_t" else blocks_of(st.p)
                    src = (p_a if k == "sa_t" else p_b)[st.h % 2]
                    wait_ready(pe, st.ready, turn)
                    for n in range(len(blocks)):
                        b = n // 4
                        if n % 4 == 0:
                            begin(b, st.fill[b], turn)
                        mm = pe.transpose(psum[:, b, n % 4 * P:n % 4 * P + P], src[:, n * P:n * P + P], ident[:])
                        if n % 4 == 3 or n == len(blocks) - 1:
                            mm.then_inc(bank_done[b], 1)
                elif k == "sa_pv":
                    begin(3, st.fill[0], turn)
                    wait_ready(pe, st.ready, turn)
                    for i in range(TT):
                        for j in range(i + 1):
                            n = CAUSAL.index((i, j))
                            mm = pe.matmul(psum[:, 3, i * A_DIM:i * A_DIM + A_DIM], pt_a[st.h % 2][:, n * P:n * P + P],
                                           va[:, j, st.h * A_DIM:st.h * A_DIM + A_DIM], start=(j == 0), stop=(j == i))
                    mm.then_inc(bank_done[3], 1)
                elif k == "ca_qk":
                    wait_ready(pe, st.ready, turn)
                    for n in range(2):
                        b = st.banks[n]
                        begin(b, st.fill[n], turn)
                        for tt in (2 * n, 2 * n + 1):
                            for e in range(2):
                                mm = pe.matmul(psum[:, b, tt % 2 * M:tt % 2 * M + M], qx[:, 2 * st.h + e, tt * P:tt * P + P],
                                               kx[:, 2 * st.h + e, :], start=(e == 0), stop=(e == 1))
                        mm.then_inc(bank_done[b], 1)
                elif k == "ca_t":
                    pe.wait_ge(px_made, st.h + 1)
                    for mt in range(MT):
                        begin(mt, st.fill[mt], turn)
                        for tt in range(TT):
                            mm = pe.transpose(psum[:, mt, tt * P:tt * P + P], p_x[st.h % 2][:, tt, mt * P:mt * P + P], ident[:])
                        mm.then_inc(bank_done[mt], 1)
                elif k == "ca_pv":
                    wait_ready(pe, st.ready, turn)
                    for e in range(2):
                        b = st.banks[e]
                        begin(b, st.fill[e], turn)
                        at_e = st.h * X_DIM + e * P
                        for mt in range(MT):
                            mm = pe.matmul(psum[:, b, :], vx[:, mt, at_e:at_e + P], pt_x[st.h % 2][:, mt, :],
                                           start=(mt == 0), stop=(mt == MT - 1))
                        mm.then_inc(bank_done[b], 1)
                elif k == "bt_qk":
                    pe.wait_ge(roped, at(st.roped, turn, 1))
                    if st.p == 0:
                        for i in range(TT):
                            begin(SIDE[i], st.fill[i], turn)
                            ks = [kt for q_, kt in BAND if q_ == i]
                            pe.matmul(psum[:, SIDE[i], 0:P * len(ks)], qk_b["q"][:, st.h, i * P:i * P + P],
                                      qk_b["k"][:, st.h, ks[0] * P:(ks[-1] + 1) * P], start=True, stop=True
                                      ).then_inc(bank_done[SIDE[i]], 1)
                    else:
                        b = st.banks[0]
                        begin(b, st.fill[0], turn)
                        for i in range(TT):
                            mm = pe.matmul(psum[:, b, i * P:i * P + P], qk_b["q"][:, st.h, i * P:i * P + P],
                                           qk_b["k"][:, st.h, i * P:i * P + P], start=True, stop=True)
                        mm.then_inc(bank_done[b], 1)
                elif k == "bt_pv":
                    begin(3, st.fill[0], turn)
                    wait_ready(pe, st.ready, turn)
                    blocks = blocks_of(st.p)
                    for i in range(TT):
                        ks = [kt for q_, kt in blocks if q_ == i]
                        for kt in ks:
                            n = blocks.index((i, kt))
                            mm = pe.matmul(psum[:, 3, i * P:i * P + P], v_b[:, kt, st.h * P:st.h * P + P],
                                           pt_b[:, n * P:n * P + P], start=(kt == ks[0]), stop=(kt == ks[-1]))
                    mm.then_inc(bank_done[3], 1)
                elif k == "spatial":
                    pe.wait_ge(ws_in, 32)
                    pe.wait_ge(vn_made, TT)
                    for g in range(4):
                        begin(SIDE[g], st.fill[g], turn)
                        for c in range(TT):
                            mm = pe.matmul(psum[:, SIDE[g], c * P:c * P + P], vt[:, c, g * P:g * P + P], ws_t[:, g, :],
                                           start=True, stop=True)
                        mm.then_inc(bank_done[SIDE[g]], 1)

            pe.wait_ge(cols_in, 32)
            walk(pe, handle)

        @block.scalar
        def _(act):
            step = [0]

            def then(ins):
                step[0] += 1
                ins.then_inc(act_step, 1)
                act.wait_ge(act_step, step[0])

            def split(st, turn):
                for tile in st.splits:
                    split_waits(act, st, turn)
                    one_split(tile, turn)

            def one_split(tile, turn):
                t = tile[0]
                act.wait_ge(raw_in[t % RAW], at([16 * (t // RAW + 1), tile[1] * 16 // RAW], turn))
                act.activation(w_hi[:, t % 8, :], w_raw[:, t % RAW, :], ACT.Copy).then_inc(hi_w, 1)

            def rms(slot, width, signal):
                then(act.activation(lnv[:, slot], sumsq[:, slot], ACT.Ln, bias=eps[:, 0:1], scale=1.0 / width))
                act.activation(rstd[:, slot], lnv[:, slot], ACT.Exp, scale=-0.5).then_inc(signal, 1)

            def gemm(st, turn):
                split(st, turn)
                b = st.bank
                filled = lambda: wait(act, bank_done[b], at(st.fill[0], turn, 1))
                plain = copies_of(st)
                if plain is not None and plain[3]:
                    filled()
                    act.activation(plain[0], plain[1], ACT.Copy, scale=plain[2]).then_inc(bank_free[b], 1)
                elif st.out == "rg":
                    filled()
                    act.activation(sg[:, b, :], psum[:, b, :], ACT.Sigmoid).then_inc(sig_made, 1)
                elif st.out == "up":
                    filled()
                    n = b % 2
                    wait(act, square_made, at(st.relu, turn, -1))
                    act.activation(relu[n][:], psum[:, b, :], ACT.Relu).then_inc(relu_made, 1)
                    act.wait_ge(relu_made, at(st.relu, turn, 1))
                    act.activation(mid_hi[st.mid][:, b, :], relu[n][:], ACT.Square).then_inc(hi_made, 1)
                elif st.out == "rope":
                    filled()
                    if b == 0 and st.after is not None:
                        act.wait_ge(roped, at(st.after, turn, 1))
                    act.activation(pack[ROPE_DIM * b:ROPE_DIM * b + ROPE_DIM, :], psum[0:ROPE_DIM, b, :], ACT.Copy
                                   ).then_inc(packed, 1)
                elif st.out == "u":
                    filled()
                    act.activation(ut[:, b, :], psum[:, b, :], ACT.Gelu_apprx_tanh).then_inc(bank_free[b], 1)
                elif st.out == "v":
                    filled()
                    act.activation(vt[:, b, :], psum[:, b, :], ACT.Gelu_apprx_tanh).then_inc(bank_free[b], 1)
                elif st.out == "gate":
                    filled()
                    if st.blk == 0 and b == 0:
                        act.wait_ge(yb_split, 1)
                    act.activation(gate[st.blk][:, b, :], psum[:, b, :], ACT.Sigmoid,
                                   bias=col("b_gate_2", 4 * st.blk + b)).then_inc(bank_free[b], 1)
                elif st.out == "merge":
                    act.wait_ge(merged, at(st.merged, turn, 1))
                    act.activation(act_hi[:, 4 * st.half + b, :], gate[st.half][:, b, :], ACT.Copy).then_inc(hi_made, 1)

            def handle(st, turn):
                k = st.kind
                if k == "start":
                    for t in range(4):
                        one_split([t, 0], None)
                    act.wait_ge(glr_in, 16)
                    act.wait_ge(pad_made, 3)
                    act.activation(g_hi[:, :, 0:G_RANK], g_raw[:], ACT.Copy).then_inc(glr_hi, 1)
                elif k == "gemm":
                    gemm(st, turn)
                elif k in ("scale", "rows"):
                    src = {"mem": mem, "x": x, "y": y}[st.src]
                    if k == "scale":
                        waste = memn if st.src == "mem" else y
                    else:
                        waste = {"norm_final": y, "norm_mix_post_2": junk["y1"], "norm_mlp_post_2": junk["y2"]}[st.row]
                    for tt in range(TT if k == "rows" else st.tiles):
                        if st.ready == "mem":
                            act.wait_ge(mem_in, 16)
                        elif st.ready == "x":
                            act.wait_ge(x_in, 16)
                        elif st.ready == "rows":
                            act.wait_ge(x_rows, at(st.after_rows, turn, tt + 1))
                        else:
                            wait_ready(act, st.ready[tt:tt + 1], turn)
                        then(act.activation(waste[:, tt, :], src[:, tt, :], ACT.Square, accum_out=sumsq[:, tt:tt + 1]))
                        rms(slice(tt, tt + 1), D, rstd_made)
                elif k == "turn":
                    for n_c, c in enumerate(st.chunks):
                        b, n = SIDE[c % 4], P * st.tiles
                        wait(act, bank_done[b], at(st.fill[n_c], turn, 1))
                        hi = {"act": act_hi, "memT": mem_hi}[st.dst][:, c, :] if st.dst != "mid" else mid_hi[c // 4][:, c % 4, :]
                        gain = st.gains[c]
                        scale = 1.0 if gain is None else col(gain, 0 if gain == "g_norm" else c)
                        act.activation(hi, psum[:, b, 0:n], ACT.Copy, scale=scale).then_inc(hi_made, 1)
                elif k == "gate":
                    for pair in range(2):
                        act.wait_ge(bank_done[5 + pair], at(st.fill[pair], turn, 1))
                        act.activation(ex_g[:, pair, :], psum[:, 5 + pair, :], ACT.Abs, bias=col("b_gate", pair)
                                       ).then_inc(gate_abs, 1)
                    act.wait_ge(gate_abs, 2)
                    then(act.activation(ex_g[:], ex_g[:], ACT.Exp, scale=-1.0))
                    act.activation(ex_g[:], ex_g[:], ACT.Ln, bias=1.0).then_inc(gate_log, 1)
                    for n in range(2):
                        act.wait_ge(lev_diff, 2 * n + 2)
                        act.activation(ex_g[:], ex_g[:], ACT.Exp, scale=1.0 / G_NORM).then_inc(lev_exp, 1)
                elif k == "flip":
                    for n in range(0, 4, 2):
                        act.wait_ge(bank_done[SIDE[n]], at(st.fill[n], turn, 1))
                        act.activation(near[:, 2 * n:2 * n + 2, :].rearrange("q h j -> q (h j)"), psum[:, SIDE[n], :], ACT.Copy
                                       ).then_inc(bank_free[SIDE[n]], 1)
                elif k == "level":
                    n = st.n + 2
                    if n < len(LEVELS):
                        act.wait_ge(lev_diff, 2 * n + 2)
                        act.activation(ex_g[:], ex_g[:], ACT.Exp, scale=1.0 / G_NORM).then_inc(lev_exp, 1)
                    if st.n == 0:
                        act.wait_ge(cum_made, 2)
                        wait_ready(act, st.ready, turn)
                        then(act.activation(q_far[:], cum[:], ACT.Exp, scale=1.0 / G_NORM))
                        last = cum[:].rearrange("q c (t n) -> q c t n", t=TT)[:, :, :, P - 1]
                        then(act.activation(decay[:], last, ACT.Exp, scale=1.0 / G_NORM))
                        act.wait_ge(far_diff, TT * 2)
                        act.activation(k_far[:], k_far[:], ACT.Exp, scale=1.0 / G_NORM).then_inc(far_exp, 1)
                elif k == "far":
                    for n in range(0, len(PAIRS), 2):
                        b = SIDE[n % 4]
                        act.wait_ge(bank_done[b], at(st.fill[n], turn, 1))
                        act.activation(a_far[:, n % 2, n - n % 2:n - n % 2 + 2].rearrange("q t c i -> q (t c i)"), psum[:, b, :], ACT.Copy).then_inc(bank_free[b], 1)
                elif k == "glaout":
                    for i in range(TT):
                        act.wait_ge(bank_done[SIDE[i]], at(st.fill[i], turn, 1))
                        wait(act, ss_g, i - 1)
                        act.activation(ex_g[:, i % 2, :], psum[:, SIDE[i], :], ACT.Square).then_inc(sq_g, 1)
                        act.wait_ge(ss_g, i + 1)
                        rms(slice(4 * i, 4 * i + 4), G_DV, rstd_g)
                elif k == "sa_qk":
                    for i in range(TT):
                        act.wait_ge(smax, at(st.smax, turn, i + 1))
                        n = CAUSAL.index((i, 0))
                        act.activation(p_a[st.h % 2][:, n * P:(n + i + 1) * P], psum[:, SIDE[i], 0:P * (i + 1)], ACT.Exp,
                                       bias=nmax[:, st.h, i:i + 1], accum_out=den[:, st.h, i:i + 1]
                                       ).then_inc(bank_free[SIDE[i]], 1)
                elif k in ("sa_t", "bt_t"):
                    dst = pt_a[st.h % 2] if k == "sa_t" else pt_b
                    n = len(CAUSAL if k == "sa_t" else blocks_of(st.p))
                    for b in range(0, (n + 3) // 4, 2):
                        w = min(4, n - 4 * b) * P
                        act.wait_ge(bank_done[b], at(st.fill[b], turn, 1))
                        act.activation(dst[:, 4 * b * P:4 * b * P + w], psum[:, b, 0:w], ACT.Copy).then_inc(bank_free[b], 1)
                elif k == "ca_qk":
                    act.wait_ge(smax, at(st.smax, turn, 1))
                    for tt in range(TT):
                        b = st.banks[tt // 2]
                        ins = act.activation(p_x[st.h % 2][:, tt, :], psum[:, b, tt % 2 * M:tt % 2 * M + M], ACT.Exp,
                                             bias=nmax[:, st.h, tt:tt + 1], accum_out=den[:, st.h, tt:tt + 1])
                        if tt % 2:
                            ins.then_inc(bank_free[b], 1)
                elif k == "ca_t":
                    act.wait_ge(bank_done[0], at(st.fill[0], turn, 1))
                    act.activation(pt_x[st.h % 2][:, 0, :], psum[:, 0, :], ACT.Copy).then_inc(bank_free[0], 1)
                elif k == "ca_pv":
                    for e in range(2):
                        b, c = st.banks[e], 2 * st.h + e
                        act.wait_ge(bank_done[b], at(st.fill[e], turn, 1))
                        act.activation(mid_hi[c // 4][:, c % 4, :], psum[:, b, :], ACT.Copy).then_inc(hi_made, 1)
                elif k == "bt_qk":
                    blocks = blocks_of(st.p)
                    act.wait_ge(smax, at(st.smax, turn, 1))
                    for i in range(TT):
                        ks = [n for n, (q_, _) in enumerate(blocks) if q_ == i]
                        w = len(ks) * P
                        src = psum[:, SIDE[i], 0:w] if st.p == 0 else psum[:, st.banks[0], i * P:i * P + P]
                        ins = act.activation(p_b[st.h % 2][:, ks[0] * P:ks[0] * P + w], src, ACT.Exp, bias=nbias[:, st.h, i:i + 1],
                                             scale=B_DIM ** -0.5, accum_out=mden[:, st.p, i, st.h, 1:2])
                        if st.p == 0:
                            ins.then_inc(bank_free[SIDE[i]], 1)
                        elif i == TT - 1:
                            ins.then_inc(bank_free[st.banks[0]], 1)
                elif k == "bt_pv":
                    act.wait_ge(bank_done[3], at(st.fill[0], turn, 1))
                    act.activation(natural(u_b[st.p][:, st.h, :], st.p), per_pattern(psum[:, 3, :], st.p), ACT.Copy
                                   ).then_inc(bank_free[3], 1)
                elif k == "joint":
                    act.wait_ge(joint_diff, 1)
                    act.activation(ex[:], ex[:], ACT.Exp, scale=B_DIM ** -0.5).then_inc(joint_exp, 1)
                elif k == "lnv":
                    act.wait_ge(vn_stats, 1)
                    then(act.activation(lnv[:, 0:TT], vmean[:, :, 1], ACT.Ln, bias=eps[:, 0:1]))
                    act.activation(rstd[:, 0:TT], lnv[:, 0:TT], ACT.Exp, scale=-0.5).then_inc(rstd_made, 1)
                elif k == "spatial":
                    for g in range(4):
                        act.wait_ge(merged, at(st.merged, turn, g + 1))
                        act.activation(mid_hi[0][:, g, :], ya_sum[:, g % 2, :], ACT.Copy).then_inc(hi_made, 1)
                elif k == "ybsplit":
                    act.wait_ge(yb_sum, 1)
                    wait_ready(act, st.ready, turn)
                    act.activation(mid_hi[1][:], u_b[0][:], ACT.Copy).then_inc(hi_made, 1)

            act.wait_ge(cols_in, 32)
            walk(act, handle)

        @block.vector
        def _(dve):
            step = [0]

            def then(ins):
                step[0] += 1
                ins.then_inc(dve_step, 1)
                dve.wait_ge(dve_step, step[0])

            def one_split(tile, turn):
                t = tile[0]
                dve.wait_ge(hi_w, at(tile, turn, 1))
                dve.tensor_tensor(w_lo[:, t % 8, :], w_raw[:, t % RAW, :], w_hi[:, t % 8, :], ALU.subtract).then_inc(lo_w, 1)

            def gemm(st, turn):
                for tile in st.splits:
                    split_waits(dve, st, turn)
                    one_split(tile, turn)
                b = st.bank
                filled = lambda: wait(dve, bank_done[b], at(st.fill[0], turn, 1))
                plain = copies_of(st)
                if plain is not None and not plain[3]:
                    filled()
                    dve.tensor_scalar(plain[0], plain[1], plain[2], None, ALU.mult).then_inc(bank_free[b], 1)
                elif st.out == "rg":
                    dve.wait_ge(sig_made, b + 1)
                    dve.tensor_tensor(sg[:, b, :], psum[:, b, :], sg[:, b, :], ALU.mult).then_inc(bank_free[b], 1)
                elif st.out == "add":
                    filled()
                    dst = {"x": x, "y": y}[st.dst]
                    col0 = 512 * (st.half if st.rows == 4 else st.blk)
                    if st.after == "x_back":
                        dve.wait_ge(x_back, 16)
                    dve.tensor_tensor(dst[:, b, col0:col0 + 512], psum[:, b, :], dst[:, b, col0:col0 + 512], ALU.add
                                      ).then_inc(bank_free[b], 1)
                elif st.out == "up":
                    n = b % 2
                    dve.wait_ge(relu_made, at(st.relu, turn, 1))
                    dve.tensor_tensor(square[n][:], relu[n][:], relu[n][:], ALU.mult).then_inc(square_made, 1)
                    dve.wait_ge(square_made, at(st.relu, turn, 1))
                    dve.wait_ge(hi_made, at(st.hi, turn, 1))
                    dve.tensor_tensor(mid_lo[st.mid][:, b, :], square[n][:], mid_hi[st.mid][:, b, :], ALU.subtract
                                      ).then_inc(bank_free[b], 1)
                elif st.out == "rope":
                    dve.wait_ge(packed, at(st.packed, turn, 1))
                    dve.tensor_copy(per_pattern(qk_b[st.dst][:, b, :], st.p), natural(psum[:, b, :], st.p)).then_inc(bank_free[b], 1)
                elif st.out == "bra":
                    filled()
                    g = gate[st.half][:, b, :]
                    dve.tensor_tensor(g, psum[:, b, :], g, ALU.mult).then_inc(bank_free[b], 1)
                elif st.out == "merge":
                    filled()
                    ga, gb = gate[st.half][:, b, :], gate[2 + st.half][:, b, :]
                    then(dve.tensor_tensor(gb, psum[:, b, :], gb, ALU.mult))
                    dve.tensor_tensor(ga, ga, gb, ALU.add).then_inc(merged, 1)
                    dve.wait_ge(merged, at(st.merged, turn, 1))
                    dve.wait_ge(hi_made, at(st.hi, turn, 1))
                    dve.tensor_tensor(act_lo[:, 4 * st.half + b, :], ga, act_hi[:, 4 * st.half + b, :], ALU.subtract
                                      ).then_inc(bank_free[b], 1)

            def handle(st, turn):
                k = st.kind
                if k == "start":
                    for t in range(4):
                        one_split([t, 0], None)
                    dve.wait_ge(glr_hi, 1)
                    dve.tensor_tensor(g_lo[:, :, 0:G_RANK], g_raw[:], g_hi[:, :, 0:G_RANK], ALU.subtract).then_inc(glr_lo, 1)
                elif k == "gemm":
                    gemm(st, turn)
                elif k == "scale":
                    src, dst = (mem, memn) if st.src == "mem" else (x, y)
                    for tt in range(st.tiles):
                        dve.wait_ge(rstd_made, at(st.rstd, turn, tt + 1))
                        dve.tensor_scalar(dst[:, tt, :], src[:, tt, :], rstd[:, tt:tt + 1], None, ALU.mult).then_inc(xn_made, 1)
                elif k == "rows":
                    dve.wait_ge(row_in, 16 * st.row_n)
                    src = {"x": x, "y": y}[st.src]
                    for tt in range(TT):
                        dve.wait_ge(rstd_made, at(st.rstd, turn, tt + 1))
                        ins = dve.scalar_tensor_tensor(src[:, tt, :], src[:, tt, :], rstd[:, tt:tt + 1], row[:], ALU.mult, ALU.mult)
                        if st.src == "y":
                            then(ins)
                            ins = dve.tensor_tensor(x[:, tt, :], x[:, tt, :], y[:, tt, :], ALU.add)
                        ins.then_inc(x_rows, 1)
                elif k == "turn":
                    for n_c, c in enumerate(st.chunks):
                        b, n = SIDE[c % 4], P * st.tiles
                        dve.wait_ge(hi_made, at(st.hi, turn, n_c + 1))
                        if st.dst == "mid":
                            hi, lo = mid_hi[c // 4][:, c % 4, :], mid_lo[c // 4][:, c % 4, :]
                        else:
                            hi, lo = [t_[:, c, :] for t_ in {"act": (act_hi, act_lo), "memT": (mem_hi, mem_lo)}[st.dst]]
                        gain = st.gains[c]
                        scale = 1.0 if gain is None else col(gain, 0 if gain == "g_norm" else c)
                        dve.scalar_tensor_tensor(lo, psum[:, b, 0:n], scale, hi, ALU.mult, ALU.subtract).then_inc(bank_free[b], 1)
                elif k == "glr":
                    dve.wait_ge(bank_done[4], at(st.fill[0], turn, 1))
                    dve.wait_ge(bias_out, 16)
                    dve.tensor_copy(glr_t[:], psum[0:G_RANK, 4, :]).then_inc(bank_free[4], 1)
                elif k == "gate":
                    for pair in range(2):
                        dve.wait_ge(gate_abs, pair + 1)
                        ins = dve.tensor_scalar(lev[0][:, pair, :], psum[:, 5 + pair, :], col("b_gate", pair), 0.0, ALU.add, ALU.min)
                        ins.then_inc(bank_free[5 + pair], 1)
                    dve.wait_ge(gate_log, 1)
                    for pair in range(2):
                        dve.wait_ge(bank_free[5 + pair], at(st.fill[pair], turn, 1))
                    then(dve.tensor_tensor(lev[0][:], lev[0][:], ex_g[:], ALU.subtract))
                    for pair in range(2):
                        for tt in range(TT):
                            part = slice(tt * P, tt * P + P)
                            ins = dve.tensor_tensor_scan(cum[:, pair, part], lev[0][:, pair, part], lev[0][:, pair, part], 0.0,
                                                         ALU.add, ALU.bypass)
                        ins.then_inc(cum_made, 1)
                elif k == "flip":
                    for n in range(1, 4, 2):
                        dve.wait_ge(bank_done[SIDE[n]], at(st.fill[n], turn, 1))
                        dve.tensor_copy(near[:, 2 * n:2 * n + 2, :].rearrange("q h j -> q (h j)"), psum[:, SIDE[n], :]
                                        ).then_inc(bank_free[SIDE[n]], 1)
                elif k == "relbias":
                    dve.wait_ge(bank_done[4], at(st.fill[0], turn, 1))
                    dve.tensor_copy(bias_row[0:A_HEADS, 0:NEAR], psum[0:A_HEADS, 4, 0:NEAR]).then_inc(bank_free[4], 1)
                    dve.memset(bias_row[0:A_HEADS, NEAR:REL], MASKED).then_inc(bias_made, 1)
                elif k == "level":
                    if st.n == 0:
                        wait_ready(dve, st.ready, turn)
                        dve.wait_ge(cum_made, 2)
                        for pair in range(2):
                            for tt in range(TT):
                                part = slice(tt * P, tt * P + P)
                                dve.tensor_scalar(k_far[:, pair, part], cum[:, pair, part], -1.0,
                                                  cum[:, pair, tt * P + P - 1:tt * P + P], ALU.mult, ALU.add).then_inc(far_diff, 1)
                    dve.wait_ge(own_clear, 1)
                    dve.wait_ge(const_in, 32)
                    for n in range(4):
                        b = SIDE[n]
                        dve.wait_ge(bank_done[b], at(st.fill[n], turn, 1))
                        own_part = a_own[:, n % 2, n // 2 * 2:n // 2 * 2 + 2].rearrange("q t c i -> q (t c) i")
                        dve.copy_predicated(own_part, over(lvl_mask[:, st.n, :], G_HEADS),
                                            psum[:, b, :].rearrange("q (h i) -> q h i", h=G_HEADS)).then_inc(bank_free[b], 1)
                    if st.n == 0:
                        dve.wait_ge(far_exp, 1)
                        dve.tensor_tensor(k_far[:], k_far[:], qk_g[:, 2:4, :], ALU.mult).then_inc(far_made, 1)
                        dve.tensor_tensor(q_far[:], q_far[:], qk_g[:, 0:2, :], ALU.mult).then_inc(far_made, 1)
                        dve.wait_ge(far_made, 2)
                        for pair in range(2):
                            dve.tensor_scalar(q_mid[:, pair, 0, :], q_far[:, pair, 2 * P:3 * P], decay[:, pair, 1:2], None,
                                              ALU.mult).then_inc(far_made, 1)
                            dve.tensor_scalar(q_mid[:, pair, 1, :], q_far[:, pair, 3 * P:4 * P], decay[:, pair, 2:3], None,
                                              ALU.mult).then_inc(far_made, 1)
                            dve.tensor_scalar(q_mid[:, pair, 2, :], q_far[:, pair, 3 * P:4 * P], decay[:, pair, 2:3],
                                              decay[:, pair, 1:2], ALU.mult, ALU.mult).then_inc(far_made, 1)
                elif k == "far":
                    for n in range(1, len(PAIRS), 2):
                        b = SIDE[n % 4]
                        dve.wait_ge(bank_done[b], at(st.fill[n], turn, 1))
                        dve.tensor_copy(a_far[:, n % 2, n - n % 2:n - n % 2 + 2].rearrange("q t c i -> q (t c i)"), psum[:, b, :]).then_inc(bank_free[b], 1)
                elif k == "glaout":
                    for i in range(TT):
                        dve.wait_ge(sq_g, i + 1)
                        dve.tensor_reduce(sumsq[:, 4 * i:4 * i + 4], ex_g[:, i % 2, :].rearrange("q (h e) -> q h e", h=G_HEADS),
                                          AX.X, ALU.add).then_inc(ss_g, 1)
                        dve.wait_ge(rstd_g, i + 1)
                        v = og[:, i, :].rearrange("q (h e) -> q h e", h=G_HEADS)
                        then(dve.tensor_tensor(v, psum[:, SIDE[i], :].rearrange("q (h e) -> q h e", h=G_HEADS),
                                               each(rstd[:, 4 * i:4 * i + 4], G_DV), ALU.mult))
                        dve.tensor_tensor(og[:, i, :], og[:, i, :], sg[:, i, :], ALU.mult).then_inc(bank_free[SIDE[i]], 1)
                elif k == "sa_qk":
                    if st.h == 0:
                        wait_ready(dve, st.ready, turn)
                    for i in range(TT):
                        b, w = SIDE[i], P * (i + 1)
                        dve.wait_ge(bank_done[b], at(st.fill[i], turn, 1))
                        n = min(w, NEAR)
                        then(dve.tensor_tensor(psum[:, b, w - n:w], psum[:, b, w - n:w], near[:, st.h, NEAR - n:NEAR], ALU.add))
                        dve.tensor_reduce(nmax[:, st.h, i:i + 1], psum[:, b, 0:w], AX.X, ALU.max, negate=True).then_inc(smax, 1)
                elif k in ("sa_t", "bt_t"):
                    dst = pt_a[st.h % 2] if k == "sa_t" else pt_b
                    if k == "sa_t" or st.p == 0:
                        dve.wait_ge(bank_done[1], at(st.fill[1], turn, 1))
                        dve.tensor_copy(dst[:, 4 * P:8 * P], psum[:, 1, :]).then_inc(bank_free[1], 1)
                elif k == "sa_pv":
                    then(dve.reciprocal(rden[:, st.h, :], den[:, st.h, :]))
                    dve.wait_ge(bank_done[3], at(st.fill[0], turn, 1))
                    dve.tensor_tensor(o_a[:, :, st.h * A_DIM:st.h * A_DIM + A_DIM],
                                      psum[:, 3, 0:TT * A_DIM].rearrange("q (t d) -> q t d", t=TT),
                                      each(rden[:, st.h, :], A_DIM), ALU.mult).then_inc(bank_free[3], 1)
                elif k == "ca_qk":
                    for n in range(2):
                        dve.wait_ge(bank_done[st.banks[n]], at(st.fill[n], turn, 1))
                    b = st.banks[0]
                    dve.tensor_reduce(nmax[:, st.h, :], psum[:, b:b + 2, :].rearrange("q b (t m) -> q (b t) m", t=2), AX.X, ALU.max,
                                      negate=True).then_inc(smax, 1)
                    for n in range(2):
                        dve.wait_ge(bank_free[st.banks[n]], at(st.fill[n], turn, 1))
                    then(dve.reciprocal(rden[:, st.h, :], den[:, st.h, :]))
                    dve.tensor_tensor(p_x[st.h % 2][:], p_x[st.h % 2][:], each(rden[:, st.h, :], M), ALU.mult).then_inc(px_made, 1)
                elif k == "ca_t":
                    dve.wait_ge(bank_done[1], at(st.fill[1], turn, 1))
                    dve.tensor_copy(pt_x[st.h % 2][:, 1, :], psum[:, 1, :]).then_inc(bank_free[1], 1)
                elif k == "ca_pv":
                    for e in range(2):
                        b, c = st.banks[e], 2 * st.h + e
                        dve.wait_ge(hi_made, at(st.hi, turn, e + 1))
                        dve.tensor_tensor(mid_lo[c // 4][:, c % 4, :], psum[:, b, :], mid_hi[c // 4][:, c % 4, :], ALU.subtract
                                          ).then_inc(bank_free[b], 1)
                elif k == "rope":
                    dve.wait_ge(packed, at(st.packed, turn))
                    if st.p == 0 and st.dst == "q":
                        dve.wait_ge(b2_in, 64)
                    swap = [(n + ROPE_DIM // 2) % ROPE_DIM for n in range(ROPE_DIM)]
                    then(dve.stream_shuffle(turned[:], pack[:], swap))
                    then(dve.tensor_tensor(pack[:], pack[:], cosine[:], ALU.mult))
                    then(dve.tensor_tensor(turned[:], turned[:], sine[:], ALU.mult))
                    for h in range(B_HEADS):
                        rows = slice(ROPE_DIM * h, ROPE_DIM * h + ROPE_DIM)
                        ins = dve.tensor_tensor(per_pattern(qk_b[st.dst][0:ROPE_DIM, h, :], st.p), natural(pack[rows, :], st.p),
                                                natural(turned[rows, :], st.p), ALU.add)
                    ins.then_inc(roped, 1)
                elif k == "bt_qk":
                    if st.p == 0:
                        for i in range(TT):
                            b, w = SIDE[i], P * len([1 for q_, _ in BAND if q_ == i])
                            dve.wait_ge(bank_done[b], at(st.fill[i], turn, 1))
                            m0 = P if i == 0 else 0
                            then(dve.tensor_tensor(psum[:, b, 0:w], psum[:, b, 0:w], band[:, m0:m0 + w], ALU.add))
                            ins = dve.tensor_reduce(mden[:, st.p, i, st.h, 0:1], psum[:, b, 0:w], AX.X, ALU.max, negate=True)
                    else:
                        b = st.banks[0]
                        dve.wait_ge(bank_done[b], at(st.fill[0], turn, 1))
                        v = psum[:, b, :].rearrange("q (t k) -> q t k", t=TT)
                        mask = band[:, P:2 * P] if st.p == 1 else own[:]
                        then(dve.tensor_tensor(v, v, over(mask, TT), ALU.add))
                        ins = dve.tensor_reduce(mden[:, st.p, :, st.h, 0], v, AX.X, ALU.max, negate=True)
                    then(ins)
                    dve.tensor_scalar(nbias[:, st.h, :], mden[:, st.p, :, st.h, 0], B_DIM ** -0.5, None, ALU.mult).then_inc(smax, 1)
                elif k == "joint":
                    dve.wait_ge(nat_in, 16)
                    low, d_ = nat[:, :, :, :, 0], nat[:, :, :, :, 1]
                    then(dve.tensor_tensor(least[:], low[:, 0], low[:, 1], ALU.min))
                    then(dve.tensor_tensor(least[:], least[:], low[:, 2], ALU.min))
                    for p in range(PATTERNS):
                        ins = dve.tensor_tensor(ex[:, p], least[:], low[:, p], ALU.subtract)
                    ins.then_inc(joint_diff, 1)
                    dve.wait_ge(joint_exp, 1)
                    for p in range(PATTERNS):
                        ins = dve.tensor_tensor(zd[:, p], ex[:, p], d_[:, p], ALU.mult)
                    then(ins)
                    then(dve.tensor_tensor(zd[:, 0], zd[:, 0], zd[:, 1], ALU.add))
                    then(dve.tensor_tensor(zd[:, 0], zd[:, 0], zd[:, 2], ALU.add))
                    then(dve.reciprocal(zd[:, 0], zd[:, 0]))
                    for p in range(PATTERNS):
                        ins = dve.tensor_tensor(share[:, p], ex[:, p], zd[:, 0], ALU.mult)
                    ins.then_inc(share_made, 1)
                elif k == "ybsum":
                    for p in range(PATTERNS):
                        dve.wait_ge(wide_in[p], 16)
                        if p == 0:
                            wait_ready(dve, st.ready, turn)
                        then(dve.tensor_tensor(u_b[p][:], u_b[p][:], wide[p][:].rearrange("q t h -> q h t"), ALU.mult))
                    then(dve.tensor_tensor(u_b[0][:], u_b[0][:], u_b[1][:], ALU.add))
                    dve.tensor_tensor(u_b[0][:], u_b[0][:], u_b[2][:], ALU.add).then_inc(yb_sum, 1)
                elif k == "lnv":
                    for tt in range(TT):
                        wait_ready(dve, st.ready[tt:tt + 1], turn)
                        ins = dve.bn_stats(vstat[:, tt, :], vt[:, tt, :])
                    then(ins)
                    for tt in range(TT):
                        ins = dve.bn_aggr(vmean[:, tt, :], vstat[:, tt, :])
                    ins.then_inc(vn_stats, 1)
                    dve.wait_ge(rstd_made, at(st.rstd, turn, 1))
                    dve.wait_ge(row_in, 16 * st.row_n)
                    for tt in range(TT):
                        then(dve.tensor_scalar(vt[:, tt, :], vt[:, tt, :], vmean[:, tt, 0:1], rstd[:, tt:tt + 1], ALU.subtract, ALU.mult))
                        then(dve.tensor_tensor(vt[:, tt, :], vt[:, tt, :], row[:, 0:512], ALU.mult))
                        dve.tensor_tensor(vt[:, tt, :], vt[:, tt, :], row[:, 512:1024], ALU.add).then_inc(vn_made, 1)
                elif k == "spatial":
                    for g in range(4):
                        b = SIDE[g]
                        dve.wait_ge(bank_done[b], at(st.fill[g], turn, 1))
                        v = ya_sum[:, g % 2, :]
                        then(dve.tensor_tensor(v.rearrange("q (c t) -> q c t", c=TT), psum[:, b, :].rearrange("q (c t) -> q c t", c=TT),
                                               over(bs_row[:, g, :], TT), ALU.add))
                        dve.tensor_tensor(v, v, ut[:, g, :], ALU.mult).then_inc(merged, 1)
                        dve.wait_ge(merged, at(st.merged, turn, g + 1))
                        dve.wait_ge(hi_made, at(st.hi, turn, g + 1))
                        dve.tensor_tensor(mid_lo[0][:, g, :], v, mid_hi[0][:, g, :], ALU.subtract).then_inc(bank_free[b], 1)
                elif k == "ybsplit":
                    dve.wait_ge(hi_made, at(st.hi, turn, 1))
                    dve.tensor_tensor(mid_lo[1][:], u_b[0][:], mid_hi[1][:], ALU.subtract).then_inc(yb_split, 1)
                elif k == "clear":
                    wait_ready(dve, st.ready, turn)
                    dve.memset(y[:], 0.0).then_inc(y_clear, 1)
                    dve.wait_ge(y_clear, 1)

            dve.wait_ge(cols_in, 32)
            walk(dve, handle)

        @block.gpsimd
        def _(pool):
            pool.memset(eps[:], EPS).then_inc(pad_made, 1)
            pool.memset(g_hi[:].bitcast(F32), 0.0).then_inc(pad_made, 1)
            pool.memset(g_lo[:].bitcast(F32), 0.0).then_inc(pad_made, 1)
            pool.dma_start(g_raw[:], a["w_glr"]).then_inc(glr_in, 16)
            pool.dma_start(w_gu[:], a["w_gate_up"]).then_inc(const_in, 16)
            pool.dma_start(lvl_mask[:], a["lvl_mask"]).then_inc(const_in, 16)

            def load_row(parts):
                for name, c0, n in parts:
                    pool.dma_start(row[:, c0:c0 + n], a[name].partition_broadcast(P)).then_inc(row_in, 16)

            pool.dma_start(table[0:RP_BUCKETS, :], a["table"]).then_inc(table_in, 16)
            pool.dma_start(bucket[0:RP_BUCKETS, :], a["bucket"]).then_inc(table_in, 16)
            load_row([("norm_final", 0, D)])

            def handle(st, turn):
                k = st.kind
                if k == "gate":
                    pool.wait_ge(cum_made, 2)
                    for n in range(2):
                        level(n, st)
                elif k == "relbias":
                    pool.wait_ge(bias_made, 1)
                    pool.wait_ge(bank_free[4], at(st.fill[0], turn, 1))
                    pool.dma_start(bias_dram, bias_row[0:A_HEADS, :]).then_inc(bias_out, 16)
                    pool.wait_ge(bias_out, 16)
                    pool.wait_ge(xn_made, MT + TT)
                    toeplitz = bass.AP(tensor=bias_dram.tensor, offset=0, ap=[[1, P], [REL, A_HEADS], [1, NEAR]])
                    pool.dma_start(near_back[:], toeplitz).then_inc(near_in, 16)
                elif k == "level":
                    if st.n == 0:
                        wait_ready(pool, st.ready, turn)
                        pool.memset(a_own[:], 0.0).then_inc(own_clear, 1)
                    if st.n + 2 < len(LEVELS):
                        level(st.n + 2, st)
                elif k == "glaout":
                    wait_ready(pool, [(b, st.fill[n], 1) for n, b in enumerate(SIDE)], turn)
                    pool.dma_start(x[:], a["x"].rearrange("(t p) d -> p t d", p=P)).then_inc(x_back, 16)
                elif k == "load2":
                    wait_ready(pool, st.ready, turn)
                    pool.dma_start(cosine[:], a["cosine"]).then_inc(b2_in, 16)
                    pool.dma_start(sine[:], a["sine"]).then_inc(b2_in, 16)
                    pool.dma_start(band[:], a["band"]).then_inc(b2_in, 16)
                    pool.dma_start(own[:], a["own"]).then_inc(b2_in, 16)
                    pool.dma_start(ws_t[:], a["w_spatial_t"]).then_inc(ws_in, 16)
                    pool.dma_start(bs_row[:].rearrange("q g t -> q (g t)"), a["b_spatial_2"].partition_broadcast(P)).then_inc(ws_in, 16)
                elif k == "rows":
                    pool.wait_ge(x_rows, at(st.xrows, turn, TT))
                    if st.row == "norm_final":
                        load_row([("ln_v_gain_2", 0, 512), ("ln_v_bias_2", 512, 512)])
                    elif st.row == "norm_mix_post_2":
                        load_row([("norm_mlp_post_2", 0, D)])
                elif k == "spatial":
                    pool.wait_ge(vn_made, TT)
                    load_row([("norm_mix_post_2", 0, D)])
                elif k == "stats":
                    wait_ready(pool, st.ready, turn)
                    src, dst = mden[:, st.p].rearrange("q t h s -> q t (h s)"), stat_dram[st.p]
                    if st.p == 0:
                        pool.dma_start(dst.rearrange("(t q) v -> q t v", t=TT), src).then_inc(stat_out, 16)
                    else:
                        pool.dma_start(dst.rearrange("(m r) v -> m r v", r=4), src).then_inc(stat_out, 16)
                elif k == "joint":
                    pool.wait_ge(stat_out, 16 * PATTERNS)
                    pool.dma_start(nat[:].rearrange("q p t h s -> q p (t h s)"), stat_dram.rearrange("p (q t) v -> q p (t v)", t=TT)).then_inc(nat_in, 16)
                    pool.wait_ge(share_made, 1)
                    pool.dma_start(share_dram.rearrange("p (q v) -> q p v", q=P), share[:].rearrange("q p t h -> q p (t h)")).then_inc(share_out, 16)
                    pool.wait_ge(share_out, 16)
                    wait_ready(pool, st.ready, turn)
                    for p in range(PATTERNS):
                        pool.dma_start(wide[p][:].rearrange("q t h -> q (t h)"), share_dram[p].partition_broadcast(P)).then_inc(wide_in[p], 16)

            def level(n, st):
                size = LEVELS[n]
                view = lambda ap: ap.rearrange("q c (b s l) -> q (c b) s l", s=2, l=size)
                c_, e_, l_ = view(cum[:]), view(ex_g[:]), view(lev[n % 2][:])
                q_, k_ = view(qk_g[:, 0:2, :]), view(qk_g[:, 2:4, :])
                ref = c_[:, :, 0, size - 1:size].broadcast_to([P, 2 * T // (2 * size), size])
                wait(pool, lev_made, n)
                if n == 0:
                    wait_ready(pool, st.qk_ready, None)
                pool.tensor_tensor(e_[:, :, 0, :], ref, c_[:, :, 0, :], ALU.subtract).then_inc(lev_diff, 1)
                pool.tensor_tensor(e_[:, :, 1, :], c_[:, :, 1, :], ref, ALU.subtract).then_inc(lev_diff, 1)
                if n >= 2:
                    for tt in range(TT):
                        pool.wait_ge(bank_done[SIDE[tt]], at(s.levels[n - 2].fill[tt], None, 1))
                pool.wait_ge(lev_exp, n + 1)
                half = pool.tensor_tensor(l_[:, :, 0, :], k_[:, :, 0, :], e_[:, :, 0, :], ALU.mult)
                half.then_inc(pool_step, 1)
                pool.tensor_tensor(l_[:, :, 1, :], q_[:, :, 1, :], e_[:, :, 1, :], ALU.mult).then_inc(lev_made, 1)

            for item in s.items:
                if not isinstance(item, tuple):
                    handle(item, None)



def rel_bucket(d):
    exact = RP_BUCKETS // 2
    large = exact + (np.log(np.maximum(d, 1).astype(np.float32) / np.float32(exact))
                     / np.float32(math.log(RP_MAX_DIST / exact)) * np.float32(RP_BUCKETS - exact)).astype(np.int32)
    return np.where(d < exact, np.maximum(d, 0), np.minimum(large, RP_BUCKETS - 1))


def shape_constants():
    u = np.arange(REL)
    d = NEAR - 1 - u
    bucket = np.zeros((RP_BUCKETS, REL), np.float32)
    bucket[rel_bucket(d[d >= 0]), u[d >= 0]] += 1.0
    bucket[RP_BUCKETS - 1, u[d >= 0]] -= 1.0
    j, i = np.arange(P)[:, None], np.arange(P)[None, :]
    lvl = [(j // (2 * n) == i // (2 * n)) & (j % (2 * n) < n) & (i % (2 * n) >= n) for n in LEVELS] + [j == i]
    half = ROPE_DIM // 2
    inv = ROPE_THETA ** (-np.arange(0, ROPE_DIM, 2, dtype=np.float32) / np.float32(ROPE_DIM))
    ang = np.arange(T, dtype=np.float32)[None, :] * inv.astype(np.float32)[:, None]
    cos, sin = np.cos(ang), np.sin(ang)
    q, k = np.arange(P)[:, None], np.arange(3 * P)[None, :] - P
    return {
        "ident": np.eye(P, dtype=np.float32),
        "mirror": np.eye(P, dtype=np.float32)[::-1],
        "bucket": bucket,
        "lvl_mask": np.stack(lvl, 1).astype(np.int32),
        "cosine": np.tile(np.concatenate([cos, cos]), (B_HEADS, 1)).astype(np.float32),
        "sine": np.tile(np.concatenate([-sin, sin]), (B_HEADS, 1)).astype(np.float32),
        "band": np.where(np.abs(q - k) <= RADIUS, 0.0, MASKED).astype(np.float32),
        "own": np.where(j % 4 == i % 4, 0.0, MASKED).astype(np.float32),
    }


def lay_out(inputs):
    a = dict(shape_constants())
    a["x"] = np.ascontiguousarray(inputs["x"][0])
    a["mem"] = np.ascontiguousarray(inputs["mem"][0])
    tiles = []
    for name, r0, rows, c0, n in GROUPS:
        w = inputs[name][0][r0:r0 + rows, c0:c0 + n]
        if n == 512:
            w = w.reshape(4, 2, P, 512).transpose(0, 2, 1, 3)
        else:
            w = w.reshape(2, 2, P, 2, 512).transpose(3, 0, 2, 1, 4)
        tiles.append(w.reshape(4, P, WORDS))
    a["weights"] = np.concatenate(tiles)
    a["cols"] = np.concatenate([inputs[n].reshape(-1, P) for n in COLS]).T.copy()
    a["w_glr"] = inputs["w_in"][0][:, W_IN["glr"]:W_IN["glr"] + G_RANK].reshape(KC, P, G_RANK).transpose(1, 0, 2).copy()
    a["w_gate_up"] = inputs["w_gate_up"][0]
    a["table"] = inputs["rp_table"]
    a["w_spatial_t"] = inputs["w_spatial_2"][0].transpose(2, 0, 1).copy()
    a["b_spatial_2"] = inputs["b_spatial_2"].reshape(-1)
    for n in ("norm_final", "ln_v_gain_2", "ln_v_bias_2", "norm_mix_post_2", "norm_mlp_post_2"):
        a[n] = inputs[n].reshape(-1)
    return {n: np.ascontiguousarray(v) for n, v in a.items()}


def kernel(**inputs):
    import concourse.bacc as bacc
    from concourse.bass_utils import run_bass_kernel_spmd

    nc = bacc.Bacc("TRN2", target_bir_lowering=False, num_devices=1)
    arrays = lay_out({n: np.asarray(v) for n, v in inputs.items()})
    aps = {n: nc.dram_tensor(f"in_{n}", v.shape, mybir.dt.from_np(v.dtype), kind="ExternalInput").ap()
           for n, v in arrays.items()}
    out = nc.dram_tensor("out", (T, D), F32, kind="ExternalOutput").ap()
    two_blocks(nc, aps, out)
    r = run_bass_kernel_spmd(nc, [{f"in_{n}": v for n, v in arrays.items()}], core_ids=[0])
    return r.results[0]["out"].reshape(1, T, D)
```

```python
import math
from contextlib import ExitStack
from itertools import chain

import numpy as np

import concourse.bass as bass
from concourse import mybir

F32 = mybir.dt.float32
F32R = mybir.dt.float32r
I32 = mybir.dt.int32
ACT = mybir.ActivationFunctionType
ALU = mybir.AluOpType
AX = mybir.AxisListType

P = 128
T = 512
TT = T // P
D = 1024
KC = D // P
M = 256
MT = M // P
A_HEADS, A_DIM = 8, 64
G_HEADS, G_DK, G_DV, G_RANK = 4, 64, 128, 16
G_NORM = 16.0
X_HEADS, X_DIM = 4, 256
FF = 4096
CHUNKS = FF // T
B_HEADS, B_DIM = 4, 128
PATTERNS = 3
RADIUS = 64
DILATION = (1, 4, 16)
ROPE_DIM = 32
ROPE_THETA = 500000.0
EPS = 1e-6
MASKED = -1e30
RP_BUCKETS, RP_MAX_DIST = 32, 128
LEVELS = (64, 32, 16, 8, 4, 2, 1)
WORDS = 1024
NEAR = 2 * P
REL = 3 * P

COLS = {}
_at = 0
for _name, _n in (("norm_mix", KC), ("norm_xattn", KC), ("norm_mem", KC), ("norm_mlp", KC),
                  ("norm_mix_pre_2", KC), ("norm_mlp_pre_2", KC), ("b_gate_2", 2 * KC), ("g_norm", 1),
                  ("b_gate", 2)):
    COLS[_name] = _at
    _at += _n
NCOLS = _at



W_IN = dict(qa=0, ka=512, va=1024, glaqk=1536, vg=2048, glr=2560, rg=2576)


def mlp_order():
    return ([("up", 0)] + [x for c in range(0, CHUNKS - 2, 2)
                           for x in (("up", c + 1), ("down", c), ("up", c + 2), ("down", c + 1))]
            + [("up", CHUNKS - 1), ("down", CHUNKS - 2), ("down", CHUNKS - 1)])


def stream_groups():
    out = [("w_in", 0, D, W_IN[n], 512) for n in ("glaqk", "vg", "rg", "qa", "ka", "va")]
    out += [("w_xkv", 0, D, 512 * n, 512) for n in range(4)]
    out += [("w_out", 0, D, 512 * n, 512) for n in range(2)]
    out += [("w_xq", 0, D, 512 * n, 512) for n in range(2)]
    out += [("w_xo", 0, D, 512 * n, 512) for n in range(2)]
    mlp = lambda up, down: [(up, 0, D, 512 * c, 512) if kind == "up" else (down, 512 * c, 512, 0, D)
                            for kind, c in mlp_order()]
    out += mlp("w_up", "w_down")
    width = B_HEADS * B_DIM
    for p in range(PATTERNS):
        out += [("w_in_2", 0, D, 1024 + (PATTERNS * n + p) * width, 512) for n in range(3)]
    out += [("w_in_2", 0, D, 512 * n, 512) for n in (1, 0)]
    out += [("w_in_2", 0, D, 1024 + 3 * PATTERNS * width + 512 * n, 512) for n in range(4)]
    out += [("w_branch_a_2", 0, 512, 0, D), ("w_branch_b_2", 0, 512, 0, D)]
    out += [("w_out_2", 0, D, 512 * n, 512) for n in range(2)]
    out += mlp("w_up_2", "w_down_2")
    return out


GROUPS = stream_groups()
TILES = 4 * len(GROUPS)
RAW = 2



class Step:

    def __init__(self, kind, banks, fill, *, n=0, h=0, p=None, out=None, major=None, src=None, dst=None, rows=KC,
                 half=0, first=False, splits=(), tile=None, slots_free=None, ready=None, bank=0, blk=0, mid=None,
                 after=None, tiles=TT, gains=(), chunks=(), after_rows=None, row=None, row_n=0, qk_ready=None,
                 roped=None, packed=None, rstd=None, xn=None, hi=None, xrows=None, smax=None, merged=None, relu=None):
        self.kind, self.banks, self.fill = kind, banks, fill
        self.n, self.h, self.p = n, h, p
        self.out, self.major, self.src, self.dst = out, major, src, dst
        self.rows, self.half, self.bank, self.blk, self.mid = rows, half, bank, blk, mid
        self.first, self.splits, self.tile, self.slots_free = first, splits, tile, slots_free
        self.ready, self.qk_ready, self.after, self.after_rows = ready, qk_ready, after, after_rows
        self.tiles, self.gains, self.chunks, self.row, self.row_n = tiles, gains, chunks, row, row_n
        self.roped, self.packed, self.rstd, self.xn, self.hi, self.xrows, self.smax, self.merged, self.relu = (
            roped, packed, rstd, xn, hi, xrows, smax, merged, relu)


class Schedule:

    def __init__(self):
        self.items, self.body, self.open = [], None, []
        self.fills, self.counts = [0] * 8, {}
        self.group = 0
        self.last_bank = None

    def fill(self, bank):
        c = [self.fills[bank], 0]
        self.fills[bank] += 1
        if self.body is not None:
            self.open.append((c, ("bank", bank)))
        return c

    def fills_of(self, bank):
        c = [self.fills[bank], 0]
        if self.body is not None:
            self.open.append((c, ("bank", bank)))
        return c

    def count(self, name, n):
        c = [self.counts.get(name, 0), 0]
        self.counts[name] = c[0] + n
        if self.body is not None:
            self.open.append((c, ("count", name)))
        return c

    def add(self, kind, banks=(), counts=(), **more):
        fields = dict(more)
        for name, n in dict(counts).items():
            fields[name] = self.count(name, n)
        st = Step(kind, list(banks), [self.fill(b) for b in banks], **fields)
        (self.items if self.body is None else self.body).append(st)
        return st

    def begin_loop(self, turns):
        self.turns, self.body, self.open = turns, [], []
        self.before = (list(self.fills), dict(self.counts), self.group)

    def end_loop(self):
        fills, counts, group = self.before
        growth = {("bank", b): self.fills[b] - fills[b] for b in range(8)}
        growth |= {("count", n): v - counts.get(n, 0) for n, v in self.counts.items()}
        growth["tile"] = 4 * (self.group - group)
        for c, key in self.open:
            c[1] = growth[key]
        more = self.turns - 1
        for b in range(8):
            self.fills[b] += more * growth["bank", b]
        for n in self.counts:
            self.counts[n] += more * growth["count", n]
        self.group += more * (self.group - group)
        self.items.append((self.turns, self.body))
        self.body, self.open = None, []

    def gemm(self, *args, **more):
        for _ in self.bank_steps(*args, **more):
            pass

    def bank_steps(self, out, major, src, rows=KC, banks=4, halves=1, ready=None, blk=0, mid=None, dst=None, p=None,
             after=None):
        g = self.group
        self.group += 1
        steps = halves * banks
        free_bank = self.last_bank
        slots_free = None if g == 0 else (free_bank, self.fills_of(free_bank))
        for i in range(steps):
            half, b = divmod(i, banks)
            splits = [4 * (g + 1) + j for j in range(4) if j * steps // 4 == i and g + 1 < len(GROUPS)]
            tiles = []
            for t in splits + [4 * g]:
                c = [t, 0]
                if self.body is not None:
                    self.open.append((c, "tile"))
                tiles.append(c)
            counts = {"up": {"hi": 1, "relu": 1}, "merge": {"hi": 1, "merged": 1}, "rope": {"packed": 1}}.get(out, {})
            st = self.add("gemm", [b], counts, out=out, major=major, src=src, rows=rows, half=half,
                          first=(b == 0), splits=tiles[:-1], tile=tiles[-1], slots_free=slots_free,
                          ready=ready if i == 0 else None, bank=b, blk=blk, mid=mid, dst=dst, p=p, after=after)
            if i == steps - 1:
                self.last_bank = banks - 1
            yield st


def at(count, turn, plus=0):
    value, growth = count
    if turn is None or growth == 0:
        return value + plus
    assert value + plus > 0
    return turn * growth + (value + plus)


SIDE = (4, 5, 6, 7)
CAUSAL = [(i, k) for i in range(TT) for k in range(i + 1)]
BAND = [(i, k) for i in range(TT) for k in range(max(0, i - 1), min(TT, i + 2))]
OWN = [(i, i) for i in range(TT)]
ROW_PLACES = [(3, 0, 0, True), (2, 1, 0, False), (0, 1, 3 * P, True), (1, 2, 0, True)]
BAND_PLACES = [(1, 0, 0, True), (2, 1, 0, True), (0, 2, 0, False), (3, 2, 2 * P, True)]
PAIRS = [(j, i) for i in range(TT) for j in range(i)]


def make_schedule():
    s = Schedule()
    s.rows_done = None

    def norm(src, tiles, gain, dst, src_ready):
        ready = [(b, s.fills_of(b), 0) for b in range(TT)] if src_ready == "evac" else src_ready
        st = s.add("scale", counts={"rstd": tiles, "xn": tiles}, src=src, tiles=tiles, ready=ready, after_rows=s.rows_done)
        return transposed(tiles, [gain] * KC, dst, st.xn)

    def transposed(tiles, gains, dst, src):
        chunks = [4, 5, 6, 7, 0, 1, 2, 3] if src == "mix" else list(range(KC))
        st = s.add("turn", SIDE + SIDE, {"hi": KC}, tiles=tiles, gains=gains, dst=dst, src=src, chunks=chunks,
                   ready=all_out() if src == "mix" else None)
        return [(SIDE[c % 4], st.fill[chunks.index(c)], 1) for c in range(KC)]

    def ready():
        return [(b, s.fills_of(b), 0) for b in range(4)]

    def all_out():
        return [(b, s.fills_of(b), 0) for b in range(8)]

    def filled_by(st):
        return [(b, f, 1) for b, f in zip(st.banks, st.fill)]

    def run_mlp(dst, act_ready):
        def up(act_ready, c):
            s.gemm("up", "T", "act", ready=act_ready, mid=c % 2)

        def down(mid_ready, c):
            s.gemm("add", "tok", "mid", rows=4, halves=2, ready=mid_ready, mid=c % 2, dst=dst)

        up(act_ready, 0)
        s.begin_loop((CHUNKS - 2) // 2)
        even = ready()
        up(None, 1)
        odd = ready()
        down(even, 0)
        up(None, 2)
        down(odd, 1)
        s.end_loop()
        even = ready()
        up(None, 1)
        odd = ready()
        down(even, 0)
        down(odd, 1)

    def rows(name, src, row_n):
        st = s.add("rows", counts={"rstd": TT, "xrows": TT}, ready=ready(), row=name, src=src, row_n=row_n)
        s.rows_done = st.xrows

    def go(steps, n):
        for _ in range(n):
            next(steps, None)

    s.add("start")
    s.add("relbias", (4,))
    act_ready = norm("x", TT, "norm_mix", "act", "x")
    s.gemm("glaqk", "T", "act", ready=act_ready)
    near_ready = filled_by(s.add("flip", SIDE))
    qk_ready = ready()
    s.glr = s.add("glr", (4,))
    s.add("gate", (5, 6), qk_ready=qk_ready)
    s.gemm("vg", "tok", "act")
    steps = chain(s.bank_steps("rg", "tok", "act"), s.bank_steps("qa", "T", "act"), s.bank_steps("ka", "T", "act"),
                  s.bank_steps("va", "tok", "act"))
    last = len(LEVELS)
    s.levels = {last: s.add("level", SIDE, n=last, qk_ready=qk_ready)}
    for n in range(last):
        go(steps, 1 if n == 0 else 2)
        s.levels[n] = s.add("level", SIDE, n=n, qk_ready=qk_ready)
        if n == 0:
            s.add("farprep")
    go(steps, 1)
    s.add("far", [SIDE[n % 4] for n in range(len(PAIRS))])
    go(steps, 1)
    s.add("glaout", SIDE)
    go(steps, 16)
    act_free = ready()
    qk = [s.add("sa_qk", (4, 5, 6), {"smax": 4}, h=0, ready=near_ready + act_free),
          s.add("sa_qk", (0, 1, 2), {"smax": 4}, h=1)]
    t = [s.add("sa_t", qk[h].banks, h=h, ready=filled_by(qk[h])) for h in range(2)]
    for h in range(2):
        s.add("sa_pv", ((7, 3)[h],), h=h, ready=filled_by(t[h]))
    mem_ready = norm("mem", MT, "norm_mem", "memT", "mem")
    steps = chain(s.bank_steps("kx", "T", "memT", ready=mem_ready, blk=0), s.bank_steps("kx", "T", "memT", blk=1),
                  s.bank_steps("vx", "tok", "memT", banks=2, blk=0), s.bank_steps("vx", "tok", "memT", banks=2, blk=1))
    for h in range(2, A_HEADS):
        qk = s.add("sa_qk", (4, 5, 6), {"smax": 4}, h=h)
        go(steps, 1)
        t = s.add("sa_t", (4, 5, 6), h=h, ready=filled_by(qk))
        go(steps, 1)
        s.add("sa_pv", (7,), h=h, ready=filled_by(t))
    go(steps, 16)
    s.add("reload", ready=ready())
    mix_ready = transposed(TT, [None] * 4 + ["g_norm"] * 4, "mid", "mix")
    s.gemm("add", "tok", "mid", ready=mix_ready, dst="x", blk=0, after="x_back")
    s.gemm("add", "tok", "mid", dst="x", blk=1)
    act_ready = norm("x", TT, "norm_xattn", "act", "evac")
    s.gemm("qx", "T", "act", ready=act_ready, blk=0)
    s.gemm("qx", "T", "act", blk=1)
    s.add("ca_qk", (4, 5), {"smax": 1}, h=0, ready=ready())
    for h in range(X_HEADS):
        if h + 1 < X_HEADS:
            s.add("ca_qk", (6, 7) if h % 2 == 0 else (4, 5), {"smax": 1}, h=h + 1, ready=[])
        t = s.add("ca_t", (0, 1), h=h)
        s.add("ca_pv", (2, 3), {"hi": 2}, h=h, ready=filled_by(t))
    ox_ready = [(2 + c % 2, [s.fills[2 + c % 2] - (X_HEADS - 1 - c // 2), 0], 0) for c in range(KC)]
    s.add("load2", ready=all_out())
    s.gemm("add", "tok", "mid", ready=ox_ready, dst="x", blk=0)
    s.gemm("add", "tok", "mid", dst="x", blk=1)
    act_ready = norm("x", TT, "norm_mlp", "act", "evac")
    run_mlp("x", act_ready)
    rows("norm_final", "x", 1)
    act_ready = norm("x", TT, "norm_mix_pre_2", "act", "rows")
    roped = [None]

    def project(p, ready=None):
        for dst in ("q", "k"):
            yield from s.bank_steps("rope", "T", "act", ready=ready if dst == "q" else None, dst=dst, p=p, after=roped[0])
            roped[0] = s.add("rope", counts={"roped": 1, "packed": 0}, dst=dst, p=p).roped

    go(project(0, act_ready), 16)
    for p in range(PATTERNS):
        s.gemm("v2", "tok", "act", p=p)
        v_ready, mine = ready(), roped[0]
        qk_banks = lambda h: (4, 5, 6) if p == 0 else (4 + h % 2,)
        t_banks = (4, 5, 6) if p == 0 else (6,)
        steps = project(p + 1) if p + 1 < PATTERNS else s.bank_steps("v", "tok", "act")
        qk = s.add("bt_qk", qk_banks(0), {"smax": 1}, h=0, p=p, roped=mine)
        for h in range(B_HEADS):
            go(steps, 1)
            t = s.add("bt_t", t_banks, h=h, p=p, ready=filled_by(qk))
            early = p > 0 and h + 1 < B_HEADS
            if early:
                qk = s.add("bt_qk", qk_banks(h + 1), {"smax": 1}, h=h + 1, p=p, roped=mine)
            if p + 1 < PATTERNS:
                go(steps, 1)
            s.add("bt_pv", (7,), h=h, p=p, ready=filled_by(t) + (v_ready if h == 0 else []))
            if not early and h + 1 < B_HEADS:
                qk = s.add("bt_qk", qk_banks(h + 1), {"smax": 1}, h=h + 1, p=p, roped=mine)
        go(steps, 16)
        s.add("stats", p=p, ready=all_out())
    attended, v_done = all_out(), ready()
    steps = s.bank_steps("u", "T", "act")
    go(steps, 1)
    s.add("joint", ready=attended)
    s.add("lnv", counts={"rstd": 1}, ready=v_done, row_n=3)
    go(steps, 16)
    s.add("ybsum", ready=attended)
    ya = s.add("spatial", SIDE, {"hi": 4, "merged": 4})
    s.add("ybsplit", counts={"hi": 1}, ready=all_out())
    for n in range(4):
        s.gemm("gate", "T", "act", blk=n)
    s.gemm("bra", "T", "mid", rows=4, halves=2, mid=0, ready=filled_by(ya))
    s.gemm("merge", "T", "mid", rows=4, halves=2, mid=1, after="yb")
    merged_ready = ready() * 2
    s.gemm("copy", "tok", "act", ready=merged_ready, dst="y", blk=0)
    s.gemm("copy", "tok", "act", dst="y", blk=1)
    rows("norm_mix_post_2", "y", 4)
    act_ready = norm("x", TT, "norm_mlp_pre_2", "act", "rows")
    s.add("clear", ready=all_out())
    run_mlp("y", act_ready)
    rows("norm_mlp_post_2", "y", 5)
    s.add("store")
    return s



def two_blocks(nc, a, out):
    s = make_schedule()
    with ExitStack() as ctx:
        def sem(name):
            return ctx.enter_context(nc.semaphore(name))

        slab_bytes = 212800
        base = -(-nc.sbuf_base // 64) * 64
        ctx.enter_context(nc.sbuf_tensor("slab", [P, slab_bytes], mybir.dt.uint8, align_bytes=64))
        top = [0]
        KB = 1024
        region = {}
        for name, size in (("x", 16 * KB), ("raw", 8 * KB), ("whi", 32 * KB), ("wlo", 32 * KB), ("act", 32 * KB),
                           ("mid", 32 * KB), ("y", 16 * KB), ("v", 8 * KB), ("u", 8 * KB), ("const", 23 * KB)):
            region[name] = top[0]
            top[0] += size
        assert top[0] <= slab_bytes, top[0]

        def place(name, where, shape, dtype=F32, skip=0):
            return nc.alloc_sbuf_tensor_at(name, [P] + shape, dtype, offset=base + region[where] + skip)

        x = place("x_tok", "x", [TT, D])
        w_raw = place("w_raw", "raw", [RAW, WORDS])
        w_hi = place("w_hi", "whi", [8, WORDS], F32R)
        w_lo = place("w_lo", "wlo", [8, WORDS], F32R)
        act_hi = place("act_hi", "act", [KC, T], F32R)
        act_lo = place("act_lo", "act", [KC, T], F32R, 16 * KB)
        mid_hi = [place(f"mid_hi{n}", "mid", [4, T], F32R, 16 * KB * n) for n in range(2)]
        mid_lo = [place(f"mid_lo{n}", "mid", [4, T], F32R, 16 * KB * n + 8 * KB) for n in range(2)]
        y = place("y_tok", "y", [TT, D])

        cat = [0]

        def const(name, shape, dtype=F32, rows=P):
            n = int(np.prod(shape)) * 4
            t = nc.alloc_sbuf_tensor_at(name, [rows] + shape, dtype, offset=base + region["const"] + cat[0])
            cat[0] += -(-n // 32) * 32
            assert cat[0] <= 23 * KB, (name, cat[0])
            return t

        ident = const("ident", [P])
        cols = const("cols", [NCOLS])
        row = const("row", [D])
        eps = const("eps", [1])
        sumsq = const("sumsq", [16])
        lnv = const("lnv", [16])
        rstd = const("rstd", [16])
        phase = cat[0]
        lvl_mask = const("lvl_mask", [len(LEVELS) + 1, P], I32)
        w_gu = const("w_gu", [G_HEADS * G_DK], rows=G_RANK)
        glr_t = const("glr_t", [T], rows=G_RANK)
        near = const("near", [A_HEADS, NEAR])
        bucket = place("bucket", "const", [REL], skip=cat[0] - 8 * KB)
        table = place("table", "const", [A_HEADS], skip=cat[0] - 4 * KB)
        bias_row = place("bias_row", "const", [REL], skip=cat[0] - 10 * KB)
        mirror = const("mirror", [P])
        nmax = const("nmax", [A_HEADS, TT])
        den = const("den", [A_HEADS, TT])
        rden = const("rden", [A_HEADS, TT])
        decay = const("decay", [2, TT])
        cat[0] = phase
        cosine = const("cosine", [T])
        sine = const("sine", [T])
        band = const("band", [3 * P])
        own = const("own", [P])
        pack = const("pack", [T])
        ya_sum = place("ya_sum", "const", [2, T], skip=cat[0] - 2 * KB)
        turned = const("turned", [T])
        mden = const("mden", [PATTERNS, TT, B_HEADS, 2])
        nbias = const("nbias", [B_HEADS, TT])
        nat = const("nat", [PATTERNS, TT, B_HEADS, 2])
        least = const("least", [TT, B_HEADS])
        ex = const("ex", [PATTERNS, TT, B_HEADS])
        zd = const("zd", [PATTERNS, TT, B_HEADS])
        share = const("share", [PATTERNS, TT, B_HEADS])
        vstat = const("vstat", [TT, 6])
        vmean = const("vmean", [TT, 2])
        ws_t = place("ws_t", "const", [4, P], skip=cat[0])
        bs_row = place("bs_row", "const", [4, P], skip=cat[0] + 2 * KB)
        assert cat[0] + 4 * KB <= 23 * KB

        mem = place("mem_tok", "v", [MT, D])
        memn = place("mem_n", "u", [MT, D])
        mem_hi = place("mem_hi", "x", [KC, M], F32R)
        mem_lo = place("mem_lo", "x", [KC, M], F32R, 8 * KB)
        kx = place("kx", "v", [KC, M])
        vx = place("vx", "u", [MT, D])
        qk_g = place("qk_g", "mid", [4, T])
        vg = place("vg", "mid", [TT, 4 * P], skip=8 * KB)
        sg = place("sg", "mid", [TT, 4 * P], skip=16 * KB)
        va = place("va", "mid", [TT, 4 * P], skip=24 * KB)
        g_hi = place("g_hi", "mid", [KC, P], F32R, 16 * KB)
        g_lo = place("g_lo", "mid", [KC, P], F32R, 20 * KB)
        g_raw = place("g_raw", "mid", [KC, G_RANK], skip=24 * KB)
        og = place("og", "mid", [TT, 4 * P])
        qa = place("qa", "y", [4, T])
        ka = place("ka", "y", [4, T], skip=8 * KB)
        cum = place("cum", "x", [2, T])
        ex_g = place("ex_g", "x", [2, T], skip=4 * KB)
        lev = [place(f"lev{n}", "x", [2, T], skip=(8 + 4 * n) * KB) for n in range(2)]
        near_back = place("near_back", "x", [A_HEADS, NEAR])
        a_own = place("a_own", "v", [2, TT, 2, P])
        a_far = place("a_far", "x", [2, len(PAIRS), 2, P], skip=4 * KB)
        q_far = place("q_far", "u", [2, T])
        k_far = place("k_far", "u", [2, T], skip=4 * KB)
        q_mid = place("q_mid", "x", [2, 3, P])
        square_g = nc.alloc_sbuf_tensor_at("square_g", [P, 2, T], F32, offset=base + region["const"] + phase)
        n_causal = len(CAUSAL) * P
        p_a = [place(f"p_a{n}", "act", [n_causal], skip=n * 4 * n_causal) for n in range(2)]
        pt_a = [place(f"pt_a{n}", "act", [n_causal], skip=(2 + n) * 4 * n_causal) for n in range(2)]
        o_a = place("o_a", "act", [TT, 4 * P], skip=24 * KB)
        qx = place("qx", "y", [KC, T])
        p_x = [place(f"p_x{n}", "act", [TT, M], skip=n * 4 * KB) for n in range(2)]
        pt_x = [place(f"pt_x{n}", "act", [MT, T], skip=(8 + 4 * n) * KB) for n in range(2)]
        relu = [place(f"relu{n}", "v", [T], skip=2 * n * KB) for n in range(2)]
        square = [place(f"square{n}", "v", [T], skip=(4 + 2 * n) * KB) for n in range(2)]
        slot = lambda name, n, shape, skip=0: place(name, *(("y", shape, F32, 8 * KB * n + skip) if n < 2 else
                                                           ("uv"[n - 2], shape, F32, skip) if n < 4 else
                                                           ("mid", shape, F32, 8 * KB * (n - 4) + skip)))
        qk_b = {"q": [slot(f"q_b{p}", (6, 1, 6)[p], [B_HEADS, T]) for p in range(PATTERNS)],
                "k": [slot(f"k_b{p}", (7, 2, 7)[p], [B_HEADS, T]) for p in range(PATTERNS)]}
        n_band, n_own = len(BAND) * P, len(OWN) * P
        p_band = [slot(f"p_band{n}", 4, [n_band], n * 4 * n_band) for n in range(2)]
        p_own = [slot(f"p_own{n}", 4, [n_own], n * 4 * n_own) for n in range(2)]
        p_b = lambda st: (p_band if st.p == 0 else p_own)[st.h % 2]
        pt_band, pt_own = slot("pt_band", 4, [n_band], 8 * n_band), slot("pt_own", 4, [n_own], 8 * n_own)
        pt_b = lambda st: pt_band if st.p == 0 else pt_own
        v_b = slot("v_b", 3, [TT, 4 * P])
        u_b = [slot(f"u_b{p}", (0, 5, 1)[p], [B_HEADS, T]) for p in range(PATTERNS)]
        wide = [slot(f"wide{p}", (3, 4, 7)[p], [T, B_HEADS]) for p in range(PATTERNS)]
        ut = slot("ut", 6, [4, T])
        vt = slot("vt", 2, [TT, 4 * P])
        gate = [place(f"gate{n}", *(("y", [4, T], F32, 8 * KB * n) if n < 2 else (("v", "u")[n - 2], [4, T]))) for n in range(4)]
        junk = {"x": y, "mem": memn, "y1": place("junk_mid", "mid", [TT, D]), "y2": place("junk_act", "act", [TT, D])}

        psum = ctx.enter_context(nc.psum_tensor("banks", [P, 8, 512], F32))
        bias_dram = nc.dram_tensor("bias_dram", [A_HEADS, REL], F32).ap()
        stat_dram = nc.dram_tensor("stat_dram", [PATTERNS, T, B_HEADS * 2], F32).ap()
        share_dram = nc.dram_tensor("share_dram", [PATTERNS, T * B_HEADS], F32).ap()

        bank_done = [sem(f"bank_done{b}") for b in range(8)]
        bank_free = [sem(f"bank_free{b}") for b in range(8)]
        raw_in = [sem(f"raw_in{n}") for n in range(RAW)]
        hi_w = sem("hi_w")
        lo_w = sem("lo_w")
        hi_made = sem("hi_made")
        relu_made = sem("relu_made")
        square_made = sem("square_made")
        rstd_made = sem("rstd_made")
        xn_made = sem("xn_made")
        x_rows = sem("x_rows")
        x_in = [sem(f"x_in{tt}") for tt in range(TT)]
        mem_in, cols_in, const_in, glr_in, table_in = (sem(n) for n in ("mem_in", "cols_in", "const_in", "glr_in", "table_in"))
        glr_hi, glr_lo, gate_abs, gate_log, cum_made = (sem(n) for n in ("glr_hi", "glr_lo", "gate_abs", "gate_log", "cum_made"))
        pad_made, lev_diff, lev_exp, lev_made, far_exp, far_made, far_diff, own_clear = (
            sem(n) for n in ("pad_made", "lev_diff", "lev_exp", "lev_made", "far_exp", "far_made", "far_diff", "own_clear"))
        sq_g, ss_g, rstd_g = sem("sq_g"), sem("ss_g"), sem("rstd_g")
        sig_made = sem("sig_made")
        smax = sem("smax")
        px_made = sem("px_made")
        bias_out, near_in = sem("bias_out"), sem("near_in")
        bias_made = sem("bias_made")
        mirror_in = sem("mirror_in")
        x_back = sem("x_back")
        packed, roped = sem("packed"), sem("roped")
        row_in = sem("row_in")
        stat_out, nat_in, joint_diff, joint_exp, share_made, share_out = (
            sem(n) for n in ("stat_out", "nat_in", "joint_diff", "joint_exp", "share_made", "share_out"))
        wide_in = [sem(f"wide_in{p}") for p in range(PATTERNS)]
        yb_sum, yb_split, vn_stats, vn_made = sem("yb_sum"), sem("yb_split"), sem("vn_stats"), sem("vn_made")
        ws_in = sem("ws_in")
        b2_in = sem("b2_in")
        merged = sem("merged")
        y_clear = sem("y_clear")
        stored = sem("stored")
        dve_step, act_step, pool_step = sem("dve_step"), sem("act_step"), sem("pool_step")

        def wait(eng, s_, value):
            if not isinstance(value, int) or value > 0:
                eng.wait_ge(s_, value)

        def wait_ready(eng, ready, turn):
            for b, count, plus in ready:
                wait(eng, bank_free[b], at(count, turn, plus))

        def walk(eng, handle):
            for item in s.items:
                if isinstance(item, tuple):
                    turns, body = item
                    with eng.Fori(0, turns) as turn:
                        for st in body:
                            handle(st, turn)
                else:
                    handle(item, None)

        def col(name, n=0, rows=P):
            return cols[0:rows, COLS[name] + n:COLS[name] + n + 1]

        def per_pattern(ap, p):
            return ap if p == 0 else ap.rearrange("q (r m) -> q m r", r=4)

        def natural(ap, p):
            return ap if p == 0 else ap.rearrange("q (m r) -> q m r", r=4)

        def over(ap, n):
            return ap.unsqueeze(1).broadcast_to([ap.shape[0], n, ap.shape[1]])

        def each(ap, n):
            return ap.unsqueeze(2).broadcast_to([ap.shape[0], ap.shape[1], n])

        def copies_of(st):
            b, half = st.bank, st.half
            full = psum[:, b, :]
            if st.out == "kx":
                return kx[:, 4 * st.blk + b, :], psum[:, b, 0:M], 1.0, b % 2 == 0
            if st.out == "vx":
                return vx[:, b, 512 * st.blk:512 * st.blk + 512], full, 1.0, b % 2 == 0
            if st.out == "glaqk":
                return qk_g[:, b, :], full, G_DK ** -0.5 if b < 2 else 1.0, b % 2 == 0
            if st.out == "vg":
                return vg[:, b, :], full, 1.0, b % 2 == 0
            if st.out == "va":
                return va[:, b, :], full, 1.0, b % 2 == 0
            if st.out == "qa":
                return qa[:, b, :], full, A_DIM ** -0.5, b % 2 == 0
            if st.out == "ka":
                return ka[:, b, :], full, 1.0, b % 2 == 0
            if st.out == "qx":
                return qx[:, 4 * st.blk + b, :], full, X_DIM ** -0.5, b % 2 == 0
            if st.out == "v2":
                return v_b[:, b, :], full, 1.0, b % 2 == 0
            if st.out == "copy":
                return y[:, b, 512 * st.blk:512 * st.blk + 512], full, 1.0, b % 2 == 0
            return None

        def blocks_of(p):
            return BAND if p == 0 else OWN

        block = ctx.enter_context(nc.Block())

        @block.sync
        def _(sp):
            for tt in range(TT):
                sp.dma_start(x[:, tt, :], a["x"][P * tt:P * tt + P, :]).then_inc(x_in[tt], 16)
            sp.dma_start(cols[:], a["cols"]).then_inc(cols_in, 16)
            sp.dma_start(ident[:], a["ident"]).then_inc(cols_in, 16)
            sp.dma_start(mirror[:], a["mirror"]).then_inc(mirror_in, 16)
            for t in range(RAW):
                sp.dma_start(w_raw[:, t, :], a["weights"][t]).then_inc(raw_in[t], 16)
            with sp.Fori(1, TILES // RAW) as n:
                for slot in range(RAW):
                    sp.wait_ge(lo_w, n * RAW + (slot + 1 - RAW))
                    sp.dma_start(w_raw[:, slot, :], a["weights"][bass.ds(n * RAW + slot, 1)].rearrange("o p w -> p (o w)")
                                 ).then_inc(raw_in[slot], 16)
            for tt in range(TT):
                sp.wait_ge(x_rows, s.counts["xrows"] - TT + tt + 1)
                sp.dma_start(out[P * tt:P * tt + P, :], x[:, tt, :]).then_inc(stored, 16)
            sp.wait_ge(stored, 16 * TT)

        def split_waits(eng, st, turn):
            if st.slots_free is not None:
                b, count = st.slots_free
                wait(eng, bank_done[b], at(count, turn))

        @block.tensor
        def _(pe):
            def product(out_ap, lhs, rhs, start, stop):
                pe.matmul(out_ap, lhs[0], rhs[0], start=start, stop=False)
                pe.matmul(out_ap, lhs[0], rhs[1], start=False, stop=False)
                return pe.matmul(out_ap, lhs[1], rhs[0], start=False, stop=stop)

            def begin(bank, count, turn):
                wait(pe, bank_free[bank], at(count, turn))

            def gemm(st, turn):
                begin(st.bank, st.fill[0], turn)
                set_at = 4 * (st.tile[0] // 4 % 2)
                b = st.bank
                if st.after == "yb" and st.half == 0 and b == 0:
                    pe.wait_ge(yb_split, 1)
                for k in range(st.rows):
                    tile = k // 2 + st.half * (st.rows // 2)
                    if st.first and k % 2 == 0:
                        pe.wait_ge(lo_w, at(st.tile, turn, tile + 1))
                    if st.ready is not None:
                        wait_ready(pe, st.ready[k:k + 1], turn)
                    if st.src == "mid":
                        n = k // 4 if st.mid is None else st.mid
                        act = (mid_hi[n][:, k % 4, :], mid_lo[n][:, k % 4, :])
                    elif st.src == "memT":
                        act = (mem_hi[:, k, :], mem_lo[:, k, :])
                    else:
                        act = (act_hi[:, k, :], act_lo[:, k, :])
                    w = [x_[:, set_at + tile, (k % 2) * 512:(k % 2) * 512 + 512] for x_ in (w_hi, w_lo)]
                    start, stop = k == 0, k == st.rows - 1
                    if st.major == "T":
                        n = M if st.src == "memT" else T
                        mm = product(psum[:, b, 0:n], [x_[:, b * P:b * P + P] for x_ in w], act, start, stop)
                    else:
                        if st.out == "v2" and st.p > 0:
                            act = [x_.rearrange("q (m r) -> q r m", r=4)[:, b, :] for x_ in act]
                        else:
                            act = [x_[:, b * P:b * P + P] for x_ in act]
                        mm = product(psum[:, b, :], act, w, start, stop)
                mm.then_inc(bank_done[b], 1)

            def handle(st, turn):
                k = st.kind
                if k == "gemm":
                    gemm(st, turn)
                elif k == "flip":
                    pe.wait_ge(mirror_in, 16)
                    pe.wait_ge(near_in, 16)
                    for n in range(4):
                        begin(SIDE[n], st.fill[n], turn)
                        pe.matmul(psum[:, SIDE[n], :], mirror[:], near_back[:, 2 * n:2 * n + 2, :].rearrange("q h j -> q (h j)"),
                                  start=True, stop=True).then_inc(bank_done[SIDE[n]], 1)
                elif k == "turn":
                    for half in range(2):
                        chunks = st.chunks[4 * half:4 * half + 4]
                        for n in range(4):
                            begin(SIDE[n], st.fill[4 * half + n], turn)
                        for tt in range(st.tiles):
                            if half == 0 and st.src != "mix":
                                pe.wait_ge(xn_made, at(st.src, turn, tt + 1))
                            if half == 0 and tt == 0 and st.src == "mix":
                                wait_ready(pe, st.ready, turn)
                            for c in chunks:
                                if st.src == "mix":
                                    src = o_a[:, tt, c * P:c * P + P] if c < 4 else og[:, tt, (c - 4) * P:(c - 3) * P]
                                else:
                                    src = (y if st.tiles == TT else memn)[:, tt, c * P:c * P + P]
                                mm = pe.transpose(psum[:, SIDE[c % 4], tt * P:tt * P + P], src, ident[:])
                                if tt == st.tiles - 1:
                                    mm.then_inc(bank_done[SIDE[c % 4]], 1)
                elif k == "glr":
                    begin(4, st.fill[0], turn)
                    pe.wait_ge(glr_lo, 1)
                    for c in range(KC):
                        mm = product(psum[:, 4, :], (g_hi[:, c, :], g_lo[:, c, :]), (act_hi[:, c, :], act_lo[:, c, :]),
                                     c == 0, c == KC - 1)
                    mm.then_inc(bank_done[4], 1)
                elif k == "gate":
                    wait(pe, bank_free[4], at(s.glr.fill[0], None, 1))
                    pe.wait_ge(const_in, 32)
                    for pair in range(2):
                        b = 5 + pair
                        begin(b, st.fill[pair], turn)
                        pe.matmul(psum[:, b, :], w_gu[:, pair * P:pair * P + P], glr_t[:], start=True, stop=True
                                  ).then_inc(bank_done[b], 1)
                elif k == "relbias":
                    begin(4, st.fill[0], turn)
                    pe.wait_ge(table_in, 32)
                    pe.matmul(psum[0:A_HEADS, 4, 0:REL], table[0:RP_BUCKETS, :], bucket[0:RP_BUCKETS, :], start=True,
                              stop=True).then_inc(bank_done[4], 1)
                elif k == "level":
                    if st.n < len(LEVELS):
                        pe.wait_ge(lev_made, st.n + 1)
                    for half in range(2):
                        for kind in range(2):
                            begin(SIDE[2 * half + kind], st.fill[2 * half + kind], turn)
                        for n in range(4):
                            tt, pair = 2 * half + n // 2, n % 2
                            for kind in range(2):
                                rows = slice(64 * kind, 64 * kind + 64)
                                if st.n < len(LEVELS):
                                    lhs = rhs = lev[st.n % 2][rows, pair, tt * P:tt * P + P]
                                else:
                                    lhs = qk_g[rows, 2 + pair, tt * P:tt * P + P]
                                    rhs = qk_g[rows, pair, tt * P:tt * P + P]
                                mm = pe.matmul(psum[:, SIDE[2 * half + kind], n * P:n * P + P], lhs, rhs, start=True, stop=True)
                                if n == 3:
                                    mm.then_inc(bank_done[SIDE[2 * half + kind]], 1)
                elif k == "far":
                    pe.wait_ge(far_made, 8)
                    for fill in range(0, len(PAIRS), 2):
                        for kind in range(2):
                            begin(SIDE[(fill + kind) % 4], st.fill[fill + kind], turn)
                        for n in range(4):
                            (j, i), pair = PAIRS[fill + n // 2], n % 2
                            for kind in range(2):
                                rows, b = slice(64 * kind, 64 * kind + 64), SIDE[(fill + kind) % 4]
                                if i - j == 1:
                                    rhs = q_far[rows, pair, i * P:i * P + P]
                                else:
                                    rhs = q_mid[rows, pair, {(0, 2): 0, (1, 3): 1, (0, 3): 2}[j, i], :]
                                mm = pe.matmul(psum[:, b, n * P:n * P + P], k_far[rows, pair, j * P:j * P + P], rhs,
                                               start=True, stop=True)
                                if n == 3:
                                    mm.then_inc(bank_done[b], 1)
                elif k == "glaout":
                    for i in range(TT):
                        b = SIDE[i]
                        if i == 0:
                            for n in range(4):
                                begin(SIDE[n], st.fill[n], turn)
                        for h in range(G_HEADS):
                            for j in range(i + 1):
                                lhs = a_own[:, h % 2, i, h // 2, :] if j == i else a_far[:, h % 2, PAIRS.index((j, i)), h // 2, :]
                                mm = pe.matmul(psum[:, b, h * P:h * P + P], lhs, vg[:, j, h * P:h * P + P],
                                               start=(j == 0), stop=(j == i))
                        mm.then_inc(bank_done[b], 1)
                elif k == "sa_qk":
                    rows, pair = slice(64 * (st.h % 2), 64 * (st.h % 2) + 64), st.h // 2
                    for i, n, c0, ends in ROW_PLACES:
                        b = st.banks[n]
                        if c0 == 0:
                            begin(b, st.fill[n], turn)
                        mm = pe.matmul(psum[:, b, c0:c0 + P * (i + 1)], qa[rows, pair, i * P:i * P + P],
                                       ka[rows, pair, 0:P * (i + 1)], start=True, stop=True)
                        if ends:
                            mm.then_inc(bank_done[b], 1)
                elif k in ("sa_t", "bt_t"):
                    blocks = CAUSAL if k == "sa_t" else blocks_of(st.p)
                    src = p_a[st.h % 2] if k == "sa_t" else p_b(st)
                    wait_ready(pe, st.ready, turn)
                    for n in range(len(blocks)):
                        b = st.banks[n // 4]
                        if n % 4 == 0:
                            begin(b, st.fill[n // 4], turn)
                        mm = pe.transpose(psum[:, b, n % 4 * P:n % 4 * P + P], src[:, n * P:n * P + P], ident[:])
                        if n % 4 == 3 or n == len(blocks) - 1:
                            mm.then_inc(bank_done[b], 1)
                elif k == "sa_pv":
                    b = st.banks[0]
                    begin(b, st.fill[0], turn)
                    wait_ready(pe, st.ready, turn)
                    for i in range(TT):
                        for j in range(i + 1):
                            n = CAUSAL.index((i, j))
                            mm = pe.matmul(psum[:, b, i * A_DIM:i * A_DIM + A_DIM], pt_a[st.h % 2][:, n * P:n * P + P],
                                           va[:, j, st.h * A_DIM:st.h * A_DIM + A_DIM], start=(j == 0), stop=(j == i))
                    mm.then_inc(bank_done[b], 1)
                elif k == "ca_qk":
                    wait_ready(pe, st.ready, turn)
                    for n in range(2):
                        b = st.banks[n]
                        begin(b, st.fill[n], turn)
                        for tt in (2 * n, 2 * n + 1):
                            for e in range(2):
                                mm = pe.matmul(psum[:, b, tt % 2 * M:tt % 2 * M + M], qx[:, 2 * st.h + e, tt * P:tt * P + P],
                                               kx[:, 2 * st.h + e, :], start=(e == 0), stop=(e == 1))
                        mm.then_inc(bank_done[b], 1)
                elif k == "ca_t":
                    pe.wait_ge(px_made, st.h + 1)
                    for mt in range(MT):
                        begin(mt, st.fill[mt], turn)
                        for tt in range(TT):
                            mm = pe.transpose(psum[:, mt, tt * P:tt * P + P], p_x[st.h % 2][:, tt, mt * P:mt * P + P], ident[:])
                        mm.then_inc(bank_done[mt], 1)
                elif k == "ca_pv":
                    wait_ready(pe, st.ready, turn)
                    for e in range(2):
                        b = st.banks[e]
                        begin(b, st.fill[e], turn)
                        at_e = st.h * X_DIM + e * P
                        for mt in range(MT):
                            mm = pe.matmul(psum[:, b, :], vx[:, mt, at_e:at_e + P], pt_x[st.h % 2][:, mt, :],
                                           start=(mt == 0), stop=(mt == MT - 1))
                        mm.then_inc(bank_done[b], 1)
                elif k == "bt_qk":
                    pe.wait_ge(roped, at(st.roped, turn, 1))
                    q_b, k_b = qk_b["q"][st.p], qk_b["k"][st.p]
                    if st.p == 0:
                        for i, n, c0, ends in BAND_PLACES:
                            b = st.banks[n]
                            if c0 == 0:
                                begin(b, st.fill[n], turn)
                            ks = [kt for q_, kt in BAND if q_ == i]
                            mm = pe.matmul(psum[:, b, c0:c0 + P * len(ks)], q_b[:, st.h, i * P:i * P + P],
                                           k_b[:, st.h, ks[0] * P:(ks[-1] + 1) * P], start=True, stop=True)
                            if ends:
                                mm.then_inc(bank_done[b], 1)
                    else:
                        b = st.banks[0]
                        begin(b, st.fill[0], turn)
                        for i in range(TT):
                            mm = pe.matmul(psum[:, b, i * P:i * P + P], q_b[:, st.h, i * P:i * P + P],
                                           k_b[:, st.h, i * P:i * P + P], start=True, stop=True)
                        mm.then_inc(bank_done[b], 1)
                elif k == "bt_pv":
                    begin(7, st.fill[0], turn)
                    wait_ready(pe, st.ready, turn)
                    blocks = blocks_of(st.p)
                    for i in range(TT):
                        ks = [kt for q_, kt in blocks if q_ == i]
                        for kt in ks:
                            n = blocks.index((i, kt))
                            mm = pe.matmul(psum[:, 7, i * P:i * P + P], v_b[:, kt, st.h * P:st.h * P + P],
                                           pt_b(st)[:, n * P:n * P + P], start=(kt == ks[0]), stop=(kt == ks[-1]))
                    mm.then_inc(bank_done[7], 1)
                elif k == "spatial":
                    pe.wait_ge(ws_in, 32)
                    pe.wait_ge(vn_made, TT)
                    for g in range(4):
                        begin(SIDE[g], st.fill[g], turn)
                        for c in range(TT):
                            mm = pe.matmul(psum[:, SIDE[g], c * P:c * P + P], vt[:, c, g * P:g * P + P], ws_t[:, g, :],
                                           start=True, stop=True)
                        mm.then_inc(bank_done[SIDE[g]], 1)

            pe.wait_ge(cols_in, 32)
            walk(pe, handle)

        @block.scalar
        def _(act):
            step = [0]

            def then(ins):
                step[0] += 1
                ins.then_inc(act_step, 1)
                act.wait_ge(act_step, step[0])

            def split(st, turn):
                for tile in st.splits:
                    split_waits(act, st, turn)
                    one_split(tile, turn)

            def one_split(tile, turn):
                t = tile[0]
                act.wait_ge(raw_in[t % RAW], at([16 * (t // RAW + 1), tile[1] * 16 // RAW], turn))
                act.activation(w_hi[:, t % 8, :], w_raw[:, t % RAW, :], ACT.Copy).then_inc(hi_w, 1)

            def tables():
                act.preload_act_table_set("natural_log_exp_and_others")

            def rms(slot, width, signal):
                then(act.activation(lnv[:, slot], sumsq[:, slot], ACT.Ln, bias=eps[:, 0:1], scale=1.0 / width))
                act.activation(rstd[:, slot], lnv[:, slot], ACT.Exp, scale=-0.5).then_inc(signal, 1)

            def gemm(st, turn):
                split(st, turn)
                b = st.bank
                filled = lambda: wait(act, bank_done[b], at(st.fill[0], turn, 1))
                plain = copies_of(st)
                if plain is not None and plain[3]:
                    filled()
                    act.activation(plain[0], plain[1], ACT.Copy, scale=plain[2]).then_inc(bank_free[b], 1)
                elif st.out == "rg":
                    filled()
                    act.activation(sg[:, b, :], psum[:, b, :], ACT.Sigmoid).then_inc(sig_made, 1)
                    if b == TT - 1:
                        tables()
                elif st.out == "up":
                    filled()
                    n = b % 2
                    wait(act, square_made, at(st.relu, turn, -1))
                    act.activation(relu[n][:], psum[:, b, :], ACT.Relu).then_inc(relu_made, 1)
                    act.wait_ge(relu_made, at(st.relu, turn, 1))
                    act.activation(mid_hi[st.mid][:, b, :], relu[n][:], ACT.Square).then_inc(hi_made, 1)
                elif st.out == "rope":
                    filled()
                    if b == 0 and st.after is not None:
                        act.wait_ge(roped, at(st.after, turn, 1))
                    act.activation(pack[ROPE_DIM * b:ROPE_DIM * b + ROPE_DIM, :], psum[0:ROPE_DIM, b, :], ACT.Copy
                                   ).then_inc(packed, 1)
                elif st.out == "u":
                    filled()
                    act.activation(ut[:, b, :], psum[:, b, :], ACT.Gelu_apprx_tanh).then_inc(bank_free[b], 1)
                elif st.out == "v":
                    filled()
                    act.activation(vt[:, b, :], psum[:, b, :], ACT.Gelu_apprx_tanh).then_inc(bank_free[b], 1)
                elif st.out == "gate":
                    filled()
                    if st.blk == 0 and b == 0:
                        act.wait_ge(yb_split, 1)
                    act.activation(gate[st.blk][:, b, :], psum[:, b, :], ACT.Sigmoid,
                                   bias=col("b_gate_2", 4 * st.blk + b)).then_inc(bank_free[b], 1)
                    if st.blk == 3 and b == TT - 1:
                        tables()
                elif st.out == "merge":
                    act.wait_ge(merged, at(st.merged, turn, 1))
                    act.activation(act_hi[:, 4 * st.half + b, :], gate[st.half][:, b, :], ACT.Copy).then_inc(hi_made, 1)

            def handle(st, turn):
                k = st.kind
                if k == "start":
                    for t in range(4):
                        one_split([t, 0], None)
                    act.wait_ge(glr_in, 16)
                    act.wait_ge(pad_made, 3)
                    act.activation(g_hi[:, :, 0:G_RANK], g_raw[:], ACT.Copy).then_inc(glr_hi, 1)
                elif k == "gemm":
                    gemm(st, turn)
                elif k in ("scale", "rows"):
                    src = {"mem": mem, "x": x, "y": y}[st.src]
                    if k == "scale":
                        waste = memn if st.src == "mem" else y
                    else:
                        waste = {"norm_final": y, "norm_mix_post_2": junk["y1"], "norm_mlp_post_2": junk["y2"]}[st.row]
                    for tt in range(TT if k == "rows" else st.tiles):
                        if st.ready == "mem":
                            act.wait_ge(mem_in, 16)
                        elif st.ready == "x":
                            act.wait_ge(x_in[tt], 16)
                        elif st.ready == "rows":
                            act.wait_ge(x_rows, at(st.after_rows, turn, tt + 1))
                        else:
                            wait_ready(act, st.ready[tt:tt + 1], turn)
                        then(act.activation(waste[:, tt, :], src[:, tt, :], ACT.Square, accum_out=sumsq[:, tt:tt + 1]))
                        rms(slice(tt, tt + 1), D, rstd_made)
                elif k == "turn":
                    for n_c, c in enumerate(st.chunks):
                        b, n = SIDE[c % 4], P * st.tiles
                        wait(act, bank_done[b], at(st.fill[n_c], turn, 1))
                        hi = {"act": act_hi, "memT": mem_hi}[st.dst][:, c, :] if st.dst != "mid" else mid_hi[c // 4][:, c % 4, :]
                        gain = st.gains[c]
                        scale = 1.0 if gain is None else col(gain, 0 if gain == "g_norm" else c)
                        act.activation(hi, psum[:, b, 0:n], ACT.Copy, scale=scale).then_inc(hi_made, 1)
                elif k == "gate":
                    for pair in range(2):
                        act.wait_ge(bank_done[5 + pair], at(st.fill[pair], turn, 1))
                        act.activation(ex_g[:, pair, :], psum[:, 5 + pair, :], ACT.Abs, bias=col("b_gate", pair)
                                       ).then_inc(gate_abs, 1)
                    act.wait_ge(gate_abs, 2)
                    then(act.activation(ex_g[:], ex_g[:], ACT.Exp, scale=-1.0))
                    act.activation(ex_g[:], ex_g[:], ACT.Ln, bias=1.0).then_inc(gate_log, 1)
                    for n in range(2):
                        act.wait_ge(lev_diff, 2 * n + 2)
                        act.activation(ex_g[:], ex_g[:], ACT.Exp, scale=1.0 / G_NORM).then_inc(lev_exp, 1)
                elif k == "flip":
                    for n in range(0, 4, 2):
                        act.wait_ge(bank_done[SIDE[n]], at(st.fill[n], turn, 1))
                        act.activation(near[:, 2 * n:2 * n + 2, :].rearrange("q h j -> q (h j)"), psum[:, SIDE[n], :], ACT.Copy
                                       ).then_inc(bank_free[SIDE[n]], 1)
                elif k == "level":
                    n = st.n + 2
                    if n < len(LEVELS):
                        act.wait_ge(lev_diff, 2 * n + 2)
                        act.activation(ex_g[:], ex_g[:], ACT.Exp, scale=1.0 / G_NORM).then_inc(lev_exp, 1)
                elif k == "farprep":
                    act.wait_ge(cum_made, 2)
                    then(act.activation(q_far[:], cum[:], ACT.Exp, scale=1.0 / G_NORM))
                    last = cum[:].rearrange("q c (t n) -> q c t n", t=TT)[:, :, :, P - 1]
                    then(act.activation(decay[:], last, ACT.Exp, scale=1.0 / G_NORM))
                    act.wait_ge(far_diff, TT * 2)
                    act.activation(k_far[:], k_far[:], ACT.Exp, scale=1.0 / G_NORM).then_inc(far_exp, 1)
                elif k == "far":
                    for n in range(0, len(PAIRS), 2):
                        b = SIDE[n % 4]
                        act.wait_ge(bank_done[b], at(st.fill[n], turn, 1))
                        act.activation(a_far[:, n % 2, n - n % 2:n - n % 2 + 2].rearrange("q t c i -> q (t c i)"), psum[:, b, :], ACT.Copy).then_inc(bank_free[b], 1)
                elif k == "glaout":
                    for i in range(TT):
                        act.wait_ge(bank_done[SIDE[i]], at(st.fill[i], turn, 1))
                        wait(act, ss_g, i - 1)
                        act.activation(square_g[:, i % 2, :], psum[:, SIDE[i], :], ACT.Square).then_inc(sq_g, 1)
                        act.wait_ge(ss_g, i + 1)
                        rms(slice(4 * i, 4 * i + 4), G_DV, rstd_g)
                elif k == "sa_qk":
                    for order, (i, b_n, c0, ends) in enumerate(ROW_PLACES):
                        act.wait_ge(smax, at(st.smax, turn, order + 1 if ends else order + 2))
                        n, b = CAUSAL.index((i, 0)), st.banks[b_n]
                        ins = act.activation(p_a[st.h % 2][:, n * P:(n + i + 1) * P], psum[:, b, c0:c0 + P * (i + 1)], ACT.Exp,
                                             bias=nmax[:, st.h, i:i + 1], accum_out=den[:, st.h, i:i + 1])
                        if ends:
                            ins.then_inc(bank_free[b], 1)
                elif k in ("sa_t", "bt_t"):
                    dst = pt_a[st.h % 2] if k == "sa_t" else pt_b(st)
                    n = len(CAUSAL if k == "sa_t" else blocks_of(st.p))
                    for part in range(0, (n + 3) // 4, 2):
                        w, b = min(4, n - 4 * part) * P, st.banks[part]
                        act.wait_ge(bank_done[b], at(st.fill[part], turn, 1))
                        act.activation(dst[:, 4 * part * P:4 * part * P + w], psum[:, b, 0:w], ACT.Copy).then_inc(bank_free[b], 1)
                elif k == "ca_qk":
                    act.wait_ge(smax, at(st.smax, turn, 1))
                    for tt in range(TT):
                        b = st.banks[tt // 2]
                        ins = act.activation(p_x[st.h % 2][:, tt, :], psum[:, b, tt % 2 * M:tt % 2 * M + M], ACT.Exp,
                                             bias=nmax[:, st.h, tt:tt + 1], accum_out=den[:, st.h, tt:tt + 1])
                        if tt % 2:
                            ins.then_inc(bank_free[b], 1)
                elif k == "ca_t":
                    act.wait_ge(bank_done[0], at(st.fill[0], turn, 1))
                    act.activation(pt_x[st.h % 2][:, 0, :], psum[:, 0, :], ACT.Copy).then_inc(bank_free[0], 1)
                elif k == "ca_pv":
                    for e in range(2):
                        b, c = st.banks[e], 2 * st.h + e
                        act.wait_ge(bank_done[b], at(st.fill[e], turn, 1))
                        act.activation(mid_hi[c // 4][:, c % 4, :], psum[:, b, :], ACT.Copy).then_inc(hi_made, 1)
                elif k == "bt_qk":
                    blocks = blocks_of(st.p)
                    act.wait_ge(smax, at(st.smax, turn, 1))
                    places = BAND_PLACES if st.p == 0 else [(i, 0, i * P, i == TT - 1) for i in range(TT)]
                    for i, b_n, c0, ends in places:
                        ks = [n for n, (q_, _) in enumerate(blocks) if q_ == i]
                        w, b = len(ks) * P, st.banks[b_n]
                        ins = act.activation(p_b(st)[:, ks[0] * P:ks[0] * P + w], psum[:, b, c0:c0 + w], ACT.Exp,
                                             bias=nbias[:, st.h, i:i + 1], scale=B_DIM ** -0.5,
                                             accum_out=mden[:, st.p, i, st.h, 1:2])
                        if ends:
                            ins.then_inc(bank_free[b], 1)
                elif k == "bt_pv":
                    act.wait_ge(bank_done[7], at(st.fill[0], turn, 1))
                    act.activation(natural(u_b[st.p][:, st.h, :], st.p), per_pattern(psum[:, 7, :], st.p), ACT.Copy
                                   ).then_inc(bank_free[7], 1)
                elif k == "joint":
                    act.wait_ge(joint_diff, 1)
                    act.activation(ex[:], ex[:], ACT.Exp, scale=B_DIM ** -0.5).then_inc(joint_exp, 1)
                elif k == "lnv":
                    tables()
                    act.wait_ge(vn_stats, 1)
                    then(act.activation(lnv[:, 0:TT], vmean[:, :, 1], ACT.Ln, bias=eps[:, 0:1]))
                    act.activation(rstd[:, 0:TT], lnv[:, 0:TT], ACT.Exp, scale=-0.5).then_inc(rstd_made, 1)
                elif k == "spatial":
                    for g in range(4):
                        act.wait_ge(merged, at(st.merged, turn, g + 1))
                        act.activation(mid_hi[0][:, g, :], ya_sum[:, g % 2, :], ACT.Copy).then_inc(hi_made, 1)
                elif k == "ybsplit":
                    act.wait_ge(yb_sum, 1)
                    wait_ready(act, st.ready, turn)
                    act.activation(mid_hi[1][:], u_b[0][:], ACT.Copy).then_inc(hi_made, 1)

            tables()
            act.wait_ge(cols_in, 32)
            walk(act, handle)

        @block.vector
        def _(dve):
            step = [0]

            def then(ins):
                step[0] += 1
                ins.then_inc(dve_step, 1)
                dve.wait_ge(dve_step, step[0])

            def one_split(tile, turn):
                t = tile[0]
                dve.wait_ge(hi_w, at(tile, turn, 1))
                dve.tensor_tensor(w_lo[:, t % 8, :], w_raw[:, t % RAW, :], w_hi[:, t % 8, :], ALU.subtract).then_inc(lo_w, 1)

            def gemm(st, turn):
                for tile in st.splits:
                    split_waits(dve, st, turn)
                    one_split(tile, turn)
                b = st.bank
                filled = lambda: wait(dve, bank_done[b], at(st.fill[0], turn, 1))
                plain = copies_of(st)
                if plain is not None and not plain[3]:
                    filled()
                    dve.tensor_scalar(plain[0], plain[1], plain[2], None, ALU.mult).then_inc(bank_free[b], 1)
                elif st.out == "rg":
                    dve.wait_ge(sig_made, b + 1)
                    dve.tensor_tensor(sg[:, b, :], psum[:, b, :], sg[:, b, :], ALU.mult).then_inc(bank_free[b], 1)
                elif st.out == "add":
                    filled()
                    dst = {"x": x, "y": y}[st.dst]
                    col0 = 512 * (st.half if st.rows == 4 else st.blk)
                    if st.after == "x_back":
                        dve.wait_ge(x_back, 16)
                    dve.tensor_tensor(dst[:, b, col0:col0 + 512], psum[:, b, :], dst[:, b, col0:col0 + 512], ALU.add
                                      ).then_inc(bank_free[b], 1)
                elif st.out == "up":
                    n = b % 2
                    dve.wait_ge(relu_made, at(st.relu, turn, 1))
                    dve.tensor_tensor(square[n][:], relu[n][:], relu[n][:], ALU.mult).then_inc(square_made, 1)
                    dve.wait_ge(square_made, at(st.relu, turn, 1))
                    dve.wait_ge(hi_made, at(st.hi, turn, 1))
                    dve.tensor_tensor(mid_lo[st.mid][:, b, :], square[n][:], mid_hi[st.mid][:, b, :], ALU.subtract
                                      ).then_inc(bank_free[b], 1)
                elif st.out == "rope":
                    dve.wait_ge(packed, at(st.packed, turn, 1))
                    dve.tensor_copy(per_pattern(qk_b[st.dst][st.p][:, b, :], st.p), natural(psum[:, b, :], st.p)).then_inc(bank_free[b], 1)
                elif st.out == "bra":
                    filled()
                    g = gate[st.half][:, b, :]
                    dve.tensor_tensor(g, psum[:, b, :], g, ALU.mult).then_inc(bank_free[b], 1)
                elif st.out == "merge":
                    filled()
                    ga, gb = gate[st.half][:, b, :], gate[2 + st.half][:, b, :]
                    then(dve.tensor_tensor(gb, psum[:, b, :], gb, ALU.mult))
                    dve.tensor_tensor(ga, ga, gb, ALU.add).then_inc(merged, 1)
                    dve.wait_ge(merged, at(st.merged, turn, 1))
                    dve.wait_ge(hi_made, at(st.hi, turn, 1))
                    dve.tensor_tensor(act_lo[:, 4 * st.half + b, :], ga, act_hi[:, 4 * st.half + b, :], ALU.subtract
                                      ).then_inc(bank_free[b], 1)

            def handle(st, turn):
                k = st.kind
                if k == "start":
                    for t in range(4):
                        one_split([t, 0], None)
                    dve.wait_ge(glr_hi, 1)
                    dve.tensor_tensor(g_lo[:, :, 0:G_RANK], g_raw[:], g_hi[:, :, 0:G_RANK], ALU.subtract).then_inc(glr_lo, 1)
                elif k == "gemm":
                    gemm(st, turn)
                elif k == "scale":
                    src, dst = (mem, memn) if st.src == "mem" else (x, y)
                    for tt in range(st.tiles):
                        dve.wait_ge(rstd_made, at(st.rstd, turn, tt + 1))
                        dve.tensor_scalar(dst[:, tt, :], src[:, tt, :], rstd[:, tt:tt + 1], None, ALU.mult).then_inc(xn_made, 1)
                elif k == "rows":
                    dve.wait_ge(row_in, 16 * st.row_n)
                    src = {"x": x, "y": y}[st.src]
                    for tt in range(TT):
                        dve.wait_ge(rstd_made, at(st.rstd, turn, tt + 1))
                        ins = dve.scalar_tensor_tensor(src[:, tt, :], src[:, tt, :], rstd[:, tt:tt + 1], row[:], ALU.mult, ALU.mult)
                        if st.src == "y":
                            then(ins)
                            ins = dve.tensor_tensor(x[:, tt, :], x[:, tt, :], y[:, tt, :], ALU.add)
                        ins.then_inc(x_rows, 1)
                elif k == "turn":
                    for n_c, c in enumerate(st.chunks):
                        b, n = SIDE[c % 4], P * st.tiles
                        dve.wait_ge(hi_made, at(st.hi, turn, n_c + 1))
                        if st.dst == "mid":
                            hi, lo = mid_hi[c // 4][:, c % 4, :], mid_lo[c // 4][:, c % 4, :]
                        else:
                            hi, lo = [t_[:, c, :] for t_ in {"act": (act_hi, act_lo), "memT": (mem_hi, mem_lo)}[st.dst]]
                        gain = st.gains[c]
                        scale = 1.0 if gain is None else col(gain, 0 if gain == "g_norm" else c)
                        dve.scalar_tensor_tensor(lo, psum[:, b, 0:n], scale, hi, ALU.mult, ALU.subtract).then_inc(bank_free[b], 1)
                elif k == "glr":
                    dve.wait_ge(bank_done[4], at(st.fill[0], turn, 1))
                    dve.wait_ge(bias_out, 16)
                    dve.tensor_copy(glr_t[:], psum[0:G_RANK, 4, :]).then_inc(bank_free[4], 1)
                elif k == "gate":
                    for pair in range(2):
                        dve.wait_ge(gate_abs, pair + 1)
                        ins = dve.tensor_scalar(lev[0][:, pair, :], psum[:, 5 + pair, :], col("b_gate", pair), 0.0, ALU.add, ALU.min)
                        ins.then_inc(bank_free[5 + pair], 1)
                    dve.wait_ge(gate_log, 1)
                    for pair in range(2):
                        dve.wait_ge(bank_free[5 + pair], at(st.fill[pair], turn, 1))
                    then(dve.tensor_tensor(lev[0][:], lev[0][:], ex_g[:], ALU.subtract))
                    for pair in range(2):
                        for tt in range(TT):
                            part = slice(tt * P, tt * P + P)
                            ins = dve.tensor_tensor_scan(cum[:, pair, part], lev[0][:, pair, part], lev[0][:, pair, part], 0.0,
                                                         ALU.add, ALU.bypass)
                        ins.then_inc(cum_made, 1)
                elif k == "flip":
                    for n in range(1, 4, 2):
                        dve.wait_ge(bank_done[SIDE[n]], at(st.fill[n], turn, 1))
                        dve.tensor_copy(near[:, 2 * n:2 * n + 2, :].rearrange("q h j -> q (h j)"), psum[:, SIDE[n], :]
                                        ).then_inc(bank_free[SIDE[n]], 1)
                elif k == "relbias":
                    dve.wait_ge(bank_done[4], at(st.fill[0], turn, 1))
                    dve.tensor_copy(bias_row[0:A_HEADS, 0:NEAR], psum[0:A_HEADS, 4, 0:NEAR]).then_inc(bank_free[4], 1)
                    dve.memset(bias_row[0:A_HEADS, NEAR:REL], MASKED).then_inc(bias_made, 1)
                elif k == "level":
                    dve.wait_ge(own_clear, 1)
                    dve.wait_ge(const_in, 32)
                    for n in range(4):
                        b = SIDE[n]
                        dve.wait_ge(bank_done[b], at(st.fill[n], turn, 1))
                        own_part = a_own[:, n % 2, n // 2 * 2:n // 2 * 2 + 2].rearrange("q t c i -> q (t c) i")
                        dve.copy_predicated(own_part, over(lvl_mask[:, st.n, :], G_HEADS),
                                            psum[:, b, :].rearrange("q (h i) -> q h i", h=G_HEADS)).then_inc(bank_free[b], 1)
                elif k == "farprep":
                    dve.wait_ge(cum_made, 2)
                    for pair in range(2):
                        for tt in range(TT):
                            part = slice(tt * P, tt * P + P)
                            dve.tensor_scalar(k_far[:, pair, part], cum[:, pair, part], -1.0,
                                              cum[:, pair, tt * P + P - 1:tt * P + P], ALU.mult, ALU.add).then_inc(far_diff, 1)
                    dve.wait_ge(far_exp, 1)
                    dve.tensor_tensor(k_far[:], k_far[:], qk_g[:, 2:4, :], ALU.mult).then_inc(far_made, 1)
                    dve.tensor_tensor(q_far[:], q_far[:], qk_g[:, 0:2, :], ALU.mult).then_inc(far_made, 1)
                elif k == "far":
                    dve.wait_ge(lev_diff, 2 * len(LEVELS))
                    dve.wait_ge(far_made, 2)
                    for pair in range(2):
                        dve.tensor_scalar(q_mid[:, pair, 0, :], q_far[:, pair, 2 * P:3 * P], decay[:, pair, 1:2], None,
                                          ALU.mult).then_inc(far_made, 1)
                        dve.tensor_scalar(q_mid[:, pair, 1, :], q_far[:, pair, 3 * P:4 * P], decay[:, pair, 2:3], None,
                                          ALU.mult).then_inc(far_made, 1)
                        dve.tensor_scalar(q_mid[:, pair, 2, :], q_far[:, pair, 3 * P:4 * P], decay[:, pair, 2:3],
                                          decay[:, pair, 1:2], ALU.mult, ALU.mult).then_inc(far_made, 1)
                    for n in range(1, len(PAIRS), 2):
                        b = SIDE[n % 4]
                        dve.wait_ge(bank_done[b], at(st.fill[n], turn, 1))
                        dve.tensor_copy(a_far[:, n % 2, n - n % 2:n - n % 2 + 2].rearrange("q t c i -> q (t c i)"), psum[:, b, :]).then_inc(bank_free[b], 1)
                elif k == "glaout":
                    for i in range(TT):
                        dve.wait_ge(sq_g, i + 1)
                        dve.tensor_reduce(sumsq[:, 4 * i:4 * i + 4], square_g[:, i % 2, :].rearrange("q (h e) -> q h e", h=G_HEADS),
                                          AX.X, ALU.add).then_inc(ss_g, 1)
                        dve.wait_ge(rstd_g, i + 1)
                        v = og[:, i, :].rearrange("q (h e) -> q h e", h=G_HEADS)
                        then(dve.tensor_tensor(v, psum[:, SIDE[i], :].rearrange("q (h e) -> q h e", h=G_HEADS),
                                               each(rstd[:, 4 * i:4 * i + 4], G_DV), ALU.mult))
                        dve.tensor_tensor(og[:, i, :], og[:, i, :], sg[:, i, :], ALU.mult).then_inc(bank_free[SIDE[i]], 1)
                elif k == "sa_qk":
                    if st.h == 0:
                        wait_ready(dve, st.ready, turn)
                    for i, b_n, c0, ends in ROW_PLACES:
                        b, end = st.banks[b_n], c0 + P * (i + 1)
                        dve.wait_ge(bank_done[b], at(st.fill[b_n], turn, 1))
                        n = min(P * (i + 1), NEAR)
                        then(dve.tensor_tensor(psum[:, b, end - n:end], psum[:, b, end - n:end], near[:, st.h, NEAR - n:NEAR], ALU.add))
                        dve.tensor_reduce(nmax[:, st.h, i:i + 1], psum[:, b, c0:end], AX.X, ALU.max, negate=True).then_inc(smax, 1)
                elif k in ("sa_t", "bt_t"):
                    dst = pt_a[st.h % 2] if k == "sa_t" else pt_b(st)
                    if k == "sa_t" or st.p == 0:
                        b = st.banks[1]
                        dve.wait_ge(bank_done[b], at(st.fill[1], turn, 1))
                        dve.tensor_copy(dst[:, 4 * P:8 * P], psum[:, b, :]).then_inc(bank_free[b], 1)
                elif k == "sa_pv":
                    then(dve.reciprocal(rden[:, st.h, :], den[:, st.h, :]))
                    b = st.banks[0]
                    dve.wait_ge(bank_done[b], at(st.fill[0], turn, 1))
                    dve.tensor_tensor(o_a[:, :, st.h * A_DIM:st.h * A_DIM + A_DIM],
                                      psum[:, b, 0:TT * A_DIM].rearrange("q (t d) -> q t d", t=TT),
                                      each(rden[:, st.h, :], A_DIM), ALU.mult).then_inc(bank_free[b], 1)
                elif k == "ca_qk":
                    for n in range(2):
                        dve.wait_ge(bank_done[st.banks[n]], at(st.fill[n], turn, 1))
                    b = st.banks[0]
                    dve.tensor_reduce(nmax[:, st.h, :], psum[:, b:b + 2, :].rearrange("q b (t m) -> q (b t) m", t=2), AX.X, ALU.max,
                                      negate=True).then_inc(smax, 1)
                    for n in range(2):
                        dve.wait_ge(bank_free[st.banks[n]], at(st.fill[n], turn, 1))
                    then(dve.reciprocal(rden[:, st.h, :], den[:, st.h, :]))
                    dve.tensor_tensor(p_x[st.h % 2][:], p_x[st.h % 2][:], each(rden[:, st.h, :], M), ALU.mult).then_inc(px_made, 1)
                elif k == "ca_t":
                    dve.wait_ge(bank_done[1], at(st.fill[1], turn, 1))
                    dve.tensor_copy(pt_x[st.h % 2][:, 1, :], psum[:, 1, :]).then_inc(bank_free[1], 1)
                elif k == "ca_pv":
                    for e in range(2):
                        b, c = st.banks[e], 2 * st.h + e
                        dve.wait_ge(hi_made, at(st.hi, turn, e + 1))
                        dve.tensor_tensor(mid_lo[c // 4][:, c % 4, :], psum[:, b, :], mid_hi[c // 4][:, c % 4, :], ALU.subtract
                                          ).then_inc(bank_free[b], 1)
                elif k == "rope":
                    dve.wait_ge(packed, at(st.packed, turn))
                    if st.p == 0 and st.dst == "q":
                        dve.wait_ge(b2_in, 64)
                    swap = [(n + ROPE_DIM // 2) % ROPE_DIM for n in range(ROPE_DIM)]
                    then(dve.stream_shuffle(turned[:], pack[:], swap))
                    then(dve.tensor_tensor(pack[:], pack[:], cosine[:], ALU.mult))
                    then(dve.tensor_tensor(turned[:], turned[:], sine[:], ALU.mult))
                    for h in range(B_HEADS):
                        rows = slice(ROPE_DIM * h, ROPE_DIM * h + ROPE_DIM)
                        ins = dve.tensor_tensor(per_pattern(qk_b[st.dst][st.p][0:ROPE_DIM, h, :], st.p), natural(pack[rows, :], st.p),
                                                natural(turned[rows, :], st.p), ALU.add)
                    ins.then_inc(roped, 1)
                elif k == "bt_qk":
                    if st.p == 0:
                        for i, b_n, c0, _ in BAND_PLACES:
                            b, w = st.banks[b_n], P * len([1 for q_, _ in BAND if q_ == i])
                            dve.wait_ge(bank_done[b], at(st.fill[b_n], turn, 1))
                            m0 = P if i == 0 else 0
                            rows = psum[:, b, c0:c0 + w]
                            then(dve.tensor_tensor(rows, rows, band[:, m0:m0 + w], ALU.add))
                            ins = dve.tensor_reduce(mden[:, st.p, i, st.h, 0:1], rows, AX.X, ALU.max, negate=True)
                    else:
                        b = st.banks[0]
                        dve.wait_ge(bank_done[b], at(st.fill[0], turn, 1))
                        v = psum[:, b, :].rearrange("q (t k) -> q t k", t=TT)
                        mask = band[:, P:2 * P] if st.p == 1 else own[:]
                        then(dve.tensor_tensor(v, v, over(mask, TT), ALU.add))
                        ins = dve.tensor_reduce(mden[:, st.p, :, st.h, 0], v, AX.X, ALU.max, negate=True)
                    then(ins)
                    dve.tensor_scalar(nbias[:, st.h, :], mden[:, st.p, :, st.h, 0], B_DIM ** -0.5, None, ALU.mult).then_inc(smax, 1)
                elif k == "joint":
                    dve.wait_ge(nat_in, 16)
                    low, d_ = nat[:, :, :, :, 0], nat[:, :, :, :, 1]
                    then(dve.tensor_tensor(least[:], low[:, 0], low[:, 1], ALU.min))
                    then(dve.tensor_tensor(least[:], least[:], low[:, 2], ALU.min))
                    for p in range(PATTERNS):
                        ins = dve.tensor_tensor(ex[:, p], least[:], low[:, p], ALU.subtract)
                    ins.then_inc(joint_diff, 1)
                    dve.wait_ge(joint_exp, 1)
                    for p in range(PATTERNS):
                        ins = dve.tensor_tensor(zd[:, p], ex[:, p], d_[:, p], ALU.mult)
                    then(ins)
                    then(dve.tensor_tensor(zd[:, 0], zd[:, 0], zd[:, 1], ALU.add))
                    then(dve.tensor_tensor(zd[:, 0], zd[:, 0], zd[:, 2], ALU.add))
                    then(dve.reciprocal(zd[:, 0], zd[:, 0]))
                    for p in range(PATTERNS):
                        ins = dve.tensor_tensor(share[:, p], ex[:, p], zd[:, 0], ALU.mult)
                    ins.then_inc(share_made, 1)
                elif k == "ybsum":
                    for p in range(PATTERNS):
                        dve.wait_ge(wide_in[p], 16)
                        if p == 0:
                            wait_ready(dve, st.ready, turn)
                        then(dve.tensor_tensor(u_b[p][:], u_b[p][:], wide[p][:].rearrange("q t h -> q h t"), ALU.mult))
                    then(dve.tensor_tensor(u_b[0][:], u_b[0][:], u_b[1][:], ALU.add))
                    dve.tensor_tensor(u_b[0][:], u_b[0][:], u_b[2][:], ALU.add).then_inc(yb_sum, 1)
                elif k == "lnv":
                    for tt in range(TT):
                        wait_ready(dve, st.ready[tt:tt + 1], turn)
                        ins = dve.bn_stats(vstat[:, tt, :], vt[:, tt, :])
                    then(ins)
                    for tt in range(TT):
                        ins = dve.bn_aggr(vmean[:, tt, :], vstat[:, tt, :])
                    ins.then_inc(vn_stats, 1)
                    dve.wait_ge(rstd_made, at(st.rstd, turn, 1))
                    dve.wait_ge(row_in, 16 * st.row_n)
                    for tt in range(TT):
                        then(dve.tensor_scalar(vt[:, tt, :], vt[:, tt, :], vmean[:, tt, 0:1], rstd[:, tt:tt + 1], ALU.subtract, ALU.mult))
                        then(dve.tensor_tensor(vt[:, tt, :], vt[:, tt, :], row[:, 0:512], ALU.mult))
                        dve.tensor_tensor(vt[:, tt, :], vt[:, tt, :], row[:, 512:1024], ALU.add).then_inc(vn_made, 1)
                elif k == "spatial":
                    for g in range(4):
                        b = SIDE[g]
                        dve.wait_ge(bank_done[b], at(st.fill[g], turn, 1))
                        v = ya_sum[:, g % 2, :]
                        then(dve.tensor_tensor(v.rearrange("q (c t) -> q c t", c=TT), psum[:, b, :].rearrange("q (c t) -> q c t", c=TT),
                                               over(bs_row[:, g, :], TT), ALU.add))
                        dve.tensor_tensor(v, v, ut[:, g, :], ALU.mult).then_inc(merged, 1)
                        dve.wait_ge(merged, at(st.merged, turn, g + 1))
                        dve.wait_ge(hi_made, at(st.hi, turn, g + 1))
                        dve.tensor_tensor(mid_lo[0][:, g, :], v, mid_hi[0][:, g, :], ALU.subtract).then_inc(bank_free[b], 1)
                elif k == "ybsplit":
                    dve.wait_ge(hi_made, at(st.hi, turn, 1))
                    dve.tensor_tensor(mid_lo[1][:], u_b[0][:], mid_hi[1][:], ALU.subtract).then_inc(yb_split, 1)
                elif k == "clear":
                    wait_ready(dve, st.ready, turn)
                    dve.memset(y[:], 0.0).then_inc(y_clear, 1)
                    dve.wait_ge(y_clear, 1)

            dve.wait_ge(cols_in, 32)
            walk(dve, handle)

        @block.gpsimd
        def _(pool):
            pool.memset(eps[:], EPS).then_inc(pad_made, 1)
            pool.memset(a_own[:], 0.0).then_inc(own_clear, 1)
            pool.memset(g_hi[:].bitcast(F32), 0.0).then_inc(pad_made, 1)
            pool.memset(g_lo[:].bitcast(F32), 0.0).then_inc(pad_made, 1)
            pool.dma_start(g_raw[:], a["w_glr"]).then_inc(glr_in, 16)
            pool.dma_start(w_gu[:], a["w_gate_up"]).then_inc(const_in, 16)
            pool.dma_start(lvl_mask[:], a["lvl_mask"]).then_inc(const_in, 16)

            def load_row(parts):
                for name, c0, n in parts:
                    pool.dma_start(row[:, c0:c0 + n], a[name].partition_broadcast(P)).then_inc(row_in, 16)

            pool.dma_start(table[0:RP_BUCKETS, :], a["table"]).then_inc(table_in, 16)
            pool.dma_start(bucket[0:RP_BUCKETS, :], a["bucket"]).then_inc(table_in, 16)
            load_row([("norm_final", 0, D)])

            def handle(st, turn):
                k = st.kind
                if k == "gate":
                    pool.wait_ge(cum_made, 2)
                    for n in range(2):
                        level(n, st)
                elif k == "relbias":
                    pool.wait_ge(bias_made, 1)
                    pool.wait_ge(bank_free[4], at(st.fill[0], turn, 1))
                    pool.dma_start(bias_dram, bias_row[0:A_HEADS, :]).then_inc(bias_out, 16)
                    pool.wait_ge(bias_out, 16)
                    pool.wait_ge(xn_made, TT)
                    toeplitz = bass.AP(tensor=bias_dram.tensor, offset=0, ap=[[1, P], [REL, A_HEADS], [1, NEAR]])
                    pool.dma_start(near_back[:], toeplitz).then_inc(near_in, 16)
                elif k == "level":
                    if st.n + 2 < len(LEVELS):
                        level(st.n + 2, st)
                elif k == "glaout":
                    wait_ready(pool, [(b, st.fill[n], 1) for n, b in enumerate(SIDE)], turn)
                    pool.dma_start(mem[:], a["mem"].rearrange("(t p) d -> p t d", p=P)).then_inc(mem_in, 16)
                elif k == "reload":
                    wait_ready(pool, st.ready, turn)
                    pool.dma_start(x[:], a["x"].rearrange("(t p) d -> p t d", p=P)).then_inc(x_back, 16)
                elif k == "load2":
                    wait_ready(pool, st.ready, turn)
                    pool.dma_start(cosine[:], a["cosine"]).then_inc(b2_in, 16)
                    pool.dma_start(sine[:], a["sine"]).then_inc(b2_in, 16)
                    pool.dma_start(band[:], a["band"]).then_inc(b2_in, 16)
                    pool.dma_start(own[:], a["own"]).then_inc(b2_in, 16)
                    pool.dma_start(ws_t[:], a["w_spatial_t"]).then_inc(ws_in, 16)
                    pool.dma_start(bs_row[:].rearrange("q g t -> q (g t)"), a["b_spatial_2"].partition_broadcast(P)).then_inc(ws_in, 16)
                elif k == "rows":
                    pool.wait_ge(x_rows, at(st.xrows, turn, TT))
                    if st.row == "norm_final":
                        load_row([("ln_v_gain_2", 0, 512), ("ln_v_bias_2", 512, 512)])
                    elif st.row == "norm_mix_post_2":
                        load_row([("norm_mlp_post_2", 0, D)])
                elif k == "spatial":
                    pool.wait_ge(vn_made, TT)
                    load_row([("norm_mix_post_2", 0, D)])
                elif k == "stats":
                    wait_ready(pool, st.ready, turn)
                    src, dst = mden[:, st.p].rearrange("q t h s -> q t (h s)"), stat_dram[st.p]
                    if st.p == 0:
                        pool.dma_start(dst.rearrange("(t q) v -> q t v", t=TT), src).then_inc(stat_out, 16)
                    else:
                        pool.dma_start(dst.rearrange("(m r) v -> m r v", r=4), src).then_inc(stat_out, 16)
                elif k == "joint":
                    pool.wait_ge(stat_out, 16 * PATTERNS)
                    pool.dma_start(nat[:].rearrange("q p t h s -> q p (t h s)"), stat_dram.rearrange("p (q t) v -> q p (t v)", t=TT)).then_inc(nat_in, 16)
                    pool.wait_ge(share_made, 1)
                    pool.dma_start(share_dram.rearrange("p (q v) -> q p v", q=P), share[:].rearrange("q p t h -> q p (t h)")).then_inc(share_out, 16)
                    pool.wait_ge(share_out, 16)
                    wait_ready(pool, st.ready, turn)
                    for p in range(PATTERNS):
                        pool.dma_start(wide[p][:].rearrange("q t h -> q (t h)"), share_dram[p].partition_broadcast(P)).then_inc(wide_in[p], 16)

            def level(n, st):
                size = LEVELS[n]
                view = lambda ap: ap.rearrange("q c (b s l) -> q (c b) s l", s=2, l=size)
                c_, e_, l_ = view(cum[:]), view(ex_g[:]), view(lev[n % 2][:])
                q_, k_ = view(qk_g[:, 0:2, :]), view(qk_g[:, 2:4, :])
                ref = c_[:, :, 0, size - 1:size].broadcast_to([P, 2 * T // (2 * size), size])
                wait(pool, lev_made, n)
                if n == 0:
                    wait_ready(pool, st.qk_ready, None)
                pool.tensor_tensor(e_[:, :, 0, :], ref, c_[:, :, 0, :], ALU.subtract).then_inc(lev_diff, 1)
                pool.tensor_tensor(e_[:, :, 1, :], c_[:, :, 1, :], ref, ALU.subtract).then_inc(lev_diff, 1)
                if n >= 2:
                    for tt in range(TT):
                        pool.wait_ge(bank_done[SIDE[tt]], at(s.levels[n - 2].fill[tt], None, 1))
                pool.wait_ge(lev_exp, n + 1)
                half = pool.tensor_tensor(l_[:, :, 0, :], k_[:, :, 0, :], e_[:, :, 0, :], ALU.mult)
                half.then_inc(pool_step, 1)
                pool.tensor_tensor(l_[:, :, 1, :], q_[:, :, 1, :], e_[:, :, 1, :], ALU.mult).then_inc(lev_made, 1)

            for item in s.items:
                if not isinstance(item, tuple):
                    handle(item, None)



def rel_bucket(d):
    exact = RP_BUCKETS // 2
    large = exact + (np.log(np.maximum(d, 1).astype(np.float32) / np.float32(exact))
                     / np.float32(math.log(RP_MAX_DIST / exact)) * np.float32(RP_BUCKETS - exact)).astype(np.int32)
    return np.where(d < exact, np.maximum(d, 0), np.minimum(large, RP_BUCKETS - 1))


def shape_constants():
    u = np.arange(REL)
    d = NEAR - 1 - u
    bucket = np.zeros((RP_BUCKETS, REL), np.float32)
    bucket[rel_bucket(d[d >= 0]), u[d >= 0]] += 1.0
    bucket[RP_BUCKETS - 1, u[d >= 0]] -= 1.0
    j, i = np.arange(P)[:, None], np.arange(P)[None, :]
    lvl = [(j // (2 * n) == i // (2 * n)) & (j % (2 * n) < n) & (i % (2 * n) >= n) for n in LEVELS] + [j == i]
    half = ROPE_DIM // 2
    inv = ROPE_THETA ** (-np.arange(0, ROPE_DIM, 2, dtype=np.float32) / np.float32(ROPE_DIM))
    ang = np.arange(T, dtype=np.float32)[None, :] * inv.astype(np.float32)[:, None]
    cos, sin = np.cos(ang), np.sin(ang)
    q, k = np.arange(P)[:, None], np.arange(3 * P)[None, :] - P
    return {
        "ident": np.eye(P, dtype=np.float32),
        "mirror": np.eye(P, dtype=np.float32)[::-1],
        "bucket": bucket,
        "lvl_mask": np.stack(lvl, 1).astype(np.int32),
        "cosine": np.tile(np.concatenate([cos, cos]), (B_HEADS, 1)).astype(np.float32),
        "sine": np.tile(np.concatenate([-sin, sin]), (B_HEADS, 1)).astype(np.float32),
        "band": np.where(np.abs(q - k) <= RADIUS, 0.0, MASKED).astype(np.float32),
        "own": np.where(j % 4 == i % 4, 0.0, MASKED).astype(np.float32),
    }


def lay_out(inputs):
    a = dict(shape_constants())
    a["x"] = np.ascontiguousarray(inputs["x"][0])
    a["mem"] = np.ascontiguousarray(inputs["mem"][0])
    tiles = []
    for name, r0, rows, c0, n in GROUPS:
        w = inputs[name][0][r0:r0 + rows, c0:c0 + n]
        if n == 512:
            w = w.reshape(4, 2, P, 512).transpose(0, 2, 1, 3)
        else:
            w = w.reshape(2, 2, P, 2, 512).transpose(3, 0, 2, 1, 4)
        tiles.append(w.reshape(4, P, WORDS))
    a["weights"] = np.concatenate(tiles)
    a["cols"] = np.concatenate([inputs[n].reshape(-1, P) for n in COLS]).T.copy()
    a["w_glr"] = inputs["w_in"][0][:, W_IN["glr"]:W_IN["glr"] + G_RANK].reshape(KC, P, G_RANK).transpose(1, 0, 2).copy()
    a["w_gate_up"] = inputs["w_gate_up"][0]
    a["table"] = inputs["rp_table"]
    a["w_spatial_t"] = inputs["w_spatial_2"][0].transpose(2, 0, 1).copy()
    a["b_spatial_2"] = inputs["b_spatial_2"].reshape(-1)
    for n in ("norm_final", "ln_v_gain_2", "ln_v_bias_2", "norm_mix_post_2", "norm_mlp_post_2"):
        a[n] = inputs[n].reshape(-1)
    return {n: np.ascontiguousarray(v) for n, v in a.items()}


def kernel(**inputs):
    import concourse.bacc as bacc
    from concourse.bass_utils import run_bass_kernel_spmd

    nc = bacc.Bacc("TRN2", target_bir_lowering=False, num_devices=1)
    arrays = lay_out({n: np.asarray(v) for n, v in inputs.items()})
    aps = {n: nc.dram_tensor(f"in_{n}", v.shape, mybir.dt.from_np(v.dtype), kind="ExternalInput").ap()
           for n, v in arrays.items()}
    out = nc.dram_tensor("out", (T, D), F32, kind="ExternalOutput").ap()
    two_blocks(nc, aps, out)
    r = run_bass_kernel_spmd(nc, [{f"in_{n}": v for n, v in arrays.items()}], core_ids=[0])
    return r.results[0]["out"].reshape(1, T, D)
```

```python
import math
from contextlib import ExitStack
from itertools import chain

import numpy as np

import concourse.bass as bass
from concourse import mybir

F32 = mybir.dt.float32
F32R = mybir.dt.float32r
I32 = mybir.dt.int32
ACT = mybir.ActivationFunctionType
ALU = mybir.AluOpType
AX = mybir.AxisListType

P = 128
T = 512
TT = T // P
D = 1024
KC = D // P
M = 256
MT = M // P
A_HEADS, A_DIM = 8, 64
G_HEADS, G_DK, G_DV, G_RANK = 4, 64, 128, 16
G_NORM = 16.0
X_HEADS, X_DIM = 4, 256
FF = 4096
CHUNKS = FF // T
B_HEADS, B_DIM = 4, 128
PATTERNS = 3
RADIUS = 64
ROPE_DIM = 32
ROPE_THETA = 500000.0
EPS = 1e-6
MASKED = -1e30
RP_BUCKETS, RP_MAX_DIST = 32, 128
LEVELS = (64, 32, 16, 8, 4, 2, 1)
WORDS = 1024
NEAR = 2 * P
REL = 3 * P

COLS = {}
_at = 0
for _name, _n in (("norm_mix", KC), ("norm_xattn", KC), ("norm_mem", KC), ("norm_mlp", KC),
                  ("norm_mix_pre_2", KC), ("norm_mlp_pre_2", KC), ("b_gate_2", 2 * KC), ("g_norm", 1),
                  ("b_gate", 2)):
    COLS[_name] = _at
    _at += _n
NCOLS = _at



W_IN = dict(qa=0, ka=512, va=1024, glaqk=1536, vg=2048, glr=2560, rg=2576)


def mlp_order():
    return ([("up", 0)] + [x for c in range(0, CHUNKS - 2, 2)
                           for x in (("up", c + 1), ("down", c), ("up", c + 2), ("down", c + 1))]
            + [("up", CHUNKS - 1), ("down", CHUNKS - 2), ("down", CHUNKS - 1)])


def stream_groups():
    out = [("w_in", 0, D, W_IN[n], 512) for n in ("glaqk", "vg", "rg", "qa", "ka", "va")]
    out += [("w_xkv", 0, D, 512 * n, 512) for n in range(4)]
    out += [("w_out", 0, D, 512 * n, 512) for n in range(2)]
    out += [("w_xq", 0, D, 512 * n, 512) for n in range(2)]
    out += [("w_xo", 0, D, 512 * n, 512) for n in range(2)]
    mlp = lambda up, down: [(up, 0, D, 512 * c, 512) if kind == "up" else (down, 512 * c, 512, 0, D)
                            for kind, c in mlp_order()]
    out += mlp("w_up", "w_down")
    width = B_HEADS * B_DIM
    for p in range(PATTERNS):
        out += [("w_in_2", 0, D, 1024 + (PATTERNS * n + p) * width, 512) for n in range(3)]
    out += [("w_in_2", 0, D, 512 * n, 512) for n in (1, 0)]
    out += [("w_in_2", 0, D, 1024 + 3 * PATTERNS * width + 512 * n, 512) for n in range(4)]
    out += [("w_branch_a_2", 0, 512, 0, D), ("w_branch_b_2", 0, 512, 0, D)]
    out += [("w_out_2", 0, D, 512 * n, 512) for n in range(2)]
    out += mlp("w_up_2", "w_down_2")
    return out


GROUPS = stream_groups()
TILES = 4 * len(GROUPS)
RAW = 2



class Step:

    def __init__(self, kind, banks, fill, *, n=0, h=0, p=None, out=None, major=None, src=None, dst=None, rows=KC,
                 half=0, first=False, splits=(), tile=None, slots_free=None, ready=None, bank=0, blk=0, mid=None,
                 after=None, tiles=TT, gains=(), chunks=(), row=None, row_n=0, qk_ready=None,
                 of=None, roped=None, packed=None, rstd=None, xn=None, hi=None, xrows=None, smax=None, merged=None, relu=None):
        self.kind, self.banks, self.fill = kind, banks, fill
        self.n, self.h, self.p = n, h, p
        self.out, self.major, self.src, self.dst = out, major, src, dst
        self.rows, self.half, self.bank, self.blk, self.mid = rows, half, bank, blk, mid
        self.first, self.splits, self.tile, self.slots_free = first, splits, tile, slots_free
        self.ready, self.qk_ready, self.after = ready, qk_ready, after
        self.tiles, self.gains, self.chunks, self.row, self.row_n = tiles, gains, chunks, row, row_n
        self.of = of
        self.roped, self.packed, self.rstd, self.xn, self.hi, self.xrows, self.smax, self.merged, self.relu = (
            roped, packed, rstd, xn, hi, xrows, smax, merged, relu)


class Schedule:

    def __init__(self):
        self.items, self.body, self.open = [], None, []
        self.fills, self.counts = [0] * 8, {}
        self.group = 0
        self.last_bank = None

    def fill(self, bank):
        c = [self.fills[bank], 0]
        self.fills[bank] += 1
        if self.body is not None:
            self.open.append((c, ("bank", bank)))
        return c

    def fills_of(self, bank):
        c = [self.fills[bank], 0]
        if self.body is not None:
            self.open.append((c, ("bank", bank)))
        return c

    def count(self, name, n):
        c = [self.counts.get(name, 0), 0]
        self.counts[name] = c[0] + n
        if self.body is not None:
            self.open.append((c, ("count", name)))
        return c

    def add(self, kind, banks=(), counts=(), **more):
        fields = dict(more)
        for name, n in dict(counts).items():
            fields[name] = self.count(name, n)
        st = Step(kind, list(banks), [self.fill(b) for b in banks], **fields)
        (self.items if self.body is None else self.body).append(st)
        return st

    def begin_loop(self, turns):
        self.turns, self.body, self.open = turns, [], []
        self.before = (list(self.fills), dict(self.counts), self.group)

    def end_loop(self):
        fills, counts, group = self.before
        growth = {("bank", b): self.fills[b] - fills[b] for b in range(8)}
        growth |= {("count", n): v - counts.get(n, 0) for n, v in self.counts.items()}
        growth["tile"] = 4 * (self.group - group)
        for c, key in self.open:
            c[1] = growth[key]
        more = self.turns - 1
        for b in range(8):
            self.fills[b] += more * growth["bank", b]
        for n in self.counts:
            self.counts[n] += more * growth["count", n]
        self.group += more * (self.group - group)
        self.items.append((self.turns, self.body))
        self.body, self.open = None, []

    def gemm(self, *args, **more):
        for _ in self.bank_steps(*args, **more):
            pass

    def bank_steps(self, out, major, src, rows=KC, banks=4, halves=1, ready=None, blk=0, mid=None, dst=None, p=None,
             after=None):
        g = self.group
        self.group += 1
        steps = halves * banks
        free_bank = self.last_bank
        slots_free = None if g == 0 else (free_bank, self.fills_of(free_bank))
        for i in range(steps):
            half, b = divmod(i, banks)
            splits = [4 * (g + 1) + j for j in range(4) if j * steps // 4 == i and g + 1 < len(GROUPS)]
            tiles = []
            for t in splits + [4 * g]:
                c = [t, 0]
                if self.body is not None:
                    self.open.append((c, "tile"))
                tiles.append(c)
            counts = {"up": {"hi": 1, "relu": 1}, "merge": {"hi": 1, "merged": 1}, "rope": {"packed": 1}}.get(out, {})
            st = self.add("gemm", [b], counts, out=out, major=major, src=src, rows=rows, half=half,
                          first=(b == 0), splits=tiles[:-1], tile=tiles[-1], slots_free=slots_free,
                          ready=ready if i == 0 else None, bank=b, blk=blk, mid=mid, dst=dst, p=p, after=after)
            if i == steps - 1:
                self.last_bank = banks - 1
            yield st


def at(count, turn, plus=0):
    value, growth = count
    if turn is None or growth == 0:
        return value + plus
    assert value + plus > 0
    return turn * growth + (value + plus)


SIDE = (4, 5, 6, 7)
CAUSAL = [(i, k) for i in range(TT) for k in range(i + 1)]
BAND = [(i, k) for i in range(TT) for k in range(max(0, i - 1), min(TT, i + 2))]
OWN = [(i, i) for i in range(TT)]
ROW_PLACES = [(3, 0, 0, True), (2, 1, 0, False), (0, 1, 3 * P, True), (1, 2, 0, True)]
BAND_PLACES = [(1, 0, 0, True), (2, 1, 0, True), (0, 2, 0, False), (3, 2, 2 * P, True)]
PAIRS = [(j, i) for i in range(TT) for j in range(i)]



def make_schedule():
    s = Schedule()
    s.applied = [None] * TT

    def go(steps, n):
        for _ in range(n):
            next(steps, None)

    def scale_rms(src, tt, at_):
        if at_ == "evac":
            at_ = ready()
        return s.add("scale_rms", src=src, n=tt, ready=at_, after=s.applied[tt] if at_ == "rows" else None)

    def scale_by(src, tt):
        st = s.add("scale", counts={"rstd": 1, "xn": 1}, src=src, n=tt)
        if tt == 0:
            s.scaled = st.xn

    def scale(src, tt, at_):
        scale_rms(src, tt, at_)
        scale_by(src, tt)

    def transposed(tiles, gains, dst, src):
        chunks = [4, 5, 6, 7, 0, 1, 2, 3] if src == "mix" else list(range(KC))
        st = s.add("turn", range(KC), {"hi": KC}, tiles=tiles, gains=gains, dst=dst, src=src, chunks=chunks,
                   ready=all_out() if src == "mix" else None)
        return [(chunks.index(c), st.fill[chunks.index(c)], 1) for c in range(KC)]

    def norm(gain, dst, tiles=TT):
        return transposed(tiles, [gain] * KC, dst, s.scaled)

    def rows_rms(name, src, tt):
        s.add("rows_rms", ready=ready(), row=name, src=src, n=tt)

    def rows_by(name, src, tt, row_n):
        st = s.add("rows", counts={"rstd": 1, "xrows": 1}, row=name, src=src, n=tt, row_n=row_n)
        s.applied[tt] = st.xrows

    def tile_by_tile(steps, work):
        for tt in range(TT):
            go(steps, 1)
            work(tt)

    def ready():
        return [(b, s.fills_of(b), 0) for b in range(4)]

    def all_out():
        return [(b, s.fills_of(b), 0) for b in range(8)]

    def filled_by(st):
        return [(b, f, 1) for b, f in zip(st.banks, st.fill)]

    def run_mlp(dst, act_ready, work):
        def up(act_ready, c):
            s.gemm("up", "T", "act", ready=act_ready, mid=c % 2)

        def down(mid_ready, c):
            s.gemm("add", "tok", "mid", rows=4, halves=2, ready=mid_ready, mid=c % 2, dst=dst)

        up(act_ready, 0)
        s.begin_loop((CHUNKS - 2) // 2)
        even = ready()
        up(None, 1)
        odd = ready()
        down(even, 0)
        up(None, 2)
        down(odd, 1)
        s.end_loop()
        even = ready()
        up(None, 1)
        odd = ready()
        down(even, 0)
        steps = s.bank_steps("add", "tok", "mid", rows=4, halves=2, ready=odd, mid=1, dst=dst)
        go(steps, TT)
        tile_by_tile(steps, work)

    for tt in range(TT):
        scale("x", tt, "x")
    s.add("start", n=0)
    act_ready = norm("norm_mix", "act")
    s.add("start", n=1)
    steps = s.bank_steps("glaqk", "T", "act", ready=act_ready)
    go(steps, 1)
    s.add("relbias", (4,))
    go(steps, 4)
    qk_ready = ready()
    s.glr = s.add("glr", (4,))
    s.add("gate", (5, 6), qk_ready=qk_ready)
    s.gemm("vg", "tok", "act")
    near_ready = filled_by(s.add("flip", SIDE))
    steps = chain(s.bank_steps("rg", "tok", "act"), s.bank_steps("qa", "T", "act"), s.bank_steps("ka", "T", "act"),
                  s.bank_steps("va", "tok", "act"))
    last = len(LEVELS)
    s.levels = {last: s.add("level", SIDE, n=last, qk_ready=qk_ready)}
    for n in range(last):
        go(steps, 1 if n in (0, last - 1) else 2)
        s.levels[n] = s.add("level", SIDE[n % 2 * 2:n % 2 * 2 + 2], n=n, ready=all_out())
        if n == 0:
            s.add("farprep")
        if n == last - 2:
            s.add("farmid")
    go(steps, 1)
    s.add("far", [SIDE[n % 4] for n in range(len(PAIRS))])
    go(steps, 1)
    s.add("glaout", SIDE)
    go(steps, 1)
    qk = [s.add("sa_qk", (0, 1, 2), {"smax": 4}, h=0, ready=near_ready + ready())]
    go(steps, 16)
    qk.append(s.add("sa_qk", (4, 5, 6), {"smax": 4}, h=1))
    t = [s.add("sa_t", qk[h].banks, h=h, ready=filled_by(qk[h])) for h in range(2)]
    for tt in range(MT):
        scale("mem", tt, "mem")
    for h in range(2):
        s.add("sa_pv", ((7, 3)[h],), h=h, ready=filled_by(t[h]))
    mem_ready = norm("norm_mem", "memT", MT)
    steps = chain(s.bank_steps("kx", "T", "memT", ready=mem_ready, blk=0), s.bank_steps("kx", "T", "memT", blk=1),
                  s.bank_steps("vx", "tok", "memT", banks=2, blk=0), s.bank_steps("vx", "tok", "memT", banks=2, blk=1))
    for h in range(2, A_HEADS):
        qk = s.add("sa_qk", (4, 5, 6), {"smax": 4}, h=h)
        go(steps, 1)
        t = s.add("sa_t", (4, 5, 6), h=h, ready=filled_by(qk))
        go(steps, 1)
        s.add("sa_pv", (7,), h=h, ready=filled_by(t))
    go(steps, 16)
    s.add("reload", ready=ready())
    mix_ready = transposed(TT, [None] * 4 + ["g_norm"] * 4, "mid", "mix")
    s.gemm("add", "tok", "mid", ready=mix_ready, dst="x", blk=0, after="x_back")
    tile_by_tile(s.bank_steps("add", "tok", "mid", dst="x", blk=1), lambda tt: scale("x", tt, "evac"))
    act_ready = norm("norm_xattn", "act")
    s.gemm("qx", "T", "act", ready=act_ready, blk=0)
    half_done = ready()
    steps = s.bank_steps("qx", "T", "act", blk=1)
    s.add("ca_qk", (4, 5), {"smax": 1}, h=0, ready=half_done)
    go(steps, 1)
    t = [s.add("ca_t", (6, 7), h=0)]
    go(steps, 1)
    pv = [s.add("ca_pv", (4, 5), {"hi": 2}, h=0, ready=filled_by(t[0]))]
    s.add("ca_qk", (6, 7), {"smax": 1}, h=1)
    go(steps, 1)
    t.append(s.add("ca_t", (4, 5), h=1))
    s.add("ca_qk", (6, 7), {"smax": 1}, h=2, ready=ready()[0:2])
    go(steps, 1)
    s.add("ca_qk", (2, 3), {"smax": 1}, h=3, ready=ready()[2:4])
    t.append(s.add("ca_t", (0, 1), h=2))
    pv.append(s.add("ca_pv", (4, 5), {"hi": 2}, h=1, ready=filled_by(t[1])))
    pv.append(s.add("ca_pv", (6, 7), {"hi": 2}, h=2, ready=filled_by(t[2])))
    t.append(s.add("ca_t", (0, 1), h=3))
    pv.append(s.add("ca_pv", (4, 5), {"hi": 2}, h=3, ready=filled_by(t[3])))
    ox_ready = [r for st in pv for r in filled_by(st)]
    s.add("load2", ready=all_out())
    s.gemm("add", "tok", "mid", ready=ox_ready, dst="x", blk=0)
    tile_by_tile(s.bank_steps("add", "tok", "mid", dst="x", blk=1), lambda tt: scale("x", tt, "evac"))
    act_ready = norm("norm_mlp", "act")

    def block_end(tt):
        if tt < TT:
            rows_rms("norm_final", "x", tt)
        if tt >= 1:
            rows_by("norm_final", "x", tt - 1, 1)
        if tt >= 2:
            scale_by("x", tt - 2)
        if tt >= 1:
            scale_rms("x", tt - 1, "rows")
        if tt == TT:
            scale_by("x", TT - 1)

    run_mlp("x", act_ready, block_end)
    block_end(TT)
    act_ready = norm("norm_mix_pre_2", "act")
    roped = [None]

    def project(p, ready=None):
        for dst in ("q", "k"):
            yield from s.bank_steps("rope", "T", "act", ready=ready if dst == "q" else None, dst=dst, p=p, after=roped[0])
            roped[0] = s.add("rope", counts={"roped": 1, "packed": 0}, dst=dst, p=p).roped

    go(project(0, act_ready), 16)
    for p in range(PATTERNS):
        s.gemm("v2", "tok", "act", p=p)
        v_ready, mine = ready(), roped[0]
        qk_banks = lambda h: (4, 5, 6) if p == 0 else (4 + h % 2,)
        t_banks = (4, 5, 6) if p == 0 else (6,)
        steps = project(p + 1) if p + 1 < PATTERNS else s.bank_steps("v", "tok", "act")
        qk = s.add("bt_qk", qk_banks(0), {"smax": 1}, h=0, p=p, roped=mine)
        for h in range(B_HEADS):
            go(steps, 1)
            t = s.add("bt_t", t_banks, h=h, p=p, ready=filled_by(qk))
            early = p > 0 and h + 1 < B_HEADS
            if early:
                qk = s.add("bt_qk", qk_banks(h + 1), {"smax": 1}, h=h + 1, p=p, roped=mine)
            if p + 1 < PATTERNS:
                go(steps, 1)
            s.add("bt_pv", (7,), h=h, p=p, ready=filled_by(t) + (v_ready if h == 0 else []))
            if not early and h + 1 < B_HEADS:
                qk = s.add("bt_qk", qk_banks(h + 1), {"smax": 1}, h=h + 1, p=p, roped=mine)
        go(steps, 16)
        s.add("stats", p=p, ready=all_out())
    attended, v_done = all_out(), ready()
    steps = s.bank_steps("u", "T", "act")
    go(steps, 1)
    s.add("joint", ready=attended)
    s.add("lnv", counts={"rstd": 1}, ready=v_done, row_n=3)
    go(steps, 16)
    ya = s.add("spatial", SIDE)
    s.add("ybsum", ready=attended)
    steps = s.bank_steps("gate", "T", "act", blk=0)
    go(steps, 4)
    steps = s.bank_steps("gate", "T", "act", blk=1)
    for g in range(4):
        go(steps, 1)
        s.add("ya", counts={"hi": 1, "merged": 1}, n=g, of=ya)
    go(steps, 4)
    s.add("ybsplit", counts={"hi": 1}, ready=filled_by(ya))
    for n in range(2, 4):
        s.gemm("gate", "T", "act", blk=n)
    s.gemm("bra", "T", "mid", rows=4, halves=2, mid=0, ready=filled_by(ya))
    s.gemm("merge", "T", "mid", rows=4, halves=2, mid=1, after="yb")
    merged_ready = [(b, count, half - 1) for half in range(2) for b, count, _ in ready()]
    s.gemm("copy", "tok", "act", ready=merged_ready, dst="y", blk=0)

    def mixed(tt):
        if tt < TT:
            rows_rms("norm_mix_post_2", "y", tt)
            rows_by("norm_mix_post_2", "y", tt, 4)
        if tt >= 1:
            scale_rms("x", tt - 1, "rows")
            scale_by("x", tt - 1)

    tile_by_tile(s.bank_steps("copy", "tok", "act", dst="y", blk=1), mixed)
    mixed(TT)
    act_ready = norm("norm_mlp_pre_2", "act")
    s.add("clear", ready=all_out())

    def end(tt):
        if tt < TT:
            rows_rms("norm_mlp_post_2", "y", tt)
        if tt >= 1:
            rows_by("norm_mlp_post_2", "y", tt - 1, 5)

    run_mlp("y", act_ready, end)
    end(TT)
    return s



def two_blocks(nc, a, out):
    s = make_schedule()
    with ExitStack() as ctx:
        def sem(name):
            return ctx.enter_context(nc.semaphore(name))

        slab_bytes = 212800
        base = -(-nc.sbuf_base // 64) * 64
        ctx.enter_context(nc.sbuf_tensor("slab", [P, slab_bytes], mybir.dt.uint8, align_bytes=64))
        top = [0]
        KB = 1024
        region = {}
        for name, size in (("x", 16 * KB), ("raw", 8 * KB), ("whi", 32 * KB), ("wlo", 32 * KB), ("act", 32 * KB),
                           ("mid", 32 * KB), ("y", 16 * KB), ("v", 8 * KB), ("u", 8 * KB), ("const", 23 * KB)):
            region[name] = top[0]
            top[0] += size
        assert top[0] <= slab_bytes, top[0]

        def place(name, where, shape, dtype=F32, skip=0):
            return nc.alloc_sbuf_tensor_at(name, [P] + shape, dtype, offset=base + region[where] + skip)

        x = place("x_tok", "x", [TT, D])
        w_raw = place("w_raw", "raw", [RAW, WORDS])
        w_first = place("w_first", "mid", [4, WORDS])
        w_hi = place("w_hi", "whi", [8, WORDS], F32R)
        w_lo = place("w_lo", "wlo", [8, WORDS], F32R)
        act_hi = place("act_hi", "act", [KC, T], F32R)
        act_lo = place("act_lo", "act", [KC, T], F32R, 16 * KB)
        mid_hi = [place(f"mid_hi{n}", "mid", [4, T], F32R, 16 * KB * n) for n in range(2)]
        mid_lo = [place(f"mid_lo{n}", "mid", [4, T], F32R, 16 * KB * n + 8 * KB) for n in range(2)]
        y = place("y_tok", "y", [TT, D])

        cat = [0]

        def const(name, shape, dtype=F32, rows=P):
            n = int(np.prod(shape)) * 4
            t = nc.alloc_sbuf_tensor_at(name, [rows] + shape, dtype, offset=base + region["const"] + cat[0])
            cat[0] += -(-n // 32) * 32
            assert cat[0] <= 23 * KB, (name, cat[0])
            return t

        ident = const("ident", [P])
        cols = const("cols", [NCOLS])
        row = const("row", [D])
        eps = const("eps", [1])
        sumsq = const("sumsq", [16])
        lnv = const("lnv", [16])
        rstd = const("rstd", [16])
        phase = cat[0]
        lvl_mask = const("lvl_mask", [len(LEVELS) + 1, P], I32)
        w_gu = const("w_gu", [G_HEADS * G_DK], rows=G_RANK)
        glr_t = const("glr_t", [T], rows=G_RANK)
        near = const("near", [A_HEADS, NEAR])
        bucket = place("bucket", "const", [REL], skip=cat[0] - 8 * KB)
        table = place("table", "const", [A_HEADS], skip=cat[0] - 4 * KB)
        bias_row = place("bias_row", "const", [REL], skip=cat[0] - 10 * KB)
        mirror = const("mirror", [P])
        nmax = const("nmax", [A_HEADS, TT])
        den = const("den", [A_HEADS, TT])
        rden = const("rden", [A_HEADS, TT])
        decay = const("decay", [2, TT])
        cat[0] = phase
        cosine = const("cosine", [T])
        sine = const("sine", [T])
        band = const("band", [3 * P])
        own = const("own", [P])
        pack = const("pack", [T])
        ya_sum = place("ya_sum", "const", [2, T], skip=cat[0] - 2 * KB)
        turned = const("turned", [T])
        mden = const("mden", [PATTERNS, TT, B_HEADS, 2])
        nbias = const("nbias", [B_HEADS, TT])
        nat = const("nat", [PATTERNS, TT, B_HEADS, 2])
        least = const("least", [TT, B_HEADS])
        ex = const("ex", [PATTERNS, TT, B_HEADS])
        zd = const("zd", [PATTERNS, TT, B_HEADS])
        share = const("share", [PATTERNS, TT, B_HEADS])
        vstat = const("vstat", [TT, 6])
        vmean = const("vmean", [TT, 2])
        ws_t = place("ws_t", "const", [4, P], skip=cat[0])
        bs_row = place("bs_row", "const", [4, P], skip=cat[0] + 2 * KB)
        assert cat[0] + 4 * KB <= 23 * KB

        mem = place("mem_tok", "v", [MT, D])
        memn = place("mem_n", "u", [MT, D])
        mem_hi = place("mem_hi", "x", [KC, M], F32R)
        mem_lo = place("mem_lo", "x", [KC, M], F32R, 8 * KB)
        kx = place("kx", "v", [KC, M])
        vx = place("vx", "u", [MT, D])
        qk_g = place("qk_g", "mid", [4, T])
        vg = place("vg", "mid", [TT, 4 * P], skip=8 * KB)
        sg = place("sg", "mid", [TT, 4 * P], skip=16 * KB)
        va = place("va", "mid", [TT, 4 * P], skip=24 * KB)
        g_hi = place("g_hi", "mid", [KC, P], F32R, 16 * KB)
        g_lo = place("g_lo", "mid", [KC, P], F32R, 20 * KB)
        g_raw = place("g_raw", "mid", [KC, G_RANK], skip=24 * KB)
        og = place("og", "mid", [TT, 4 * P])
        qa = place("qa", "y", [4, T])
        ka = place("ka", "y", [4, T], skip=8 * KB)
        cum = place("cum", "x", [2, T])
        ex_g = place("ex_g", "x", [2, T], skip=4 * KB)
        lev = [place(f"lev{n}", "x", [2, T], skip=(8 + 4 * n) * KB) for n in range(2)]
        near_back = place("near_back", "u", [A_HEADS, NEAR])
        a_own = place("a_own", "v", [2, TT, 2, P])
        a_far = place("a_far", "x", [2, len(PAIRS), 2, P], skip=4 * KB)
        q_far = place("q_far", "u", [2, T])
        k_far = place("k_far", "u", [2, T], skip=4 * KB)
        q_mid = place("q_mid", "x", [2, 3, P])
        square_g = nc.alloc_sbuf_tensor_at("square_g", [P, 2, T], F32, offset=base + region["const"] + phase)
        n_causal = len(CAUSAL) * P
        p_even, p_odd = (place(f"p_a{n}", "act", [n_causal], skip=n * 4 * n_causal) for n in range(2))
        p_first = place("p_first", "x", [n_causal])
        p_a = lambda h: p_first if h == 0 else (p_even, p_odd)[h % 2]
        pt_a = [place(f"pt_a{n}", "act", [n_causal], skip=(2 + n) * 4 * n_causal) for n in range(2)]
        o_a = place("o_a", "act", [TT, 4 * P], skip=24 * KB)
        qx = place("qx", "y", [KC, T])
        spot = lambda h: ("mid", 16 + 4 * h) if h < 2 else ("act", 4 * (h - 2))
        p_x = [place(f"p_x{h}", spot(n)[0], [TT, M], skip=spot(n)[1] * KB) for h, n in enumerate((0, 1, 0, 3))]
        pt_x = [place(f"pt_x{h}", spot(h)[0], [MT, T], skip=(spot(h)[1] + 8) * KB) for h in range(X_HEADS)]
        relu = [place(f"relu{n}", "v", [T], skip=2 * n * KB) for n in range(2)]
        square = [place(f"square{n}", "v", [T], skip=(4 + 2 * n) * KB) for n in range(2)]
        slot = lambda name, n, shape, skip=0: place(name, *(("y", shape, F32, 8 * KB * n + skip) if n < 2 else
                                                           ("uv"[n - 2], shape, F32, skip) if n < 4 else
                                                           ("mid", shape, F32, 8 * KB * (n - 4) + skip)))
        qk_b = {"q": [slot(f"q_b{p}", (6, 1, 6)[p], [B_HEADS, T]) for p in range(PATTERNS)],
                "k": [slot(f"k_b{p}", (7, 2, 7)[p], [B_HEADS, T]) for p in range(PATTERNS)]}
        n_band, n_own = len(BAND) * P, len(OWN) * P
        p_band = [slot(f"p_band{n}", 4, [n_band], n * 4 * n_band) for n in range(2)]
        p_own = [slot(f"p_own{n}", 4, [n_own], n * 4 * n_own) for n in range(2)]
        p_b = lambda st: (p_band if st.p == 0 else p_own)[st.h % 2]
        pt_band, pt_own = slot("pt_band", 4, [n_band], 8 * n_band), slot("pt_own", 4, [n_own], 8 * n_own)
        pt_b = lambda st: pt_band if st.p == 0 else pt_own
        v_b = slot("v_b", 3, [TT, 4 * P])
        u_b = [slot(f"u_b{p}", (0, 5, 1)[p], [B_HEADS, T]) for p in range(PATTERNS)]
        wide = [slot(f"wide{p}", (3, 4, 7)[p], [T, B_HEADS]) for p in range(PATTERNS)]
        ut = slot("ut", 6, [4, T])
        vt = slot("vt", 2, [TT, 4 * P])
        gate = [slot(f"gate{n}", (2, 3, 1, 0)[n], [4, T]) for n in range(4)]
        squares = {"norm_final": y, "norm_mix_post_2": place("squares_mid", "mid", [TT, D]),
                   "norm_mlp_post_2": place("squares_act", "act", [TT, D])}

        psum = ctx.enter_context(nc.psum_tensor("banks", [P, 8, 512], F32))
        bias_dram = nc.dram_tensor("bias_dram", [A_HEADS, REL], F32).ap()
        stat_dram = nc.dram_tensor("stat_dram", [PATTERNS, T, B_HEADS * 2], F32).ap()
        share_dram = nc.dram_tensor("share_dram", [PATTERNS, T * B_HEADS], F32).ap()

        bank_done = [sem(f"bank_done{b}") for b in range(8)]
        bank_free = [sem(f"bank_free{b}") for b in range(8)]
        raw_in = [sem(f"raw_in{n}") for n in range(RAW)]
        first_in = [sem(f"first_in{n}") for n in range(4)]
        hi_w = sem("hi_w")
        lo_w = sem("lo_w")
        hi_made = sem("hi_made")
        relu_made = sem("relu_made")
        square_made = sem("square_made")
        rstd_made = sem("rstd_made")
        xn_made = sem("xn_made")
        x_rows = sem("x_rows")
        x_in = [sem(f"x_in{tt}") for tt in range(TT)]
        mem_in, cols_in, const_in, glr_in, table_in = (sem(n) for n in ("mem_in", "cols_in", "const_in", "glr_in", "table_in"))
        glr_hi, glr_lo, gate_abs, gate_log, cum_made = (sem(n) for n in ("glr_hi", "glr_lo", "gate_abs", "gate_log", "cum_made"))
        pad_made, lev_diff, lev_exp, lev_made, far_exp, far_made, far_diff, own_clear = (
            sem(n) for n in ("pad_made", "lev_diff", "lev_exp", "lev_made", "far_exp", "far_made", "far_diff", "own_clear"))
        sq_g, ss_g, rstd_g = sem("sq_g"), sem("ss_g"), sem("rstd_g")
        sig_made = sem("sig_made")
        smax = sem("smax")
        px_made = sem("px_made")
        bias_out, near_in = sem("bias_out"), sem("near_in")
        bias_made = sem("bias_made")
        mirror_in = sem("mirror_in")
        x_back = sem("x_back")
        packed, roped = sem("packed"), sem("roped")
        row_in = sem("row_in")
        stat_out, nat_in, joint_diff, joint_exp, share_made, share_out = (
            sem(n) for n in ("stat_out", "nat_in", "joint_diff", "joint_exp", "share_made", "share_out"))
        wide_in = [sem(f"wide_in{p}") for p in range(PATTERNS)]
        yb_sum, yb_split, vn_stats, vn_made = sem("yb_sum"), sem("yb_split"), sem("vn_stats"), sem("vn_made")
        ws_in = sem("ws_in")
        b2_in = sem("b2_in")
        merged = sem("merged")
        y_clear = sem("y_clear")
        stored = sem("stored")
        yb_first = sem("yb_first")
        y_made = sem("y_made")
        dve_step, act_step = sem("dve_step"), sem("act_step")

        def wait(eng, s_, value):
            if not isinstance(value, int) or value > 0:
                eng.wait_ge(s_, value)

        def landed(t):
            return w_first[:, t, :] if t < 4 else w_raw[:, t % RAW, :]

        def wait_ready(eng, ready, turn):
            for b, count, plus in ready:
                wait(eng, bank_free[b], at(count, turn, plus))

        def walk(eng, handle):
            for item in s.items:
                if isinstance(item, tuple):
                    turns, body = item
                    with eng.Fori(0, turns) as turn:
                        for st in body:
                            handle(st, turn)
                else:
                    handle(item, None)

        def col(name, n=0, rows=P):
            return cols[0:rows, COLS[name] + n:COLS[name] + n + 1]

        def per_pattern(ap, p):
            return ap if p == 0 else ap.rearrange("q (r m) -> q m r", r=4)

        def natural(ap, p):
            return ap if p == 0 else ap.rearrange("q (m r) -> q m r", r=4)

        def over(ap, n):
            return ap.unsqueeze(1).broadcast_to([ap.shape[0], n, ap.shape[1]])

        def each(ap, n):
            return ap.unsqueeze(2).broadcast_to([ap.shape[0], ap.shape[1], n])

        def copies_of(st):
            b, half = st.bank, st.half
            full = psum[:, b, :]
            if st.out == "kx":
                return kx[:, 4 * st.blk + b, :], psum[:, b, 0:M], 1.0, b % 2 == 0
            if st.out == "vx":
                return vx[:, b, 512 * st.blk:512 * st.blk + 512], full, 1.0, b % 2 == 0
            if st.out == "glaqk":
                return qk_g[:, b, :], full, G_DK ** -0.5 if b < 2 else 1.0, b % 2 == 0
            if st.out == "vg":
                return vg[:, b, :], full, 1.0, b % 2 == 0
            if st.out == "va":
                return va[:, b, :], full, 1.0, b % 2 == 0
            if st.out == "qa":
                return qa[:, b, :], full, A_DIM ** -0.5, b % 2 == 0
            if st.out == "ka":
                return ka[:, b, :], full, 1.0, b % 2 == 0
            if st.out == "qx":
                return qx[:, 4 * st.blk + b, :], full, X_DIM ** -0.5, b % 2 == 0
            if st.out == "v2":
                return v_b[:, b, :], full, 1.0, b % 2 == 0
            if st.out == "copy":
                return y[:, b, 512 * st.blk:512 * st.blk + 512], full, 1.0, b % 2 == 0
            return None

        def blocks_of(p):
            return BAND if p == 0 else OWN

        block = ctx.enter_context(nc.Block())

        @block.sync
        def _(sp):
            sp.dma_start(ident[:], a["ident"]).then_inc(cols_in, 16)
            sp.dma_start(cols[:], a["cols"]).then_inc(cols_in, 16)
            for tt in range(TT):
                sp.dma_start(x[:, tt, :], a["x"][P * tt:P * tt + P, :]).then_inc(x_in[tt], 16)
            sp.dma_start(mirror[:], a["mirror"]).then_inc(mirror_in, 16)
            for t in range(4):
                sp.dma_start(w_first[:, t, :], a["weights"][t]).then_inc(first_in[t], 16)
            for slot in range(RAW):
                sp.dma_start(w_raw[:, slot, :], a["weights"][4 + slot]).then_inc(raw_in[slot], 16)
            with sp.Fori(4 // RAW + 1, TILES // RAW) as n:
                for slot in range(RAW):
                    sp.wait_ge(lo_w, n * RAW + (slot + 1 - RAW))
                    sp.dma_start(w_raw[:, slot, :], a["weights"][bass.ds(n * RAW + slot, 1)].rearrange("o p w -> p (o w)")
                                 ).then_inc(raw_in[slot], 16)
            for tt in range(TT):
                sp.wait_ge(x_rows, s.counts["xrows"] - TT + tt + 1)
                sp.dma_start(out[P * tt:P * tt + P, :], x[:, tt, :]).then_inc(stored, 16)
            sp.wait_ge(stored, 16 * TT)

        def split_waits(eng, st, turn):
            if st.slots_free is not None:
                b, count = st.slots_free
                wait(eng, bank_done[b], at(count, turn))

        @block.tensor
        def _(pe):
            def product(out_ap, lhs, rhs, start, stop):
                pe.matmul(out_ap, lhs[0], rhs[0], start=start, stop=False)
                pe.matmul(out_ap, lhs[0], rhs[1], start=False, stop=False)
                return pe.matmul(out_ap, lhs[1], rhs[0], start=False, stop=stop)

            def begin(bank, count, turn):
                wait(pe, bank_free[bank], at(count, turn))

            def gemm(st, turn):
                begin(st.bank, st.fill[0], turn)
                set_at = 4 * (st.tile[0] // 4 % 2)
                b = st.bank
                if st.after == "yb" and st.half == 0 and b == 0:
                    pe.wait_ge(yb_split, 1)
                for k in range(st.rows):
                    tile = k // 2 + st.half * (st.rows // 2)
                    if st.first and k % 2 == 0:
                        pe.wait_ge(lo_w, at(st.tile, turn, tile + 1))
                    if st.ready is not None:
                        wait_ready(pe, st.ready[k:k + 1], turn)
                    if st.src == "mid":
                        n = k // 4 if st.mid is None else st.mid
                        act = (mid_hi[n][:, k % 4, :], mid_lo[n][:, k % 4, :])
                    elif st.src == "memT":
                        act = (mem_hi[:, k, :], mem_lo[:, k, :])
                    else:
                        act = (act_hi[:, k, :], act_lo[:, k, :])
                    w = [x_[:, set_at + tile, (k % 2) * 512:(k % 2) * 512 + 512] for x_ in (w_hi, w_lo)]
                    start, stop = k == 0, k == st.rows - 1
                    if st.major == "T":
                        n = M if st.src == "memT" else T
                        mm = product(psum[:, b, 0:n], [x_[:, b * P:b * P + P] for x_ in w], act, start, stop)
                    else:
                        if st.out == "v2" and st.p > 0:
                            act = [x_.rearrange("q (m r) -> q r m", r=4)[:, b, :] for x_ in act]
                        else:
                            act = [x_[:, b * P:b * P + P] for x_ in act]
                        mm = product(psum[:, b, :], act, w, start, stop)
                mm.then_inc(bank_done[b], 1)

            def handle(st, turn):
                k = st.kind
                if k == "gemm":
                    gemm(st, turn)
                elif k == "flip":
                    pe.wait_ge(mirror_in, 16)
                    pe.wait_ge(near_in, 16)
                    for n in range(4):
                        begin(SIDE[n], st.fill[n], turn)
                        pe.matmul(psum[:, SIDE[n], :], mirror[:], near_back[:, 2 * n:2 * n + 2, :].rearrange("q h j -> q (h j)"),
                                  start=True, stop=True).then_inc(bank_done[SIDE[n]], 1)
                elif k == "turn":
                    if st.src == "mix":
                        wait_ready(pe, st.ready, turn)
                        order = [(n, tt) for n in range(KC) for tt in range(st.tiles)]
                    else:
                        order = [(n, tt) for tt in range(st.tiles) for n in range(KC)]
                    for n, tt in order:
                        c = st.chunks[n]
                        if tt == 0:
                            begin(n, st.fill[n], turn)
                        if st.src == "mix":
                            src = o_a[:, tt, c * P:c * P + P] if c < 4 else og[:, tt, (c - 4) * P:(c - 3) * P]
                        else:
                            if n == 0:
                                pe.wait_ge(xn_made, at(st.src, turn, tt + 1))
                            src = (y if st.tiles == TT else memn)[:, tt, c * P:c * P + P]
                        mm = pe.transpose(psum[:, n, tt * P:tt * P + P], src, ident[:])
                        if tt == st.tiles - 1:
                            mm.then_inc(bank_done[n], 1)
                elif k == "glr":
                    begin(4, st.fill[0], turn)
                    pe.wait_ge(glr_lo, 1)
                    for c in range(KC):
                        mm = product(psum[:, 4, :], (g_hi[:, c, :], g_lo[:, c, :]), (act_hi[:, c, :], act_lo[:, c, :]),
                                     c == 0, c == KC - 1)
                    mm.then_inc(bank_done[4], 1)
                elif k == "gate":
                    wait(pe, bank_free[4], at(s.glr.fill[0], None, 1))
                    pe.wait_ge(const_in, 32)
                    for pair in range(2):
                        b = 5 + pair
                        begin(b, st.fill[pair], turn)
                        pe.matmul(psum[:, b, :], w_gu[:, pair * P:pair * P + P], glr_t[:], start=True, stop=True
                                  ).then_inc(bank_done[b], 1)
                elif k == "relbias":
                    begin(4, st.fill[0], turn)
                    pe.wait_ge(table_in, 32)
                    pe.matmul(psum[0:A_HEADS, 4, 0:REL], table[0:RP_BUCKETS, :], bucket[0:RP_BUCKETS, :], start=True,
                              stop=True).then_inc(bank_done[4], 1)
                elif k == "level":
                    if st.n < len(LEVELS):
                        pe.wait_ge(lev_made, 2 * st.n + 2)
                        for kind in range(2):
                            begin(st.banks[kind], st.fill[kind], turn)
                        right = lev[st.n % 2].rearrange("q c (t b s l) -> q c t b s l", t=TT, s=2, l=LEVELS[st.n])
                        for n in range(2 * TT):
                            tt, pair = n // 2, n % 2
                            for kind in range(2):
                                rows, b = slice(64 * kind, 64 * kind + 64), st.banks[kind]
                                mm = pe.matmul(psum[:, b, n * P // 2:(n + 1) * P // 2], lev[st.n % 2][rows, pair, tt * P:tt * P + P],
                                               right[rows, pair, tt, :, 1, :], start=True, stop=True)
                                if n == 2 * TT - 1:
                                    mm.then_inc(bank_done[b], 1)
                    else:
                        for half in range(2):
                            for kind in range(2):
                                begin(SIDE[2 * half + kind], st.fill[2 * half + kind], turn)
                            for n in range(4):
                                tt, pair = 2 * half + n // 2, n % 2
                                for kind in range(2):
                                    rows, b = slice(64 * kind, 64 * kind + 64), SIDE[2 * half + kind]
                                    mm = pe.matmul(psum[:, b, n * P:n * P + P], qk_g[rows, 2 + pair, tt * P:tt * P + P],
                                                   qk_g[rows, pair, tt * P:tt * P + P], start=True, stop=True)
                                    if n == 3:
                                        mm.then_inc(bank_done[b], 1)
                elif k == "far":
                    pe.wait_ge(far_made, 8)
                    for fill in range(0, len(PAIRS), 2):
                        for kind in range(2):
                            begin(SIDE[(fill + kind) % 4], st.fill[fill + kind], turn)
                        for n in range(4):
                            (j, i), pair = PAIRS[fill + n // 2], n % 2
                            for kind in range(2):
                                rows, b = slice(64 * kind, 64 * kind + 64), SIDE[(fill + kind) % 4]
                                if i - j == 1:
                                    rhs = q_far[rows, pair, i * P:i * P + P]
                                else:
                                    rhs = q_mid[rows, pair, {(0, 2): 0, (1, 3): 1, (0, 3): 2}[j, i], :]
                                mm = pe.matmul(psum[:, b, n * P:n * P + P], k_far[rows, pair, j * P:j * P + P], rhs,
                                               start=True, stop=True)
                                if n == 3:
                                    mm.then_inc(bank_done[b], 1)
                elif k == "glaout":
                    for i in range(TT):
                        b = SIDE[i]
                        if i == 0:
                            for n in range(4):
                                begin(SIDE[n], st.fill[n], turn)
                        for h in range(G_HEADS):
                            for j in range(i + 1):
                                lhs = a_own[:, h % 2, i, h // 2, :] if j == i else a_far[:, h % 2, PAIRS.index((j, i)), h // 2, :]
                                mm = pe.matmul(psum[:, b, h * P:h * P + P], lhs, vg[:, j, h * P:h * P + P],
                                               start=(j == 0), stop=(j == i))
                        mm.then_inc(bank_done[b], 1)
                elif k == "sa_qk":
                    rows, pair = slice(64 * (st.h % 2), 64 * (st.h % 2) + 64), st.h // 2
                    for i, n, c0, ends in ROW_PLACES:
                        b = st.banks[n]
                        if c0 == 0:
                            begin(b, st.fill[n], turn)
                        mm = pe.matmul(psum[:, b, c0:c0 + P * (i + 1)], qa[rows, pair, i * P:i * P + P],
                                       ka[rows, pair, 0:P * (i + 1)], start=True, stop=True)
                        if ends:
                            mm.then_inc(bank_done[b], 1)
                elif k in ("sa_t", "bt_t"):
                    blocks = CAUSAL if k == "sa_t" else blocks_of(st.p)
                    src = p_a(st.h) if k == "sa_t" else p_b(st)
                    wait_ready(pe, st.ready, turn)
                    for n in range(len(blocks)):
                        b = st.banks[n // 4]
                        if n % 4 == 0:
                            begin(b, st.fill[n // 4], turn)
                        mm = pe.transpose(psum[:, b, n % 4 * P:n % 4 * P + P], src[:, n * P:n * P + P], ident[:])
                        if n % 4 == 3 or n == len(blocks) - 1:
                            mm.then_inc(bank_done[b], 1)
                elif k == "sa_pv":
                    b = st.banks[0]
                    begin(b, st.fill[0], turn)
                    wait_ready(pe, st.ready, turn)
                    for i in range(TT):
                        for j in range(i + 1):
                            n = CAUSAL.index((i, j))
                            mm = pe.matmul(psum[:, b, i * A_DIM:i * A_DIM + A_DIM], pt_a[st.h % 2][:, n * P:n * P + P],
                                           va[:, j, st.h * A_DIM:st.h * A_DIM + A_DIM], start=(j == 0), stop=(j == i))
                    mm.then_inc(bank_done[b], 1)
                elif k == "ca_qk":
                    if st.ready is not None:
                        wait_ready(pe, st.ready, turn)
                    for n in range(2):
                        b = st.banks[n]
                        begin(b, st.fill[n], turn)
                        for tt in (2 * n, 2 * n + 1):
                            for e in range(2):
                                mm = pe.matmul(psum[:, b, tt % 2 * M:tt % 2 * M + M], qx[:, 2 * st.h + e, tt * P:tt * P + P],
                                               kx[:, 2 * st.h + e, :], start=(e == 0), stop=(e == 1))
                        mm.then_inc(bank_done[b], 1)
                elif k == "ca_t":
                    pe.wait_ge(px_made, st.h + 1)
                    for mt in range(MT):
                        b = st.banks[mt]
                        begin(b, st.fill[mt], turn)
                        for tt in range(TT):
                            mm = pe.transpose(psum[:, b, tt * P:tt * P + P], p_x[st.h][:, tt, mt * P:mt * P + P], ident[:])
                        mm.then_inc(bank_done[b], 1)
                elif k == "ca_pv":
                    wait_ready(pe, st.ready, turn)
                    for e in range(2):
                        b = st.banks[e]
                        begin(b, st.fill[e], turn)
                        at_e = st.h * X_DIM + e * P
                        for mt in range(MT):
                            mm = pe.matmul(psum[:, b, :], vx[:, mt, at_e:at_e + P], pt_x[st.h][:, mt, :],
                                           start=(mt == 0), stop=(mt == MT - 1))
                        mm.then_inc(bank_done[b], 1)
                elif k == "bt_qk":
                    pe.wait_ge(roped, at(st.roped, turn, 1))
                    q_b, k_b = qk_b["q"][st.p], qk_b["k"][st.p]
                    if st.p == 0:
                        for i, n, c0, ends in BAND_PLACES:
                            b = st.banks[n]
                            if c0 == 0:
                                begin(b, st.fill[n], turn)
                            ks = [kt for q_, kt in BAND if q_ == i]
                            mm = pe.matmul(psum[:, b, c0:c0 + P * len(ks)], q_b[:, st.h, i * P:i * P + P],
                                           k_b[:, st.h, ks[0] * P:(ks[-1] + 1) * P], start=True, stop=True)
                            if ends:
                                mm.then_inc(bank_done[b], 1)
                    else:
                        b = st.banks[0]
                        begin(b, st.fill[0], turn)
                        for i in range(TT):
                            mm = pe.matmul(psum[:, b, i * P:i * P + P], q_b[:, st.h, i * P:i * P + P],
                                           k_b[:, st.h, i * P:i * P + P], start=True, stop=True)
                        mm.then_inc(bank_done[b], 1)
                elif k == "bt_pv":
                    begin(7, st.fill[0], turn)
                    wait_ready(pe, st.ready, turn)
                    blocks = blocks_of(st.p)
                    for i in range(TT):
                        ks = [kt for q_, kt in blocks if q_ == i]
                        for kt in ks:
                            n = blocks.index((i, kt))
                            mm = pe.matmul(psum[:, 7, i * P:i * P + P], v_b[:, kt, st.h * P:st.h * P + P],
                                           pt_b(st)[:, n * P:n * P + P], start=(kt == ks[0]), stop=(kt == ks[-1]))
                    mm.then_inc(bank_done[7], 1)
                elif k == "spatial":
                    pe.wait_ge(ws_in, 32)
                    pe.wait_ge(vn_made, TT)
                    for g in range(4):
                        begin(SIDE[g], st.fill[g], turn)
                        for c in range(TT):
                            mm = pe.matmul(psum[:, SIDE[g], c * P:c * P + P], vt[:, c, g * P:g * P + P], ws_t[:, g, :],
                                           start=True, stop=True)
                        mm.then_inc(bank_done[SIDE[g]], 1)

            pe.wait_ge(cols_in, 32)
            walk(pe, handle)

        @block.scalar
        def _(act):
            step = [0]

            def then(ins):
                step[0] += 1
                ins.then_inc(act_step, 1)
                act.wait_ge(act_step, step[0])

            def split(st, turn):
                for tile in st.splits:
                    split_waits(act, st, turn)
                    one_split(tile, turn)

            def one_split(tile, turn):
                t = tile[0]
                if t < 4:
                    act.wait_ge(first_in[t], 16)
                else:
                    act.wait_ge(raw_in[t % RAW], at([16 * ((t - 4) // RAW + 1), tile[1] * 16 // RAW], turn))
                act.activation(w_hi[:, t % 8, :], landed(t), ACT.Copy).then_inc(hi_w, 1)

            def tables():
                act.preload_act_table_set("natural_log_exp_and_others")

            def rms(slot, width, signal):
                then(act.activation(lnv[:, slot], sumsq[:, slot], ACT.Ln, bias=eps[:, 0:1], scale=1.0 / width))
                act.activation(rstd[:, slot], lnv[:, slot], ACT.Exp, scale=-0.5).then_inc(signal, 1)

            def gemm(st, turn):
                split(st, turn)
                b = st.bank
                filled = lambda: wait(act, bank_done[b], at(st.fill[0], turn, 1))
                plain = copies_of(st)
                if plain is not None and plain[3]:
                    filled()
                    act.activation(plain[0], plain[1], ACT.Copy, scale=plain[2]).then_inc(bank_free[b], 1)
                elif st.out == "rg":
                    filled()
                    act.activation(sg[:, b, :], psum[:, b, :], ACT.Sigmoid).then_inc(sig_made, 1)
                    if b == TT - 1:
                        tables()
                elif st.out == "up":
                    filled()
                    n = b % 2
                    wait(act, square_made, at(st.relu, turn, -1))
                    act.activation(relu[n][:], psum[:, b, :], ACT.Relu).then_inc(relu_made, 1)
                    act.wait_ge(relu_made, at(st.relu, turn, 1))
                    act.activation(mid_hi[st.mid][:, b, :], relu[n][:], ACT.Square).then_inc(hi_made, 1)
                elif st.out == "rope":
                    filled()
                    if b == 0 and st.after is not None:
                        act.wait_ge(roped, at(st.after, turn, 1))
                    act.activation(pack[ROPE_DIM * b:ROPE_DIM * b + ROPE_DIM, :], psum[0:ROPE_DIM, b, :], ACT.Copy
                                   ).then_inc(packed, 1)
                elif st.out == "u":
                    filled()
                    act.activation(ut[:, b, :], psum[:, b, :], ACT.Gelu_apprx_tanh).then_inc(bank_free[b], 1)
                elif st.out == "v":
                    filled()
                    act.activation(vt[:, b, :], psum[:, b, :], ACT.Gelu_apprx_tanh).then_inc(bank_free[b], 1)
                elif st.out == "gate":
                    filled()
                    if st.blk == 1 and b == 0:
                        act.wait_ge(yb_sum, 1)
                    if st.blk == 3 and b == 0:
                        act.wait_ge(yb_split, 1)
                    act.activation(gate[st.blk][:, b, :], psum[:, b, :], ACT.Sigmoid,
                                   bias=col("b_gate_2", 4 * st.blk + b)).then_inc(bank_free[b], 1)
                    if st.blk == 3 and b == TT - 1:
                        tables()
                elif st.out == "merge":
                    act.wait_ge(merged, at(st.merged, turn, 1))
                    act.activation(act_hi[:, 4 * st.half + b, :], gate[st.half][:, b, :], ACT.Copy).then_inc(hi_made, 1)

            def handle(st, turn):
                k = st.kind
                if k == "start":
                    for t in (2 * st.n, 2 * st.n + 1):
                        one_split([t, 0], None)
                elif k == "relbias":
                    act.wait_ge(glr_in, 16)
                    act.wait_ge(pad_made, 3)
                    act.activation(g_hi[:, :, 0:G_RANK], g_raw[:], ACT.Copy).then_inc(glr_hi, 1)
                elif k == "gemm":
                    gemm(st, turn)
                elif k in ("scale_rms", "rows_rms"):
                    src = {"mem": mem, "x": x, "y": y}[st.src]
                    if k == "scale_rms":
                        waste = memn if st.src == "mem" else y
                    else:
                        waste = squares[st.row]
                    tt = st.n
                    if st.ready == "mem":
                        act.wait_ge(mem_in, 16)
                    elif st.ready == "x":
                        act.wait_ge(x_in[tt], 16)
                    elif st.ready == "rows":
                        act.wait_ge(x_rows, at(st.after, turn, 1))
                    else:
                        wait_ready(act, st.ready[tt:tt + 1], turn)
                    then(act.activation(waste[:, tt, :], src[:, tt, :], ACT.Square, accum_out=sumsq[:, tt:tt + 1]))
                    rms(slice(tt, tt + 1), D, rstd_made)
                elif k == "turn":
                    act.wait_ge(cols_in, 32)
                    for n_c, c in enumerate(st.chunks):
                        b, n = n_c, P * st.tiles
                        wait(act, bank_done[b], at(st.fill[n_c], turn, 1))
                        hi = {"act": act_hi, "memT": mem_hi}[st.dst][:, c, :] if st.dst != "mid" else mid_hi[c // 4][:, c % 4, :]
                        gain = st.gains[c]
                        scale = 1.0 if gain is None else col(gain, 0 if gain == "g_norm" else c)
                        act.activation(hi, psum[:, b, 0:n], ACT.Copy, scale=scale).then_inc(hi_made, 1)
                elif k == "gate":
                    for pair in range(2):
                        act.wait_ge(bank_done[5 + pair], at(st.fill[pair], turn, 1))
                        act.activation(ex_g[:, pair, :], psum[:, 5 + pair, :], ACT.Abs, bias=col("b_gate", pair)
                                       ).then_inc(gate_abs, 1)
                    act.wait_ge(gate_abs, 2)
                    then(act.activation(ex_g[:], ex_g[:], ACT.Exp, scale=-1.0))
                    act.activation(ex_g[:], ex_g[:], ACT.Ln, bias=1.0).then_inc(gate_log, 1)
                    for n in range(2):
                        act.wait_ge(lev_diff, 2 * n + 2)
                        act.activation(ex_g[:], ex_g[:], ACT.Exp, scale=1.0 / G_NORM).then_inc(lev_exp, 1)
                elif k == "flip":
                    for n in range(0, 4, 2):
                        act.wait_ge(bank_done[SIDE[n]], at(st.fill[n], turn, 1))
                        act.activation(near[:, 2 * n:2 * n + 2, :].rearrange("q h j -> q (h j)"), psum[:, SIDE[n], :], ACT.Copy
                                       ).then_inc(bank_free[SIDE[n]], 1)
                elif k == "level":
                    n = st.n + 2
                    if n < len(LEVELS):
                        act.wait_ge(lev_diff, 2 * n + 2)
                        act.activation(ex_g[:], ex_g[:], ACT.Exp, scale=1.0 / G_NORM).then_inc(lev_exp, 1)
                elif k == "farprep":
                    act.wait_ge(cum_made, 2)
                    then(act.activation(q_far[:], cum[:], ACT.Exp, scale=1.0 / G_NORM))
                    last = cum[:].rearrange("q c (t n) -> q c t n", t=TT)[:, :, :, P - 1]
                    then(act.activation(decay[:], last, ACT.Exp, scale=1.0 / G_NORM))
                    act.wait_ge(far_diff, TT * 2)
                    act.activation(k_far[:], k_far[:], ACT.Exp, scale=1.0 / G_NORM).then_inc(far_exp, 1)
                elif k == "far":
                    for n in range(0, len(PAIRS), 2):
                        b = SIDE[n % 4]
                        act.wait_ge(bank_done[b], at(st.fill[n], turn, 1))
                        act.activation(a_far[:, n % 2, n - n % 2:n - n % 2 + 2].rearrange("q t c i -> q (t c i)"), psum[:, b, :], ACT.Copy).then_inc(bank_free[b], 1)
                elif k == "glaout":
                    for i in range(TT):
                        act.wait_ge(bank_done[SIDE[i]], at(st.fill[i], turn, 1))
                        wait(act, ss_g, i - 1)
                        act.activation(square_g[:, i % 2, :], psum[:, SIDE[i], :], ACT.Square).then_inc(sq_g, 1)
                        act.wait_ge(ss_g, i + 1)
                        rms(slice(4 * i, 4 * i + 4), G_DV, rstd_g)
                elif k == "sa_qk":
                    for order, (i, b_n, c0, ends) in enumerate(ROW_PLACES):
                        act.wait_ge(smax, at(st.smax, turn, order + 1 if ends else order + 2))
                        n, b = CAUSAL.index((i, 0)), st.banks[b_n]
                        ins = act.activation(p_a(st.h)[:, n * P:(n + i + 1) * P], psum[:, b, c0:c0 + P * (i + 1)], ACT.Exp,
                                             bias=nmax[:, st.h, i:i + 1], accum_out=den[:, st.h, i:i + 1])
                        if ends:
                            ins.then_inc(bank_free[b], 1)
                elif k in ("sa_t", "bt_t"):
                    dst = pt_a[st.h % 2] if k == "sa_t" else pt_b(st)
                    n = len(CAUSAL if k == "sa_t" else blocks_of(st.p))
                    for part in range(0, (n + 3) // 4, 2):
                        w, b = min(4, n - 4 * part) * P, st.banks[part]
                        act.wait_ge(bank_done[b], at(st.fill[part], turn, 1))
                        act.activation(dst[:, 4 * part * P:4 * part * P + w], psum[:, b, 0:w], ACT.Copy).then_inc(bank_free[b], 1)
                elif k == "ca_qk":
                    act.wait_ge(smax, at(st.smax, turn, 1))
                    for tt in range(TT):
                        b = st.banks[tt // 2]
                        ins = act.activation(p_x[st.h][:, tt, :], psum[:, b, tt % 2 * M:tt % 2 * M + M], ACT.Exp,
                                             bias=nmax[:, st.h, tt:tt + 1], accum_out=den[:, st.h, tt:tt + 1])
                        if tt % 2:
                            ins.then_inc(bank_free[b], 1)
                elif k == "ca_t":
                    b = st.banks[0]
                    act.wait_ge(bank_done[b], at(st.fill[0], turn, 1))
                    act.activation(pt_x[st.h][:, 0, :], psum[:, b, :], ACT.Copy).then_inc(bank_free[b], 1)
                elif k == "ca_pv":
                    for e in range(2):
                        b, c = st.banks[e], 2 * st.h + e
                        act.wait_ge(bank_done[b], at(st.fill[e], turn, 1))
                        act.activation(mid_hi[c // 4][:, c % 4, :], psum[:, b, :], ACT.Copy).then_inc(hi_made, 1)
                elif k == "bt_qk":
                    blocks = blocks_of(st.p)
                    act.wait_ge(smax, at(st.smax, turn, 1))
                    places = BAND_PLACES if st.p == 0 else [(i, 0, i * P, i == TT - 1) for i in range(TT)]
                    for i, b_n, c0, ends in places:
                        ks = [n for n, (q_, _) in enumerate(blocks) if q_ == i]
                        w, b = len(ks) * P, st.banks[b_n]
                        ins = act.activation(p_b(st)[:, ks[0] * P:ks[0] * P + w], psum[:, b, c0:c0 + w], ACT.Exp,
                                             bias=nbias[:, st.h, i:i + 1], scale=B_DIM ** -0.5,
                                             accum_out=mden[:, st.p, i, st.h, 1:2])
                        if ends:
                            ins.then_inc(bank_free[b], 1)
                elif k == "bt_pv":
                    act.wait_ge(bank_done[7], at(st.fill[0], turn, 1))
                    act.activation(natural(u_b[st.p][:, st.h, :], st.p), per_pattern(psum[:, 7, :], st.p), ACT.Copy
                                   ).then_inc(bank_free[7], 1)
                elif k == "joint":
                    act.wait_ge(joint_diff, 1)
                    act.activation(ex[:], ex[:], ACT.Exp, scale=B_DIM ** -0.5).then_inc(joint_exp, 1)
                elif k == "lnv":
                    tables()
                    act.wait_ge(vn_stats, 1)
                    then(act.activation(lnv[:, 0:TT], vmean[:, :, 1], ACT.Ln, bias=eps[:, 0:1]))
                    act.activation(rstd[:, 0:TT], lnv[:, 0:TT], ACT.Exp, scale=-0.5).then_inc(rstd_made, 1)
                elif k == "ya":
                    act.wait_ge(merged, at(st.merged, turn, 1))
                    act.activation(mid_hi[0][:, st.n, :], ya_sum[:, st.n % 2, :], ACT.Copy).then_inc(hi_made, 1)
                elif k == "ybsplit":
                    act.wait_ge(yb_sum, 1)
                    wait_ready(act, st.ready, turn)
                    act.activation(mid_hi[1][:], u_b[0][:], ACT.Copy).then_inc(hi_made, 1)

            tables()
            act.wait_ge(pad_made, 1)
            walk(act, handle)

        @block.vector
        def _(dve):
            step = [0]

            def then(ins):
                step[0] += 1
                ins.then_inc(dve_step, 1)
                dve.wait_ge(dve_step, step[0])

            def one_split(tile, turn):
                t = tile[0]
                dve.wait_ge(hi_w, at(tile, turn, 1))
                dve.tensor_tensor(w_lo[:, t % 8, :], landed(t), w_hi[:, t % 8, :], ALU.subtract).then_inc(lo_w, 1)

            def split(st, turn):
                for tile in st.splits:
                    split_waits(dve, st, turn)
                    one_split(tile, turn)

            def gemm(st, turn):
                split(st, turn)
                b = st.bank
                filled = lambda: wait(dve, bank_done[b], at(st.fill[0], turn, 1))
                plain = copies_of(st)
                if plain is not None and not plain[3]:
                    filled()
                    dve.tensor_scalar(plain[0], plain[1], plain[2], None, ALU.mult).then_inc(bank_free[b], 1)
                elif st.out == "rg":
                    dve.wait_ge(sig_made, b + 1)
                    dve.tensor_tensor(sg[:, b, :], psum[:, b, :], sg[:, b, :], ALU.mult).then_inc(bank_free[b], 1)
                elif st.out == "add":
                    filled()
                    dst = {"x": x, "y": y}[st.dst]
                    col0 = 512 * (st.half if st.rows == 4 else st.blk)
                    if st.after == "x_back":
                        dve.wait_ge(x_back, 16)
                    dve.tensor_tensor(dst[:, b, col0:col0 + 512], psum[:, b, :], dst[:, b, col0:col0 + 512], ALU.add
                                      ).then_inc(bank_free[b], 1)
                elif st.out == "up":
                    n = b % 2
                    dve.wait_ge(relu_made, at(st.relu, turn, 1))
                    dve.tensor_tensor(square[n][:], relu[n][:], relu[n][:], ALU.mult).then_inc(square_made, 1)
                    dve.wait_ge(square_made, at(st.relu, turn, 1))
                    dve.wait_ge(hi_made, at(st.hi, turn, 1))
                    dve.tensor_tensor(mid_lo[st.mid][:, b, :], square[n][:], mid_hi[st.mid][:, b, :], ALU.subtract
                                      ).then_inc(bank_free[b], 1)
                elif st.out == "rope":
                    dve.wait_ge(packed, at(st.packed, turn, 1))
                    dve.tensor_copy(per_pattern(qk_b[st.dst][st.p][:, b, :], st.p), natural(psum[:, b, :], st.p)).then_inc(bank_free[b], 1)
                elif st.out == "bra":
                    filled()
                    g = gate[st.half][:, b, :]
                    dve.tensor_tensor(g, psum[:, b, :], g, ALU.mult).then_inc(bank_free[b], 1)
                elif st.out == "merge":
                    filled()
                    ga, gb = gate[st.half][:, b, :], gate[2 + st.half][:, b, :]
                    then(dve.tensor_tensor(gb, psum[:, b, :], gb, ALU.mult))
                    dve.tensor_tensor(ga, ga, gb, ALU.add).then_inc(merged, 1)

            def handle(st, turn):
                k = st.kind
                if k == "start":
                    for t in (2 * st.n, 2 * st.n + 1):
                        one_split([t, 0], None)
                elif k == "gemm":
                    gemm(st, turn)
                elif k == "scale":
                    src, dst = (mem, memn) if st.src == "mem" else (x, y)
                    tt = st.n
                    dve.wait_ge(rstd_made, at(st.rstd, turn, 1))
                    dve.tensor_scalar(dst[:, tt, :], src[:, tt, :], rstd[:, tt:tt + 1], None, ALU.mult).then_inc(xn_made, 1)
                elif k == "rows":
                    dve.wait_ge(row_in, 16 * st.row_n)
                    src = {"x": x, "y": y}[st.src]
                    tt = st.n
                    dve.wait_ge(rstd_made, at(st.rstd, turn, 1))
                    ins = dve.scalar_tensor_tensor(src[:, tt, :], src[:, tt, :], rstd[:, tt:tt + 1], row[:], ALU.mult, ALU.mult)
                    if st.row == "norm_mlp_post_2" and tt < TT - 1:
                        ins.then_inc(y_made, 1)
                    elif st.src == "y":
                        then(ins)
                        if st.row == "norm_mlp_post_2":
                            dve.wait_ge(x_rows, s.counts["xrows"] - 1)
                        dve.tensor_tensor(x[:, tt, :], x[:, tt, :], y[:, tt, :], ALU.add).then_inc(x_rows, 1)
                    else:
                        ins.then_inc(x_rows, 1)
                elif k == "turn":
                    for n_c, c in enumerate(st.chunks):
                        b, n = n_c, P * st.tiles
                        dve.wait_ge(hi_made, at(st.hi, turn, n_c + 1))
                        if st.dst == "mid":
                            hi, lo = mid_hi[c // 4][:, c % 4, :], mid_lo[c // 4][:, c % 4, :]
                        else:
                            hi, lo = [t_[:, c, :] for t_ in {"act": (act_hi, act_lo), "memT": (mem_hi, mem_lo)}[st.dst]]
                        gain = st.gains[c]
                        scale = 1.0 if gain is None else col(gain, 0 if gain == "g_norm" else c)
                        dve.scalar_tensor_tensor(lo, psum[:, b, 0:n], scale, hi, ALU.mult, ALU.subtract).then_inc(bank_free[b], 1)
                elif k == "glr":
                    dve.wait_ge(bank_done[4], at(st.fill[0], turn, 1))
                    dve.wait_ge(bias_out, 16)
                    dve.tensor_copy(glr_t[:], psum[0:G_RANK, 4, :]).then_inc(bank_free[4], 1)
                elif k == "gate":
                    for pair in range(2):
                        dve.wait_ge(gate_abs, pair + 1)
                        ins = dve.tensor_scalar(lev[0][:, pair, :], psum[:, 5 + pair, :], col("b_gate", pair), 0.0, ALU.add, ALU.min)
                        ins.then_inc(bank_free[5 + pair], 1)
                    dve.wait_ge(gate_log, 1)
                    for pair in range(2):
                        dve.wait_ge(bank_free[5 + pair], at(st.fill[pair], turn, 1))
                    then(dve.tensor_tensor(lev[0][:], lev[0][:], ex_g[:], ALU.subtract))
                    for pair in range(2):
                        for tt in range(TT):
                            part = slice(tt * P, tt * P + P)
                            ins = dve.tensor_tensor_scan(cum[:, pair, part], lev[0][:, pair, part], lev[0][:, pair, part], 0.0,
                                                         ALU.add, ALU.bypass)
                        ins.then_inc(cum_made, 1)
                elif k == "flip":
                    for n in range(1, 4, 2):
                        dve.wait_ge(bank_done[SIDE[n]], at(st.fill[n], turn, 1))
                        dve.tensor_copy(near[:, 2 * n:2 * n + 2, :].rearrange("q h j -> q (h j)"), psum[:, SIDE[n], :]
                                        ).then_inc(bank_free[SIDE[n]], 1)
                elif k == "relbias":
                    dve.wait_ge(glr_hi, 1)
                    dve.tensor_tensor(g_lo[:, :, 0:G_RANK], g_raw[:], g_hi[:, :, 0:G_RANK], ALU.subtract).then_inc(glr_lo, 1)
                    dve.wait_ge(bank_done[4], at(st.fill[0], turn, 1))
                    dve.tensor_copy(bias_row[0:A_HEADS, 0:NEAR], psum[0:A_HEADS, 4, 0:NEAR]).then_inc(bank_free[4], 1)
                    dve.memset(bias_row[0:A_HEADS, NEAR:REL], MASKED).then_inc(bias_made, 1)
                elif k == "level":
                    dve.wait_ge(own_clear, 1)
                    dve.wait_ge(const_in, 32)
                    if st.n < len(LEVELS):
                        size = LEVELS[st.n]
                        halves = lambda ap: ap.rearrange("q n (b s l) -> q n b s l", s=2, l=size)[:, :, :, 1, :]
                        wait_ready(dve, st.ready[4:], turn)
                        for kind in range(2):
                            b = st.banks[kind]
                            dve.wait_ge(bank_done[b], at(st.fill[kind], turn, 1))
                            dve.copy_predicated(halves(a_own[:, kind].rearrange("q t c i -> q (t c) i")),
                                                halves(over(lvl_mask[:, st.n, :], 2 * TT)),
                                                psum[:, b, :].rearrange("q (n b l) -> q n b l", n=2 * TT, l=size)
                                                ).then_inc(bank_free[b], 1)
                    else:
                        for n in range(4):
                            b = SIDE[n]
                            dve.wait_ge(bank_done[b], at(st.fill[n], turn, 1))
                            own_part = a_own[:, n % 2, n // 2 * 2:n // 2 * 2 + 2].rearrange("q t c i -> q (t c) i")
                            dve.copy_predicated(own_part, over(lvl_mask[:, st.n, :], G_HEADS),
                                                psum[:, b, :].rearrange("q (h i) -> q h i", h=G_HEADS)).then_inc(bank_free[b], 1)
                elif k == "farprep":
                    dve.wait_ge(cum_made, 2)
                    for pair in range(2):
                        for tt in range(TT):
                            part = slice(tt * P, tt * P + P)
                            dve.tensor_scalar(k_far[:, pair, part], cum[:, pair, part], -1.0,
                                              cum[:, pair, tt * P + P - 1:tt * P + P], ALU.mult, ALU.add).then_inc(far_diff, 1)
                    dve.wait_ge(far_exp, 1)
                    dve.tensor_tensor(k_far[:], k_far[:], qk_g[:, 2:4, :], ALU.mult).then_inc(far_made, 1)
                    dve.tensor_tensor(q_far[:], q_far[:], qk_g[:, 0:2, :], ALU.mult).then_inc(far_made, 1)
                elif k == "farmid":
                    dve.wait_ge(lev_diff, 2 * len(LEVELS))
                    dve.wait_ge(far_made, 2)
                    for pair in range(2):
                        dve.tensor_scalar(q_mid[:, pair, 0, :], q_far[:, pair, 2 * P:3 * P], decay[:, pair, 1:2], None,
                                          ALU.mult).then_inc(far_made, 1)
                        dve.tensor_scalar(q_mid[:, pair, 1, :], q_far[:, pair, 3 * P:4 * P], decay[:, pair, 2:3], None,
                                          ALU.mult).then_inc(far_made, 1)
                        dve.tensor_scalar(q_mid[:, pair, 2, :], q_far[:, pair, 3 * P:4 * P], decay[:, pair, 2:3],
                                          decay[:, pair, 1:2], ALU.mult, ALU.mult).then_inc(far_made, 1)
                elif k == "far":
                    for n in range(1, len(PAIRS), 2):
                        b = SIDE[n % 4]
                        dve.wait_ge(bank_done[b], at(st.fill[n], turn, 1))
                        dve.tensor_copy(a_far[:, n % 2, n - n % 2:n - n % 2 + 2].rearrange("q t c i -> q (t c i)"), psum[:, b, :]).then_inc(bank_free[b], 1)
                elif k == "glaout":
                    for i in range(TT):
                        dve.wait_ge(sq_g, i + 1)
                        dve.tensor_reduce(sumsq[:, 4 * i:4 * i + 4], square_g[:, i % 2, :].rearrange("q (h e) -> q h e", h=G_HEADS),
                                          AX.X, ALU.add).then_inc(ss_g, 1)
                        dve.wait_ge(rstd_g, i + 1)
                        v = og[:, i, :].rearrange("q (h e) -> q h e", h=G_HEADS)
                        then(dve.tensor_tensor(v, psum[:, SIDE[i], :].rearrange("q (h e) -> q h e", h=G_HEADS),
                                               each(rstd[:, 4 * i:4 * i + 4], G_DV), ALU.mult))
                        dve.tensor_tensor(og[:, i, :], og[:, i, :], sg[:, i, :], ALU.mult).then_inc(bank_free[SIDE[i]], 1)
                elif k == "sa_qk":
                    if st.h == 0:
                        wait_ready(dve, st.ready, turn)
                    for i, b_n, c0, ends in ROW_PLACES:
                        b, end = st.banks[b_n], c0 + P * (i + 1)
                        dve.wait_ge(bank_done[b], at(st.fill[b_n], turn, 1))
                        n = min(P * (i + 1), NEAR)
                        then(dve.tensor_tensor(psum[:, b, end - n:end], psum[:, b, end - n:end], near[:, st.h, NEAR - n:NEAR], ALU.add))
                        dve.tensor_reduce(nmax[:, st.h, i:i + 1], psum[:, b, c0:end], AX.X, ALU.max, negate=True).then_inc(smax, 1)
                elif k in ("sa_t", "bt_t"):
                    dst = pt_a[st.h % 2] if k == "sa_t" else pt_b(st)
                    if k == "sa_t" or st.p == 0:
                        b = st.banks[1]
                        dve.wait_ge(bank_done[b], at(st.fill[1], turn, 1))
                        dve.tensor_copy(dst[:, 4 * P:8 * P], psum[:, b, :]).then_inc(bank_free[b], 1)
                elif k == "sa_pv":
                    then(dve.reciprocal(rden[:, st.h, :], den[:, st.h, :]))
                    b = st.banks[0]
                    dve.wait_ge(bank_done[b], at(st.fill[0], turn, 1))
                    dve.tensor_tensor(o_a[:, :, st.h * A_DIM:st.h * A_DIM + A_DIM],
                                      psum[:, b, 0:TT * A_DIM].rearrange("q (t d) -> q t d", t=TT),
                                      each(rden[:, st.h, :], A_DIM), ALU.mult).then_inc(bank_free[b], 1)
                elif k == "ca_qk":
                    for n in range(2):
                        dve.wait_ge(bank_done[st.banks[n]], at(st.fill[n], turn, 1))
                    b = st.banks[0]
                    dve.tensor_reduce(nmax[:, st.h, :], psum[:, b:b + 2, :].rearrange("q b (t m) -> q (b t) m", t=2), AX.X, ALU.max,
                                      negate=True).then_inc(smax, 1)
                    for n in range(2):
                        dve.wait_ge(bank_free[st.banks[n]], at(st.fill[n], turn, 1))
                    then(dve.reciprocal(rden[:, st.h, :], den[:, st.h, :]))
                    dve.tensor_tensor(p_x[st.h][:], p_x[st.h][:], each(rden[:, st.h, :], M), ALU.mult).then_inc(px_made, 1)
                elif k == "ca_t":
                    b = st.banks[1]
                    dve.wait_ge(bank_done[b], at(st.fill[1], turn, 1))
                    dve.tensor_copy(pt_x[st.h][:, 1, :], psum[:, b, :]).then_inc(bank_free[b], 1)
                elif k == "ca_pv":
                    for e in range(2):
                        b, c = st.banks[e], 2 * st.h + e
                        dve.wait_ge(hi_made, at(st.hi, turn, e + 1))
                        dve.tensor_tensor(mid_lo[c // 4][:, c % 4, :], psum[:, b, :], mid_hi[c // 4][:, c % 4, :], ALU.subtract
                                          ).then_inc(bank_free[b], 1)
                elif k == "rope":
                    dve.wait_ge(packed, at(st.packed, turn))
                    if st.p == 0 and st.dst == "q":
                        dve.wait_ge(b2_in, 64)
                    swap = [(n + ROPE_DIM // 2) % ROPE_DIM for n in range(ROPE_DIM)]
                    then(dve.stream_shuffle(turned[:], pack[:], swap))
                    then(dve.tensor_tensor(pack[:], pack[:], cosine[:], ALU.mult))
                    then(dve.tensor_tensor(turned[:], turned[:], sine[:], ALU.mult))
                    for h in range(B_HEADS):
                        rows = slice(ROPE_DIM * h, ROPE_DIM * h + ROPE_DIM)
                        ins = dve.tensor_tensor(per_pattern(qk_b[st.dst][st.p][0:ROPE_DIM, h, :], st.p), natural(pack[rows, :], st.p),
                                                natural(turned[rows, :], st.p), ALU.add)
                    ins.then_inc(roped, 1)
                elif k == "bt_qk":
                    if st.p == 0:
                        for i, b_n, c0, _ in BAND_PLACES:
                            b, w = st.banks[b_n], P * len([1 for q_, _ in BAND if q_ == i])
                            dve.wait_ge(bank_done[b], at(st.fill[b_n], turn, 1))
                            m0 = P if i == 0 else 0
                            rows = psum[:, b, c0:c0 + w]
                            then(dve.tensor_tensor(rows, rows, band[:, m0:m0 + w], ALU.add))
                            ins = dve.tensor_reduce(mden[:, st.p, i, st.h, 0:1], rows, AX.X, ALU.max, negate=True)
                    else:
                        b = st.banks[0]
                        dve.wait_ge(bank_done[b], at(st.fill[0], turn, 1))
                        v = psum[:, b, :].rearrange("q (t k) -> q t k", t=TT)
                        mask = band[:, P:2 * P] if st.p == 1 else own[:]
                        then(dve.tensor_tensor(v, v, over(mask, TT), ALU.add))
                        ins = dve.tensor_reduce(mden[:, st.p, :, st.h, 0], v, AX.X, ALU.max, negate=True)
                    then(ins)
                    dve.tensor_scalar(nbias[:, st.h, :], mden[:, st.p, :, st.h, 0], B_DIM ** -0.5, None, ALU.mult).then_inc(smax, 1)
                elif k == "joint":
                    dve.wait_ge(nat_in, 16)
                    low, d_ = nat[:, :, :, :, 0], nat[:, :, :, :, 1]
                    then(dve.tensor_tensor(least[:], low[:, 0], low[:, 1], ALU.min))
                    then(dve.tensor_tensor(least[:], least[:], low[:, 2], ALU.min))
                    for p in range(PATTERNS):
                        ins = dve.tensor_tensor(ex[:, p], least[:], low[:, p], ALU.subtract)
                    ins.then_inc(joint_diff, 1)
                    dve.wait_ge(joint_exp, 1)
                    for p in range(PATTERNS):
                        ins = dve.tensor_tensor(zd[:, p], ex[:, p], d_[:, p], ALU.mult)
                    then(ins)
                    then(dve.tensor_tensor(zd[:, 0], zd[:, 0], zd[:, 1], ALU.add))
                    then(dve.tensor_tensor(zd[:, 0], zd[:, 0], zd[:, 2], ALU.add))
                    then(dve.reciprocal(zd[:, 0], zd[:, 0]))
                    for p in range(PATTERNS):
                        ins = dve.tensor_tensor(share[:, p], ex[:, p], zd[:, 0], ALU.mult)
                    ins.then_inc(share_made, 1)
                elif k == "ybsum":
                    wait_ready(dve, st.ready, turn)
                    for p in (1, 2):
                        dve.wait_ge(wide_in[p], 16)
                        then(dve.tensor_tensor(u_b[p][:], u_b[p][:], wide[p][:].rearrange("q t h -> q h t"), ALU.mult))
                    then(dve.tensor_tensor(u_b[1][:], u_b[1][:], u_b[2][:], ALU.add))
                    dve.wait_ge(yb_first, 1)
                    dve.tensor_tensor(u_b[0][:], u_b[0][:], u_b[1][:], ALU.add).then_inc(yb_sum, 1)
                elif k == "lnv":
                    for tt in range(TT):
                        wait_ready(dve, st.ready[tt:tt + 1], turn)
                        ins = dve.bn_stats(vstat[:, tt, :], vt[:, tt, :])
                    then(ins)
                    for tt in range(TT):
                        ins = dve.bn_aggr(vmean[:, tt, :], vstat[:, tt, :])
                    ins.then_inc(vn_stats, 1)
                    dve.wait_ge(rstd_made, at(st.rstd, turn, 1))
                    dve.wait_ge(row_in, 16 * st.row_n)
                    for tt in range(TT):
                        then(dve.tensor_scalar(vt[:, tt, :], vt[:, tt, :], vmean[:, tt, 0:1], rstd[:, tt:tt + 1], ALU.subtract, ALU.mult))
                        then(dve.tensor_tensor(vt[:, tt, :], vt[:, tt, :], row[:, 0:512], ALU.mult))
                        dve.tensor_tensor(vt[:, tt, :], vt[:, tt, :], row[:, 512:1024], ALU.add).then_inc(vn_made, 1)
                elif k == "ya":
                    g, b = st.n, SIDE[st.n]
                    dve.wait_ge(bank_done[b], at(st.of.fill[g], turn, 1))
                    v = ya_sum[:, g % 2, :]
                    then(dve.tensor_tensor(v.rearrange("q (c t) -> q c t", c=TT), psum[:, b, :].rearrange("q (c t) -> q c t", c=TT),
                                           over(bs_row[:, g, :], TT), ALU.add))
                    dve.tensor_tensor(v, v, ut[:, g, :], ALU.mult).then_inc(merged, 1)
                    dve.wait_ge(merged, at(st.merged, turn, 1))
                    dve.wait_ge(hi_made, at(st.hi, turn, 1))
                    dve.tensor_tensor(mid_lo[0][:, g, :], v, mid_hi[0][:, g, :], ALU.subtract).then_inc(bank_free[b], 1)
                elif k == "ybsplit":
                    dve.wait_ge(hi_made, at(st.hi, turn, 1))
                    dve.tensor_tensor(mid_lo[1][:], u_b[0][:], mid_hi[1][:], ALU.subtract).then_inc(yb_split, 1)
                elif k == "clear":
                    wait_ready(dve, st.ready, turn)
                    dve.memset(y[:], 0.0).then_inc(y_clear, 1)
                    dve.wait_ge(y_clear, 1)

            dve.wait_ge(cols_in, 32)
            walk(dve, handle)

        @block.gpsimd
        def _(pool):
            pool.memset(eps[:], EPS).then_inc(pad_made, 1)
            pool.memset(g_hi[:].bitcast(F32), 0.0).then_inc(pad_made, 1)
            pool.memset(g_lo[:].bitcast(F32), 0.0).then_inc(pad_made, 1)
            pool.dma_start(g_raw[:], a["w_glr"]).then_inc(glr_in, 16)
            pool.dma_start(w_gu[:], a["w_gate_up"]).then_inc(const_in, 16)
            pool.dma_start(lvl_mask[:], a["lvl_mask"]).then_inc(const_in, 16)

            def load_row(parts):
                for name, c0, n in parts:
                    pool.dma_start(row[:, c0:c0 + n], a[name].partition_broadcast(P)).then_inc(row_in, 16)

            pool.dma_start(table[0:RP_BUCKETS, :], a["table"]).then_inc(table_in, 16)
            pool.dma_start(bucket[0:RP_BUCKETS, :], a["bucket"]).then_inc(table_in, 16)
            load_row([("norm_final", 0, D)])
            pool.memset(a_own[:], 0.0).then_inc(own_clear, 1)

            def handle(st, turn):
                k = st.kind
                if k == "gemm":
                    if st.out == "merge":
                        b = st.bank
                        pool.wait_ge(hi_made, at(st.hi, turn, 1))
                        pool.tensor_tensor(act_lo[:, 4 * st.half + b, :], gate[st.half][:, b, :], act_hi[:, 4 * st.half + b, :],
                                           ALU.subtract).then_inc(bank_free[b], 1)
                elif k == "gate":
                    pool.wait_ge(cum_made, 2)
                    for n in range(2):
                        level(n, st)
                elif k == "relbias":
                    pool.wait_ge(bias_made, 1)
                    pool.wait_ge(bank_free[4], at(st.fill[0], turn, 1))
                    pool.dma_start(bias_dram, bias_row[0:A_HEADS, :]).then_inc(bias_out, 16)
                    pool.wait_ge(bias_out, 16)
                    toeplitz = bass.AP(tensor=bias_dram.tensor, offset=0, ap=[[1, P], [REL, A_HEADS], [1, NEAR]])
                    pool.dma_start(near_back[:], toeplitz).then_inc(near_in, 16)
                elif k == "level":
                    if st.n + 2 < len(LEVELS):
                        level(st.n + 2, st)
                elif k == "glaout":
                    wait_ready(pool, [(b, st.fill[n], 1) for n, b in enumerate(SIDE)], turn)
                    pool.dma_start(mem[:], a["mem"].rearrange("(t p) d -> p t d", p=P)).then_inc(mem_in, 16)
                elif k == "reload":
                    wait_ready(pool, st.ready, turn)
                    pool.dma_start(x[:], a["x"].rearrange("(t p) d -> p t d", p=P)).then_inc(x_back, 16)
                elif k == "load2":
                    wait_ready(pool, st.ready, turn)
                    pool.dma_start(cosine[:], a["cosine"]).then_inc(b2_in, 16)
                    pool.dma_start(sine[:], a["sine"]).then_inc(b2_in, 16)
                    pool.dma_start(band[:], a["band"]).then_inc(b2_in, 16)
                    pool.dma_start(own[:], a["own"]).then_inc(b2_in, 16)
                    pool.dma_start(ws_t[:], a["w_spatial_t"]).then_inc(ws_in, 16)
                    pool.dma_start(bs_row[:].rearrange("q g t -> q (g t)"), a["b_spatial_2"].partition_broadcast(P)).then_inc(ws_in, 16)
                elif k == "rows" and st.row == "norm_mlp_post_2" and st.n == TT - 1:
                    pass
                elif k == "rows" and st.row == "norm_mlp_post_2":
                    pool.wait_ge(y_made, st.n + 1)
                    pool.tensor_tensor(x[:, st.n, :], x[:, st.n, :], y[:, st.n, :], ALU.add).then_inc(x_rows, 1)
                elif k == "rows" and st.n == TT - 1:
                    pool.wait_ge(x_rows, at(st.xrows, turn, 1))
                    if st.row == "norm_final":
                        load_row([("ln_v_gain_2", 0, 512), ("ln_v_bias_2", 512, 512)])
                    elif st.row == "norm_mix_post_2":
                        load_row([("norm_mlp_post_2", 0, D)])
                elif k == "spatial":
                    pool.wait_ge(vn_made, TT)
                    load_row([("norm_mix_post_2", 0, D)])
                elif k == "ybsum":
                    pool.wait_ge(wide_in[0], 16)
                    wait_ready(pool, st.ready, turn)
                    pool.tensor_tensor(u_b[0][:], u_b[0][:], wide[0][:].rearrange("q t h -> q h t"), ALU.mult).then_inc(yb_first, 1)
                elif k == "stats":
                    wait_ready(pool, st.ready, turn)
                    src, dst = mden[:, st.p].rearrange("q t h s -> q t (h s)"), stat_dram[st.p]
                    if st.p == 0:
                        pool.dma_start(dst.rearrange("(t q) v -> q t v", t=TT), src).then_inc(stat_out, 16)
                    else:
                        pool.dma_start(dst.rearrange("(m r) v -> m r v", r=4), src).then_inc(stat_out, 16)
                elif k == "joint":
                    pool.wait_ge(stat_out, 16 * PATTERNS)
                    pool.dma_start(nat[:].rearrange("q p t h s -> q p (t h s)"), stat_dram.rearrange("p (q t) v -> q p (t v)", t=TT)).then_inc(nat_in, 16)
                    pool.wait_ge(share_made, 1)
                    pool.dma_start(share_dram.rearrange("p (q v) -> q p v", q=P), share[:].rearrange("q p t h -> q p (t h)")).then_inc(share_out, 16)
                    pool.wait_ge(share_out, 16)
                    wait_ready(pool, st.ready, turn)
                    for p in range(PATTERNS):
                        pool.dma_start(wide[p][:].rearrange("q t h -> q (t h)"), share_dram[p].partition_broadcast(P)).then_inc(wide_in[p], 16)

            def level(n, st):
                size = LEVELS[n]
                view = lambda ap: ap.rearrange("q c (b s l) -> q (c b) s l", s=2, l=size)
                c_, e_, l_ = view(cum[:]), view(ex_g[:]), view(lev[n % 2][:])
                q_, k_ = view(qk_g[:, 0:2, :]), view(qk_g[:, 2:4, :])
                ref = c_[:, :, 0, size - 1:size].broadcast_to([P, 2 * T // (2 * size), size])
                wait(pool, lev_made, 2 * n)
                if n == 0:
                    wait_ready(pool, st.qk_ready, None)
                pool.tensor_tensor(e_[:, :, 0, :], ref, c_[:, :, 0, :], ALU.subtract).then_inc(lev_diff, 1)
                pool.tensor_tensor(e_[:, :, 1, :], c_[:, :, 1, :], ref, ALU.subtract).then_inc(lev_diff, 1)
                if n >= 2:
                    for b, count in zip(s.levels[n - 2].banks, s.levels[n - 2].fill):
                        pool.wait_ge(bank_done[b], at(count, None, 1))
                pool.wait_ge(lev_exp, n + 1)
                pool.tensor_tensor(l_[:, :, 0, :], k_[:, :, 0, :], e_[:, :, 0, :], ALU.mult).then_inc(lev_made, 1)
                pool.tensor_tensor(l_[:, :, 1, :], q_[:, :, 1, :], e_[:, :, 1, :], ALU.mult).then_inc(lev_made, 1)

            for item in s.items:
                if not isinstance(item, tuple):
                    handle(item, None)



def rel_bucket(d):
    exact = RP_BUCKETS // 2
    large = exact + (np.log(np.maximum(d, 1).astype(np.float32) / np.float32(exact))
                     / np.float32(math.log(RP_MAX_DIST / exact)) * np.float32(RP_BUCKETS - exact)).astype(np.int32)
    return np.where(d < exact, np.maximum(d, 0), np.minimum(large, RP_BUCKETS - 1))


def shape_constants():
    u = np.arange(REL)
    d = NEAR - 1 - u
    bucket = np.zeros((RP_BUCKETS, REL), np.float32)
    bucket[rel_bucket(d[d >= 0]), u[d >= 0]] += 1.0
    bucket[RP_BUCKETS - 1, u[d >= 0]] -= 1.0
    j, i = np.arange(P)[:, None], np.arange(P)[None, :]
    lvl = [(j // (2 * n) == i // (2 * n)) & (j % (2 * n) < n) & (i % (2 * n) >= n) for n in LEVELS] + [j == i]
    half = ROPE_DIM // 2
    inv = ROPE_THETA ** (-np.arange(0, ROPE_DIM, 2, dtype=np.float32) / np.float32(ROPE_DIM))
    ang = np.arange(T, dtype=np.float32)[None, :] * inv.astype(np.float32)[:, None]
    cos, sin = np.cos(ang), np.sin(ang)
    q, k = np.arange(P)[:, None], np.arange(3 * P)[None, :] - P
    return {
        "ident": np.eye(P, dtype=np.float32),
        "mirror": np.eye(P, dtype=np.float32)[::-1],
        "bucket": bucket,
        "lvl_mask": np.stack(lvl, 1).astype(np.int32),
        "cosine": np.tile(np.concatenate([cos, cos]), (B_HEADS, 1)).astype(np.float32),
        "sine": np.tile(np.concatenate([-sin, sin]), (B_HEADS, 1)).astype(np.float32),
        "band": np.where(np.abs(q - k) <= RADIUS, 0.0, MASKED).astype(np.float32),
        "own": np.where(j % 4 == i % 4, 0.0, MASKED).astype(np.float32),
    }


def lay_out(inputs):
    a = dict(shape_constants())
    a["x"] = np.ascontiguousarray(inputs["x"][0])
    a["mem"] = np.ascontiguousarray(inputs["mem"][0])
    tiles = []
    for name, r0, rows, c0, n in GROUPS:
        w = inputs[name][0][r0:r0 + rows, c0:c0 + n]
        if n == 512:
            w = w.reshape(4, 2, P, 512).transpose(0, 2, 1, 3)
        else:
            w = w.reshape(2, 2, P, 2, 512).transpose(3, 0, 2, 1, 4)
        tiles.append(w.reshape(4, P, WORDS))
    a["weights"] = np.concatenate(tiles)
    a["cols"] = np.concatenate([inputs[n].reshape(-1, P) for n in COLS]).T.copy()
    a["w_glr"] = inputs["w_in"][0][:, W_IN["glr"]:W_IN["glr"] + G_RANK].reshape(KC, P, G_RANK).transpose(1, 0, 2).copy()
    a["w_gate_up"] = inputs["w_gate_up"][0]
    a["table"] = inputs["rp_table"]
    a["w_spatial_t"] = inputs["w_spatial_2"][0].transpose(2, 0, 1).copy()
    a["b_spatial_2"] = inputs["b_spatial_2"].reshape(-1)
    for n in ("norm_final", "ln_v_gain_2", "ln_v_bias_2", "norm_mix_post_2", "norm_mlp_post_2"):
        a[n] = inputs[n].reshape(-1)
    return {n: np.ascontiguousarray(v) for n, v in a.items()}


def kernel(**inputs):
    import concourse.bacc as bacc
    from concourse.bass_utils import run_bass_kernel_spmd

    nc = bacc.Bacc("TRN2", target_bir_lowering=False, num_devices=1)
    arrays = lay_out({n: np.asarray(v) for n, v in inputs.items()})
    aps = {n: nc.dram_tensor(f"in_{n}", v.shape, mybir.dt.from_np(v.dtype), kind="ExternalInput").ap()
           for n, v in arrays.items()}
    out = nc.dram_tensor("out", (T, D), F32, kind="ExternalOutput").ap()
    two_blocks(nc, aps, out)
    r = run_bass_kernel_spmd(nc, [{f"in_{n}": v for n, v in arrays.items()}], core_ids=[0])
    return r.results[0]["out"].reshape(1, T, D)
```
